# Optimizing a Trainium2 kernel written in Bass

```python
import math
import jax, jax.numpy as jnp
from jax import lax
import numpy as np

D_MODEL = 1024
BATCH = 1
SEQ = 512
DEPTH = 1

ATT_WIDTH = D_MODEL // 2
RWKV_WIDTH = D_MODEL - ATT_WIDTH
DA_HEAD_DIM = 64
DA_HEADS = ATT_WIDTH // (2 * DA_HEAD_DIM)
DA_V_DIM = 2 * DA_HEAD_DIM
Q_BLOCK = 128
RW_HEAD = 64
RW_HEADS = RWKV_WIDTH // RW_HEAD
DECAY_LORA = 64
ICLR_LORA = 64
GATE_LORA = 128
RWKV_COLS = 3 * RWKV_WIDTH + 2 * DECAY_LORA + 2 * ICLR_LORA + GATE_LORA
IN_COLS = 3 * ATT_WIDTH + RWKV_COLS
GN_EPS = 64e-5
PEER_HEADS = 8
PEER_NKEYS = 128
PEER_EXPERTS = PEER_NKEYS * PEER_NKEYS
PEER_TOPK = 16
PEER_QDIM = 256
PEER_SUBDIM = PEER_QDIM // 2
PEER_CHUNK = 128
NORM_EPS = 1e-6

kernel_name = "hymba_diffattn_rwkv7_peer_adaln"

def rms_norm(x, g, eps=NORM_EPS):
    xf = x.astype(jnp.float32)
    y = xf * lax.rsqrt(jnp.mean(xf * xf, axis=-1, keepdims=True) + eps)
    return (y * g.astype(jnp.float32)).astype(x.dtype)

def alibi_slopes(n):
    return jnp.asarray([2.0 ** (-8.0 * (h + 1) / n) for h in range(n)], jnp.float32)

def lambda_init_fn(layer_idx):
    return 0.8 - 0.6 * math.exp(-0.3 * layer_idx)

def diff_attention(q, k, v, qn_g, kn_g, lam, subln_g, lambda_init):
    B, S = q.shape[0], q.shape[1]
    q = rms_norm(q, qn_g)
    k = rms_norm(k, kn_g)
    lf = lam.astype(jnp.float32)
    lam_full = jnp.exp(jnp.sum(lf[0] * lf[1])) - jnp.exp(jnp.sum(lf[2] * lf[3])) + lambda_init
    slopes = alibi_slopes(DA_HEADS)
    scale = DA_HEAD_DIM ** -0.5
    kpos = jnp.arange(S)
    n_blk = S // Q_BLOCK
    qb = q.reshape(B, n_blk, Q_BLOCK, DA_HEADS, 2, DA_HEAD_DIM).transpose(1, 0, 2, 3, 4, 5)
    starts = jnp.arange(n_blk) * Q_BLOCK

    def block(args):
        qblk, start = args
        s = jnp.einsum('bqhcd,bkhcd->bhcqk', qblk, k, preferred_element_type=jnp.float32) * scale
        qpos = start + jnp.arange(Q_BLOCK)
        dist = jnp.abs(qpos[:, None] - kpos[None, :]).astype(jnp.float32)
        s = s - slopes[None, :, None, None, None] * dist[None, None, None]
        p = jax.nn.softmax(s, axis=-1)
        a = p[:, :, 0] - lam_full * p[:, :, 1]
        return jnp.einsum('bhqk,bkhv->bqhv', a.astype(v.dtype), v)

    o = lax.map(block, (qb, starts))
    o = o.transpose(1, 0, 2, 3, 4).reshape(B, S, DA_HEADS, DA_V_DIM)
    o = rms_norm(o, subln_g) * (1.0 - lambda_init)
    return o.reshape(B, S, DA_HEADS * DA_V_DIM)

def centred_shift(p, mu):
    prev = jnp.pad(p, ((0, 0), (1, 0), (0, 0)))[:, :-1]
    nxt = jnp.pad(p, ((0, 0), (0, 1), (0, 0)))[:, 1:]
    return p + mu[0] * (prev - p) + mu[1] * (nxt - p)

def rwkv7_bidir(p, mu, w0, w2, a0, a2, g2, k_k, k_a, r_k, ln_g, ln_b):
    B, S = p.shape[0], p.shape[1]
    out_dtype = p.dtype
    p = centred_shift(p.astype(jnp.float32), mu.astype(jnp.float32))
    W = RWKV_WIDTH
    o1 = 3 * W
    o2 = o1 + 2 * DECAY_LORA
    o3 = o2 + 2 * ICLR_LORA
    r, k, v = p[..., :W], p[..., W:2 * W], p[..., 2 * W:o1]
    wd = p[..., o1:o2].reshape(B, S, 2, DECAY_LORA)
    ad = p[..., o2:o3].reshape(B, S, 2, ICLR_LORA)
    gd = p[..., o3:]
    f = lambda t: t.astype(jnp.float32)
    w = -jax.nn.softplus(-(f(w0) + jnp.einsum('bsdr,drc->bsdc', jnp.tanh(wd), f(w2)))) - 0.5
    decay = jnp.exp(-jnp.exp(w))
    a = jax.nn.sigmoid(f(a0) + jnp.einsum('bsdr,drc->bsdc', ad, f(a2)))
    g = jax.nn.sigmoid(gd) @ f(g2)
    kk = (k * f(k_k)).reshape(B, S, RW_HEADS, RW_HEAD)
    kk = kk / jnp.maximum(jnp.sqrt(jnp.sum(kk * kk, -1, keepdims=True)), 1e-12)
    k_dir = k[:, :, None, :] * (1.0 + (a - 1.0) * f(k_a))
    hd = lambda t: t.reshape(t.shape[:-1] + (RW_HEADS, RW_HEAD))
    rh, kh, vh = hd(r), hd(k), hd(v)

    def shared_dirs(t):
        return jnp.stack([t, t[:, ::-1]], 0).transpose(2, 0, 1, 3, 4)

    def split_dirs(t):
        return jnp.stack([t[:, :, 0], t[:, ::-1, 1]], 0).transpose(2, 0, 1, 3, 4)

    xs = (shared_dirs(rh), split_dirs(hd(decay)), split_dirs(hd(k_dir)), shared_dirs(vh),
          shared_dirs(kk), split_dirs(hd(a)))

    def step(state, inp):
        r_t, dec_t, k_t, v_t, kk_t, a_t = inp
        sa = jnp.einsum('dbhvk,dbhk->dbhv', state, -kk_t)
        new = (state * dec_t[..., None, :] + sa[..., :, None] * (kk_t * a_t)[..., None, :]
               + v_t[..., :, None] * k_t[..., None, :])
        y_fwd = jnp.einsum('bhvk,bhk->bhv', new[0], r_t[0])
        y_bwd = jnp.einsum('bhvk,bhk->bhv', state[1], r_t[1])
        return new, jnp.stack([y_fwd, y_bwd], 0)

    s0 = jnp.zeros((2, B, RW_HEADS, RW_HEAD, RW_HEAD), jnp.float32)
    _, ys = lax.scan(step, s0, xs)
    y = (ys[:, 0] + ys[::-1, 1]).transpose(1, 0, 2, 3)
    mean = jnp.mean(y, -1, keepdims=True)
    var = jnp.mean(jnp.square(y - mean), -1, keepdims=True)
    yn = ((y - mean) * lax.rsqrt(var + GN_EPS)).reshape(B, S, W) * f(ln_g) + f(ln_b)
    bonus = (jnp.sum(rh * kh * f(r_k), -1, keepdims=True) * vh).reshape(B, S, W)
    return ((yn + bonus) * g).astype(out_dtype)

def peer_ffn(h, wq, keys, U, V):
    B, S, D = h.shape
    T = B * S
    hf = h.reshape(T, D)
    q = (hf @ wq).reshape(T, PEER_HEADS, 2, PEER_SUBDIM)
    s = jnp.einsum('thpd,hpkd->thpk', q, keys, preferred_element_type=jnp.float32)
    s1, i1 = lax.top_k(s[:, :, 0], PEER_TOPK)
    s2, i2 = lax.top_k(s[:, :, 1], PEER_TOPK)
    cand = (s1[..., :, None] + s2[..., None, :]).reshape(T, PEER_HEADS, PEER_TOPK * PEER_TOPK)
    sc, ci = lax.top_k(cand, PEER_TOPK)
    e1 = jnp.take_along_axis(i1, ci // PEER_TOPK, axis=-1)
    e2 = jnp.take_along_axis(i2, ci % PEER_TOPK, axis=-1)
    idx = e1 * PEER_NKEYS + e2
    gates = jax.nn.softmax(sc, axis=-1)
    n_chunks = T // PEER_CHUNK

    def chunk(args):
        xc, ic, gc = args
        act = jax.nn.gelu(jnp.einsum('chkd,cd->chk', U[ic], xc, preferred_element_type=jnp.float32),
                          approximate=False)
        return jnp.einsum('chk,chkd->cd', (gc * act).astype(V.dtype), V[ic])

    out = lax.map(chunk, (hf.reshape(n_chunks, PEER_CHUNK, D),
                          idx.reshape(n_chunks, PEER_CHUNK, PEER_HEADS, PEER_TOPK),
                          gates.reshape(n_chunks, PEER_CHUNK, PEER_HEADS, PEER_TOPK)))
    return out.reshape(B, S, D).astype(h.dtype)

def setup_inputs(seed: int = 0) -> dict:
    key = jax.random.key(seed)
    ks = jax.random.split(key, 32)
    f32 = jnp.float32
    L, D = DEPTH, D_MODEL
    nrm = lambda k, shape, s: jax.random.normal(k, shape, f32) * s
    gain = lambda k, shape: 1.0 + 0.05 * jax.random.normal(k, shape, f32)
    return {
        'x': nrm(ks[0], (BATCH, SEQ, D), 1.0),
        'c': nrm(ks[1], (BATCH, D), 1.0),
        'ada_w': nrm(ks[2], (L, D, 6 * D), D ** -0.5),
        'ada_b': nrm(ks[3], (L, 6 * D), 0.02),
        'norm1_g': gain(ks[4], (L, D)),
        'w_in': nrm(ks[5], (L, D, IN_COLS), D ** -0.5),
        'da_qnorm_g': gain(ks[6], (L, DA_HEAD_DIM)),
        'da_knorm_g': gain(ks[7], (L, DA_HEAD_DIM)),
        'da_lambda': nrm(ks[8], (L, 4, DA_HEAD_DIM), 0.1),
        'da_subln_g': gain(ks[9], (L, DA_V_DIM)),
        'rw_shift_mu': jax.random.uniform(ks[10], (L, 2, RWKV_COLS), f32, 0.0, 0.5),
        'rw_w0': jax.random.uniform(ks[11], (L, 2, RWKV_WIDTH), f32, -6.0, 1.0),
        'rw_w2': nrm(ks[12], (L, 2, DECAY_LORA, RWKV_WIDTH), 0.1),
        'rw_a0': nrm(ks[13], (L, 2, RWKV_WIDTH), 0.3),
        'rw_a2': nrm(ks[14], (L, 2, ICLR_LORA, RWKV_WIDTH), 0.1),
        'rw_g2': nrm(ks[15], (L, GATE_LORA, RWKV_WIDTH), GATE_LORA ** -0.5),
        'rw_k_k': 0.85 + 0.05 * jax.random.normal(ks[16], (L, RWKV_WIDTH), f32),
        'rw_k_a': gain(ks[17], (L, RWKV_WIDTH)),
        'rw_r_k': nrm(ks[18], (L, RW_HEADS, RW_HEAD), 0.1),
        'rw_ln_g': gain(ks[19], (L, RWKV_WIDTH)),
        'rw_ln_b': nrm(ks[20], (L, RWKV_WIDTH), 0.02),
        'w_out': nrm(ks[21], (L, D, D), D ** -0.5),
        'norm2_g': gain(ks[22], (L, D)),
        'peer_wq': nrm(ks[23], (L, D, PEER_HEADS * PEER_QDIM), D ** -0.5),
        'peer_keys': nrm(ks[24], (L, PEER_HEADS, 2, PEER_NKEYS, PEER_SUBDIM), PEER_SUBDIM ** -0.5),
        'peer_u': nrm(ks[25], (L, PEER_EXPERTS, D), D ** -0.5),
        'peer_v': nrm(ks[26], (L, PEER_EXPERTS, D), PEER_TOPK ** -0.5),
    }

def reference(x, c, ada_w, ada_b, norm1_g, w_in, da_qnorm_g, da_knorm_g, da_lambda, da_subln_g,
              rw_shift_mu, rw_w0, rw_w2, rw_a0, rw_a2, rw_g2, rw_k_k, rw_k_a, rw_r_k, rw_ln_g, rw_ln_b,
              w_out, norm2_g, peer_wq, peer_keys, peer_u, peer_v):
    B, S, D = x.shape
    for l in range(DEPTH):
        mod = (jax.nn.silu(c) @ ada_w[l] + ada_b[l]).reshape(B, 6, D)
        shift1, scale1, gate1, shift2, scale2, gate2 = [mod[:, i, None, :] for i in range(6)]
        h = rms_norm(x, norm1_g[l]) * (1.0 + scale1) + shift1
        p = h @ w_in[l]
        q = p[..., :ATT_WIDTH].reshape(B, S, DA_HEADS, 2, DA_HEAD_DIM)
        k = p[..., ATT_WIDTH:2 * ATT_WIDTH].reshape(B, S, DA_HEADS, 2, DA_HEAD_DIM)
        v = p[..., 2 * ATT_WIDTH:3 * ATT_WIDTH].reshape(B, S, DA_HEADS, DA_V_DIM)
        att = diff_attention(q, k, v, da_qnorm_g[l], da_knorm_g[l], da_lambda[l], da_subln_g[l],
                             lambda_init_fn(l))
        rw = rwkv7_bidir(p[..., 3 * ATT_WIDTH:], rw_shift_mu[l], rw_w0[l], rw_w2[l], rw_a0[l], rw_a2[l],
                         rw_g2[l], rw_k_k[l], rw_k_a[l], rw_r_k[l], rw_ln_g[l], rw_ln_b[l])
        x = x + gate1 * (jnp.concatenate([att, rw], axis=-1) @ w_out[l])
        h2 = rms_norm(x, norm2_g[l]) * (1.0 + scale2) + shift2
        x = x + gate2 * peer_ffn(h2, peer_wq[l], peer_keys[l], peer_u[l], peer_v[l])
    return x


_drawn_inputs = setup_inputs


def setup_inputs(seed=0):
    import zlib

    import numpy as np

    out = dict(_drawn_inputs(seed))
    spreads = {}
    factors = {'da_qnorm_g': 5.799,
     'da_knorm_g': 5.988,
     'da_lambda': 2.717,
     'da_subln_g': 2.771,
     'rw_ln_g': 4.223,
     'rw_ln_b': 8.0,
     'norm2_g': 2.733}
    for name, (base, spread) in spreads.items():
        noise = np.random.default_rng([zlib.crc32(name.encode()), seed]).standard_normal(out[name].shape)
        drawn = base * np.exp(spread * noise) if base else spread * noise
        out[name] = __import__('jax').numpy.asarray(drawn.astype(out[name].dtype))
    for name, factor in factors.items():
        out[name] = (out[name] * factor).astype(out[name].dtype)
    return out
```

```python
import math
from contextlib import ExitStack

import concourse.bass as bass
from concourse import mybir

F32 = mybir.dt.float32
I32 = mybir.dt.int32
U32 = mybir.dt.uint32
ALU = mybir.AluOpType
ACT = mybir.ActivationFunctionType
AX = mybir.AxisListType

P = 128
D = 1024
S = 512
NT = S // P
KD = D // P
HD = 64
DA = 4
NB = 4
RW0 = 3 * 512
CH = 64
NC = S // CH
LEVELS = 6
PH = 8
TOPK = 16
NKEY = 128
SLOTS = PH * TOPK
U_SLOTS, V_SLOTS = 4, 8
CHOICE_OPS = 16
NORM_EPS = 1e-6
GN_EPS = 64e-5
DECAY = math.exp(-0.5)
LAMBDA0 = 0.8 - 0.6 * math.exp(0.0)
LOWEST = -3.0e38
UNIT = 512


class Tally:

    def __init__(self, eng, sem):
        self.eng, self.sem, self.n = eng, sem, 0

    def __call__(self, instruction):
        instruction.then_inc(self.sem, 1)
        self.n += 1

    def link(self, instruction):
        self(instruction)
        self.eng.wait_ge(self.sem, self.n)


STEPS = ["decay", "iclr", "alpha_t", "beta_t", "kappa_t", "gram_b", "gram_k", "mv", "w0"]
for _k in range(1, LEVELS):
    STEPS += [f"w{_k}"] + ([f"x{_k}"] if _k < LEVELS - 1 else []) + [f"xt{_k}"]
STEPS += ["gh", "phi", "psi", "rho", "y"]
ACT_STEPS = ["decay", "iclr", "alpha_t", "beta_t", "kappa_t", "mv"] + [f"w{_k}" for _k in range(1, LEVELS)] + ["gh", "psi"]
DVE_STEPS = ["gram_b", "gram_k", "w0"]
for _k in range(1, LEVELS):
    DVE_STEPS += ([f"x{_k}"] if _k < LEVELS - 1 else []) + [f"xt{_k}"]
DVE_STEPS += ["phi", "rho", "y"]


def upto(steps, name, i):
    return i * len(steps) + (steps.index(name) + 1)


def hymba_kernel(nc, x, c, ada_w, ada_b, norm1_g, w_in, da_qnorm_g, da_knorm_g, da_lambda, da_subln_g,
                 rw_shift_mu, rw_w0, rw_w2, rw_a0, rw_a2, rw_g2, rw_k_k, rw_k_a, rw_r_k, rw_ln_g, rw_ln_b,
                 w_out, norm2_g, peer_wq, peer_keys, peer_u, peer_v, out):
    with ExitStack() as ctx:
        def sb(name, shape, dt=F32):
            return ctx.enter_context(nc.sbuf_tensor(name, shape, dt))

        def sem(name):
            return ctx.enter_context(nc.semaphore(name))

        ident = sb("ident", [P, P])
        sel = sb("sel", [P, 8, 16])
        selT = sb("selT", [16, 8, P])
        selh = sb("selh", [P, DA, DA])
        selhT = sb("selhT", [DA, DA, P])
        half_ones = sb("half_ones", [P, P])
        qk_fold = sb("qk_fold", [16, 1])
        restart = sb("restart", [P, S])
        s_idx = sb("s_idx", [P, CH], I32)
        t_idx = sb("t_idx", [P, CH], I32)
        xor_idx = sb("xor_idx", [P, CH], I32)
        level = sb("level", [P, 2, LEVELS, CH])
        tri = sb("tri", [P, 2, 2, CH])
        eye = sb("eye", [P, CH])
        c_col = sb("c_col", [P, KD])
        silu_c = sb("silu_c", [P, KD])
        ada_bc = sb("ada_bc", [P, 16])
        n1_col = sb("n1_col", [P, KD])
        mod1 = sb("mod1", [P, 16])
        qk_gain = sb("qk_gain", [P, 2])
        mu = sb("mu", [P, 2, 15])
        mu_self = sb("mu_self", [P, 15])
        sub_g = sb("sub_g", [P, 1])
        lam = sb("lam", [P, 4 * HD])
        lam_p = sb("lam_p", [P, 2 * HD])
        lam_e = sb("lam_e", [P, 2])
        neg_lam = sb("neg_lam", [P, 1])
        w0_col = sb("w0_col", [P, 2, NB])
        a0_col = sb("a0_col", [P, 2, NB])
        kk_col = sb("kk_col", [P, NB])
        ka_col = sb("ka_col", [P, NB])
        ka1_col = sb("ka1_col", [P, NB])
        rk_col = sb("rk_col", [P, NB])
        lg_col = sb("lg_col", [P, NB])
        lb_col = sb("lb_col", [P, NB])
        w2_sb = sb("w2_sb", [P, 512])
        a2_sb = sb("a2_sb", [P, 512])
        g2_sb = sb("g2_sb", [P, 512])
        w2_pair = sb("w2_pair", [P, P])
        a2_pair = sb("a2_pair", [P, P])
        sumsq = sb("sumsq", [P, NT])
        rstd = sb("rstd", [P, NT])
        stat = sb("stat", [16, S])
        mx = sb("mx", [P, 2, 2])
        nmx = sb("nmx", [P, 2, 2])
        den = sb("den", [P, 2, 2])
        rden = sb("rden", [P, 2, 2])
        ptot = sb("ptot", [P, 2, NC])

        top = sb("top", [P, 3, TOPK])
        top_i = sb("top_i", [P, 3, TOPK], U32)
        neg_top = sb("neg_top", [P, 1])
        ci_lo = sb("ci_lo", [P, TOPK], I32)
        ci_hi = sb("ci_hi", [P, TOPK], I32)
        e_half = sb("e_half", [P, 2, TOPK])
        g_exp_t = sb("g_exp_t", [P, TOPK])
        g_den = sb("g_den", [P, 1])
        iota16i = sb("iota16i", [P, TOPK], I32)
        idx_col = sb("idx_col", [P, TOPK], I32)
        act16 = sb("act16", [P, TOPK])
        gelu16 = sb("gelu16", [P, TOPK])
        w16 = sb("w16", [P, TOPK])
        zero_w = sb("zero_w", [P, P])

        NU = 87
        arena = sb("arena", [P, NU, UNIT])

        def units(u, n):
            return arena[:, u:u + n, :]

        rT, kT, vT, kkT = units(0, 4), units(4, 4), units(8, 4), units(12, 4)
        attT = units(16, 4)
        loT = units(20, 3)
        qkT = units(23, 8)
        vA = units(31, 4)
        hT = units(35, 8)
        ring = units(43, 16)
        xs = units(59, 8)
        xr = units(67, 8)
        sq = units(75, 2)
        sq_o = units(67, DA)
        stat_kk, stat_o = arena[0:8, 84, :], arena[0:DA, 85, :]
        bias = units(77, 7)
        bias_h = bias.rearrange("p u n -> p (u n)").rearrange("p (h n) -> p h n", h=DA)
        probs = units(59, 4)
        mix = units(63, 2)
        mixT = units(65, 2)
        PHI, PSI, RP, YT = units(23, 8), units(31, 8), units(39, 8), units(47, 4)
        vt_u = units(51, 1)
        dir_u = [52, 69]
        ps = ctx.enter_context(nc.psum_tensor("ps", [P, 8, 512], F32))

        def chunks(ap):
            return ap.rearrange("p u n -> p (u n)").rearrange("p (c n) -> p c n", c=NC)

        class Dir:

            def __init__(self, u):
                self.bk = units(u, 2)
                self.beta, self.kappa = arena[:, u, :], arena[:, u + 1, :]
                self.gh = chunks(units(u, 2))
                self.hat_b, self.hat_k = arena[:, u + 2, :], arena[:, u + 3, :]
                self.la = chunks(units(u + 2, 2))
                self.ar = chunks(units(u + 4, 2))
                self.rhs = chunks(units(u + 6, 2))
                self.beta_t, self.kappa_t = chunks(units(u + 8, 1)), chunks(units(u + 9, 1))
                self.mb = chunks(units(u + 10, 2))
                t = u + 12
                self.dg = chunks(units(t, 1))
                self.sg, self.a, self.cum = arena[:, t, :], arena[:, t + 1, :], arena[:, t + 2, :]
                self.pinc, self.pinv, self.pexc = arena[:, t + 3, :], arena[:, t + 4, :], self.sgx(t)
                self.c = [chunks(units(t, 1)), chunks(units(t + 1, 1))]
                self.x, self.xt, self.w = chunks(units(t + 2, 1)), chunks(units(t + 3, 1)), chunks(units(t + 4, 1))

            def sgx(self, t):
                return arena[:, t, :]

        dirs = [Dir(u) for u in dir_u]
        x1 = units(0, 8).rearrange("p u n -> p (u n)").rearrange("p (t d) -> p t d", t=NT)
        mod_rows = units(8, 8).rearrange("p u n -> p (u n)").rearrange("p (m d) -> p m d", m=4)
        gate1, shift2, scale2, gate2 = (mod_rows[:, m, :] for m in range(4))
        n2_rows = units(20, 2).rearrange("p u n -> p (u n)")
        ring2 = units(23, 16)
        h2T = units(39, 8)
        h2 = units(52, 8).rearrange("p u n -> p (u n)").rearrange("p (t d) -> p t d", t=NT)
        wo = units(69, 16).rearrange("p u n -> p (u n)").rearrange("p (k n) -> p k n", k=KD)
        silu_rows = units(85, 2).rearrange("p u n -> p (u n)").rearrange("p (k m) -> p k m", k=KD)
        keys_raw = units(60, 4).rearrange("p u n -> p (u n)").rearrange("p (b n) -> p b n", b=16)
        keysT = units(64, 4).rearrange("p u n -> p (u n)").rearrange("p (b n) -> p b n", b=16)
        qT = units(47, 4)
        scores_all = units(69, 17).rearrange("p u n -> p (u n)")
        gates = units(16, 2).rearrange("p u n -> p (u n)")
        e_idx = units(18, 2).rearrange("p u n -> p (u n)").bitcast(I32)
        sc, sc_cut = arena[:, 20, 0:256], arena[:, 20, 256:512]
        cand, cand_cut = arena[:, 21, 0:256], arena[:, 21, 256:512]
        pick = arena[:, 22, :].rearrange("p (a r m) -> p a r m", a=2, r=TOPK)
        v_ring = units(23, 16).rearrange("p u n -> p (u n)").rearrange("p (s d) -> p s d", s=V_SLOTS)
        u_ring = units(39, 8).rearrange("p u n -> p (u n)").rearrange("p (s d) -> p s d", s=U_SLOTS)
        o_rows = units(47, 2).rearrange("p u n -> p (u n)")
        diag = units(49, 2).rearrange("p u n -> p (u n)").rearrange("p (s m) -> p s m", s=V_SLOTS)
        h2_fix = units(8, 2).rearrange("p u n -> p (u n)")
        waste = units(10, 4).rearrange("p u n -> p (u n)").rearrange("p (s d) -> p s d", s=2)
        v_t = chunks(vt_u)
        v_fix = arena[:, 86, :]
        states = units(52, NC)
        tmp = units(60, 4)
        tmp2 = units(64, 4)
        stat_y = arena[0:8, 68, :]

        def pair_of(u, i, n=1):
            return arena[:, bass.ds(i + u, 1), :].rearrange("p a n -> p (a n)")

        def by_chunk(ap):
            return ap.rearrange("p (c n) -> p c n", c=NC)

        ld_c = sem("ld_c"); ld_par = sem("ld_par"); ld_mu = sem("ld_mu"); ld_rw = sem("ld_rw"); ld_lam = sem("ld_lam")
        ld_x = [sem(f"ld_x{t}") for t in range(NT)]
        ld_w = [sem(f"ld_w{i}") for i in range(4)]
        w_used = sem("w_used")
        zeroed = sem("zeroed"); consts = sem("consts"); sel_done = sem("sel_done"); masks = sem("masks")
        silu_done = sem("silu_done"); mod1_done = sem("mod1_done"); mu_done = sem("mu_done")
        ss_done = sem("ss_done"); rv_done = sem("rv_done"); rstd_done = sem("rstd_done")
        xs_done = sem("xs_done"); xT_mm = sem("xT_mm"); hT_done = sem("hT_done")
        proj_mm = sem("proj_mm"); proj_a = sem("proj_a"); proj_v = sem("proj_v")
        qk_sqr = sem("qk_sqr"); qk_stat = sem("qk_stat")
        v_mm = sem("v_mm"); v_done = sem("v_done")
        qk_var = sem("qk_var"); qk_rstd = sem("qk_rstd"); qk_bc = sem("qk_bc"); qk_done = sem("qk_done")
        lo_done = sem("lo_done")
        kk_raw = sem("kk_raw"); kk_sqr = sem("kk_sqr"); kk_stat = sem("kk_stat")
        kk_norm = sem("kk_norm"); kk_inv = sem("kk_inv"); kk_bc = sem("kk_bc"); kk_done = sem("kk_done")
        bias_done = sem("bias_done"); lam_sum = sem("lam_sum"); lam_exp = sem("lam_exp")
        s_mm = sem("s_mm"); s_max = sem("s_max"); s_exp = sem("s_exp"); mixed = sem("mixed")
        mixT_mm = sem("mixT_mm"); mixT_done = sem("mixT_done"); o_mm = sem("o_mm"); o_copy = sem("o_copy"); o_sqr = sem("o_sqr")
        o_stat = sem("o_stat"); o_var = sem("o_var"); o_rstd = sem("o_rstd"); o_bc = sem("o_bc"); o_done = sem("o_done")
        dve_s = sem("dve_s"); 
        ld_wo = sem("ld_wo"); ld_rows = sem("ld_rows"); ld_keys = sem("ld_keys")
        sr_done = sem("sr_done"); rows_mm = sem("rows_mm"); rows_done = sem("rows_done"); 
        wo_mm = sem("wo_mm"); wo_gated = sem("wo_gated"); x1_done = sem("x1_done")
        ss2 = sem("ss2"); rv2 = sem("rv2"); rstd2 = sem("rstd2"); h2a = sem("h2a"); h2_done = sem("h2_done")
        h2T_mm = sem("h2T_mm"); h2T_done = sem("h2T_done"); keysT_mm = sem("keysT_mm"); keysT_done = sem("keysT_done")
        q_mm = sem("q_mm"); q_done = sem("q_done"); sc_mm = sem("sc_mm"); sc_done = sem("sc_done")
        sc_fixed = sem("sc_fixed"); best = sem("best"); neg_done = sem("neg_done"); g_exp = sem("g_exp"); math_s = sem("math_s")
        e_done = sem("e_done"); g_done = sem("g_done"); g_rec = sem("g_rec"); col_done = sem("col_done")
        ld_u = [sem(f"ld_u{n}") for n in range(U_SLOTS)]; ld_v = [sem(f"ld_v{n}") for n in range(V_SLOTS)]
        u_free = sem("u_free"); v_free = sem("v_free")
        h2_fixed = sem("h2_fixed"); gelu_done = sem("gelu_done"); w_done = sem("w_done"); diags = sem("diags")
        tile_mm = sem("tile_mm"); o_gated = sem("o_gated"); o_sum = sem("o_sum"); st_out = sem("st_out")
        masks_done = sem("masks_done"); v_fixed = sem("v_fixed"); vt_mm = sem("vt_mm"); vt_done = sem("vt_done")
        pair_w = sem("pair_w")
        mm = [sem(f"step_mm{d}") for d in range(2)]
        by_act = [sem(f"step_act{d}") for d in range(2)]
        by_dve = [sem(f"step_dve{d}") for d in range(2)]
        cum_done = sem("cum_done")
        exps = sem("exps")
        feat_v = sem("feat_v")
        feat_p = sem("feat_p")
        c_done = [sem(f"c_done{d}") for d in range(2)]
        kap = sem("kap")
        x_one = sem("x_one")
        state_mm = sem("state_mm"); state_done = sem("state_done"); yst_mm = sem("yst_mm"); y_sum = sem("y_sum")
        mean_mm = sem("mean_mm"); centred = sem("centred"); y_sqr = sem("y_sqr"); y_stat = sem("y_stat"); y_var = sem("y_var")
        y_rstd = sem("y_rstd"); y_bc = sem("y_bc"); rk_done = sem("rk_done"); bon_mm = sem("bon_mm")
        bon_done = sem("bon_done"); gate_mm = sem("gate_mm"); rw_out = sem("rw_out")

        strips = [(ada_w, i * 256, 256) for i in range(8)]
        strips += [(w_in, RW0 + i * 256, 256 if i < 7 else 128) for i in range(8)]
        strips += [(w_in, 1024 + i * 256, 256) for i in range(2)]
        strips += [(w_in, i * 256, 256) for i in range(4)]
        rw_blocks = [(8 + b // 2, P * (b % 2)) for b in range(15)]
        qk_blocks = [(18 + b // 2, P * (b % 2)) for b in range(8)]

        def strip(n):
            w = strips[n][2]
            flat = ring[:, 4 * (n % 4):4 * (n % 4) + 4, :].rearrange("p u n -> p (u n)")
            return flat[:, 0:KD * w].rearrange("p (k n) -> p k n", k=KD)

        def strip_read(eng, n):
            if n < 8:
                eng.wait_ge(w_used, n + 1)
            elif n < 16:
                eng.wait_ge(proj_mm, min(2 * (n - 8) + 2, 15))
            elif n < 18:
                eng.wait_ge(v_mm, NT)
            else:
                eng.wait_ge(proj_mm, 15 + 2 * (n - 18) + 2)

        def rw_dest(b):
            return arena[:, b, :] if b < 12 else loT[:, b - 12, :]

        def strip2(n):
            return ring2[:, 4 * (n % 4):4 * (n % 4) + 4, :].rearrange("p u n -> p (u n)").rearrange("p (k n) -> p k n", k=KD)

        def ring2_loaded(n):
            first = len(strips[n % 4::4])
            return 16 * (first + n // 4 + 1)

        def cat(k):
            return attT[:, k, :] if k < 4 else YT[:, k - 4, :]

        UN = DA * NT
        x_rows = xr.rearrange("p u n -> p (u n)").rearrange("p (t d) -> p t d", t=NT)
        xs_rows = xs.rearrange("p u n -> p (u n)").rearrange("p (t d) -> p t d", t=NT)

        def bank_of(d, name):
            return 4 * d + 2 * (STEPS.index(name) % 2)

        CONSTS = 10
        RW_LOADS = 12 * 16

        block = ctx.enter_context(nc.Block())

        @block.sync
        def _(sp):
            sp.dma_start(c_col[:], c.rearrange("o (k p) -> p (o k)", p=P), allow_slow_non_contiguous=True).then_inc(ld_c, 16)

            def load_strip(n):
                src, c0, w = strips[n]
                if n >= 4:
                    strip_read(sp, n - 4)
                sp.dma_start(strip(n), src[:, c0:c0 + w].rearrange("(k p) n -> p k n", p=P)).then_inc(ld_w[n % 4], 16)

            for n in range(4):
                load_strip(n)
                sp.dma_start(x_rows[:, n, :], x[n * P:(n + 1) * P, :]).then_inc(ld_x[n], 16)
            for n in range(4, len(strips)):
                load_strip(n)
            for d in range(2):
                sp.wait_ge(mm[d], NB * len(STEPS))
                sp.wait_ge(by_dve[d], NB * len(DVE_STEPS))
                sp.wait_ge(by_act[d], NB * len(ACT_STEPS))
                sp.wait_ge(c_done[d], NB * 7)
            sp.dma_start(wo, w_out.rearrange("(k p) n -> p k n", p=P)).then_inc(ld_wo, 16)
            sp.wait_ge(rw_out, NB)

            def load_ring2(n):
                if 4 <= n < 20:
                    sp.wait_ge(rows_mm, n - 3)
                elif n >= 20:
                    sp.wait_ge(q_mm, 2 * (n - 20) + 2)
                src = ada_w[:, 2048 + 256 * n:2304 + 256 * n] if n < 16 else peer_wq[:, 256 * (n - 16):256 * (n - 15)]
                sp.dma_start(strip2(n), src.rearrange("(k p) n -> p k n", p=P)).then_inc(ld_w[n % 4], 16)

            for m in range(4):
                sp.dma_start(mod_rows[:, m, :], ada_b[:, 2048 + 1024 * m:3072 + 1024 * m].to_broadcast([P, D])).then_inc(ld_rows, 16)
                load_ring2(m)
            for t in range(NT):
                sp.dma_start(x1[:, t, :], x[t * P:(t + 1) * P, :]).then_inc(ld_x[t], 16)
            sp.dma_start(n2_rows, norm2_g.to_broadcast([P, D])).then_inc(ld_rows, 16)
            sp.dma_start(keys_raw, peer_keys.rearrange("b n d -> n b d")).then_inc(ld_keys, 16)
            for n in range(4, 24):
                load_ring2(n)
            for t in range(NT):
                sp.wait_ge(o_sum, 2 * t + 2)
                sp.dma_start(out[t * P:(t + 1) * P, :], o_rows).then_inc(st_out, 16)
            sp.wait_ge(st_out, 16 * NT)

        @block.gpsimd
        def _(pool):
            slow = dict(allow_slow_non_contiguous=True)
            pool.dma_start(ada_bc[:], ada_b[0, 0:2048].rearrange("(j p) -> p j", p=P), **slow).then_inc(ld_par, 16)
            pool.dma_start(n1_col[:], norm1_g.rearrange("o (j p) -> p (o j)", p=P), **slow).then_inc(ld_par, 16)
            for d in range(2):
                pool.dma_start(mu[:, d, :], rw_shift_mu[0, d, :].rearrange("(j p) -> p j", p=P), **slow).then_inc(ld_mu, 16)
            for i, g in enumerate((da_qnorm_g, da_knorm_g)):
                for h in range(2):
                    pool.dma_start(qk_gain[HD * h:HD * h + HD, i:i + 1], g.rearrange("o d -> d o"), **slow).then_inc(ld_mu, 16)
            pool.memset(ident[:], 0.0).then_inc(zeroed, 1)
            pool.memset(sel[:], 0.0).then_inc(zeroed, 1)
            pool.memset(selT[:], 0.0).then_inc(zeroed, 1)
            pool.memset(half_ones[:], 0.0).then_inc(zeroed, 1)
            pool.memset(selh[:], 0.0).then_inc(zeroed, 1)
            pool.memset(selhT[:], 0.0).then_inc(zeroed, 1)
            pool.memset(qk_fold[:], 1.0).then_inc(zeroed, 1)
            pool.memset(restart[:], 1.0).then_inc(zeroed, 1)
            pool.memset(zero_w[:], 0.0).then_inc(zeroed, 1)
            pool.wait_ge(zeroed, 9)
            pool.affine_select(out=ident[:], in_=ident[:], compare_op=ALU.not_equal, fill=1.0, base=0,
                               pattern=[[-1, P]], channel_multiplier=1).then_inc(consts, 1)
            split = selT[:].rearrange("m b (h p) -> m b h p", h=2)
            pool.affine_select(out=split, in_=split, compare_op=ALU.not_equal, fill=1.0, base=0,
                               pattern=[[-2, 8], [-1, 2], [0, 64]], channel_multiplier=1).then_inc(consts, 1)
            pool.affine_select(out=selhT[:], in_=selhT[:], compare_op=ALU.not_equal, fill=1.0, base=0,
                               pattern=[[-1, DA], [0, P]], channel_multiplier=1).then_inc(consts, 1)
            pool.memset(selh[:].rearrange("p h m -> p (h m)")[:, 0:DA * DA:DA + 1], 1.0).then_inc(consts, 1)
            pool.memset(qk_fold[0:8, :], 1.0 / HD).then_inc(consts, 1)
            pool.memset(restart[:, 0:S:CH], 0.0).then_inc(consts, 1)
            pool.iota(s_idx[:], [[0, CH]], base=0, channel_multiplier=1).then_inc(consts, 1)
            pool.iota(t_idx[:], [[1, CH]], base=0, channel_multiplier=0).then_inc(consts, 1)
            pool.iota(iota16i[:], [[1, TOPK]], base=0, channel_multiplier=0).then_inc(consts, 1)
            pool.iota(bias_h[:, 0, :], [[-1, 896]], base=384, channel_multiplier=1,
                      allow_small_or_imprecise_dtypes=True).then_inc(consts, 1)
            pool.dma_start(lam[:], da_lambda.rearrange("o a d -> o (a d)").to_broadcast([P, 4 * HD]), **slow).then_inc(ld_lam, 16)
            pool.dma_start(sub_g[:], da_subln_g.rearrange("o d -> d o"), **slow).then_inc(ld_lam, 16)
            for d in range(2):
                pool.dma_start(w0_col[:, d, :], rw_w0[0, d, :].rearrange("(j p) -> p j", p=P), **slow).then_inc(ld_rw, 16)
                pool.dma_start(a0_col[:, d, :], rw_a0[0, d, :].rearrange("(j p) -> p j", p=P), **slow).then_inc(ld_rw, 16)
            for col, src in ((kk_col, rw_k_k), (ka_col, rw_k_a), (lg_col, rw_ln_g), (lb_col, rw_ln_b),
                             (rk_col, rw_r_k.rearrange("o h d -> o (h d)"))):
                pool.dma_start(col[:], src.rearrange("o (j p) -> p (o j)", p=P), **slow).then_inc(ld_rw, 16)
            pool.dma_start(w2_sb[:], rw_w2.rearrange("o d r n -> (o d r) n")).then_inc(ld_rw, 16)
            pool.dma_start(a2_sb[:], rw_a2.rearrange("o d r n -> (o d r) n")).then_inc(ld_rw, 16)
            pool.dma_start(g2_sb[:], rw_g2.rearrange("o r n -> (o r) n")).then_inc(ld_rw, 16)


            pool.wait_ge(ld_rw, RW_LOADS)
            pool.wait_ge(masks_done, 1)
            pool.wait_ge(o_done, DA)
            with pool.Fori(0, NB) as i:
                for fixed, src in ((w2_pair, w2_sb), (a2_pair, a2_sb)):
                    pool.tensor_copy(fixed[:], src[:, bass.ds(i * P, P)]).then_inc(pair_w, 1)
                for d, r in enumerate(dirs):
                    pool.wait_ge(cum_done, 2 * i + d + 1)
                    pool.tensor_tensor(r.pexc, r.cum, r.sg, ALU.subtract).then_inc(feat_p, 1)
                    pool.wait_ge(by_act[d], upto(ACT_STEPS, "iclr", i))
                    pool.nop(nofuse=True)
                    pool.tensor_tensor(r.beta, pair_of(12, i), r.a, ALU.mult).then_inc(feat_p, 1)
                    pool.wait_ge(exps, 6 * i + 3 * d + 2)
                    pool.wait_ge(feat_p, 8 * i + 4 * d + 2)
                    pool.tensor_tensor(r.beta, r.beta, r.pinv, ALU.mult).then_inc(feat_p, 1)
                    pool.wait_ge(feat_v, 10 * i + 5 * d + 1)
                    pool.wait_ge(feat_p, 8 * i + 4 * d + 3)
                    pool.tensor_tensor(by_chunk(r.hat_b), by_chunk(r.beta), ptot[:, d, :].unsqueeze(2).to_broadcast([P, NC, CH]),
                                       ALU.mult).then_inc(feat_p, 1)
                for k in range(LEVELS):
                    for d, r in enumerate(dirs):
                        pool.wait_ge(by_dve[d], upto(DVE_STEPS, "gram_b", i) if k < 2 else upto(DVE_STEPS, "w0", i))
                        if k >= 2:
                            pool.wait_ge(mm[d], upto(STEPS, f"w{k - 2}", i))
                        pool.tensor_tensor(r.c[k % 2], r.la[:, :, 0:CH],
                                           level[:, d, k, :].unsqueeze(1).to_broadcast([P, NC, CH]), ALU.mult).then_inc(c_done[d], 1)
                for d, r in enumerate(dirs):
                    pool.wait_ge(mm[d], upto(STEPS, "w4", i))
                    pool.tensor_tensor(r.dg, eye[:].unsqueeze(1).to_broadcast([P, NC, CH]),
                                       ptot[:, d, :].unsqueeze(2).to_broadcast([P, NC, CH]), ALU.mult).then_inc(c_done[d], 1)
                for d in range(2):
                    pool.wait_ge(mm[d], (i + 1) * len(STEPS))
                    pool.wait_ge(by_dve[d], (i + 1) * len(DVE_STEPS))
                    pool.wait_ge(by_act[d], (i + 1) * len(ACT_STEPS))


            pool.wait_ge(e_done, 1)
            pool.wait_ge(h2_fixed, 1)
            pool.memset(w16[:], 0.0).then_inc(v_free, V_SLOTS)
            pool.memset(act16[:], 0.0).then_inc(u_free, U_SLOTS)
            pool.tensor_copy(idx_col[:, 0:1], e_idx[:, 0:1]).then_inc(col_done, 1)
            with pool.Fori(0, PH * NT) as u:
                for s in range(TOPK):
                    pool.wait_ge(col_done, u * TOPK + (s + 1))
                    pool.wait_ge(u_free, u * TOPK + (s + 1))
                    pool.wait_ge(v_free, u * TOPK + (s + 1))
                    if s == TOPK - 1:
                        pool.wait_ge(e_done, u + 2)
                    nxt = (s + 1) % TOPK
                    pool.tensor_copy(idx_col[:, nxt:nxt + 1], e_idx[:, bass.ds(u * TOPK + (s + 1), 1)]).then_inc(col_done, 1)
                    pool.indirect_dma_start(u_ring[:, s % U_SLOTS, :], None, peer_u,
                                            bass.IndirectOffsetOnAxis(idx_col[:, s:s + 1], 0)).then_inc(ld_u[s % U_SLOTS], 16)
                    pool.indirect_dma_start(v_ring[:, s % V_SLOTS, :], None, peer_v,
                                            bass.IndirectOffsetOnAxis(idx_col[:, s:s + 1], 0)).then_inc(ld_v[s % V_SLOTS], 16)

        @block.scalar
        def _(act):
            act.wait_ge(ld_c, 16)
            nc.scalar.activation(silu_c[:], c_col[:], ACT.Silu).then_inc(silu_done, 1)
            for t in range(NT):
                act.wait_ge(ld_x[t], 16)
                nc.scalar.activation(xs_rows[:, t, :], x_rows[:, t, :], ACT.Square, accum_out=sumsq[:, t:t + 1]).then_inc(ss_done, 1)
            act.wait_ge(rv_done, 1)
            nc.scalar.activation(rstd[:], rstd[:], ACT.Sqrt).then_inc(rstd_done, 1)
            act.wait_ge(mod1_done, 1)
            for j in range(KD):
                act.wait_ge(xT_mm, j + 1)
                nc.scalar.activation(hT[:, j, :], ps[:, j % 4, :], ACT.Identity, bias=mod1[:, j:j + 1],
                                     scale=mod1[:, 8 + j:9 + j]).then_inc(hT_done, 1)
            act.wait_ge(mu_done, 1)
            for b in range(15):
                act.wait_ge(proj_mm, b + 1)
                nc.scalar.activation(rw_dest(b), ps[:, b % 4, :], ACT.Copy, scale=mu_self[:, b:b + 1]).then_inc(proj_a, 1)
            for t in range(NT):
                act.wait_ge(v_mm, t + 1)
                nc.scalar.activation(vA[:, t, :], ps[:, 4 + t, :], ACT.Copy).then_inc(v_done, 1)
            for b in range(8):
                act.wait_ge(proj_mm, 16 + b)
                if b >= 2:
                    act.wait_ge(qk_stat, b - 1)
                nc.scalar.activation(sq[:, b % 2, :], ps[:, (15 + b) % 4, :], ACT.Square).then_inc(qk_sqr, 1)
            for b in range(NB):
                act.wait_ge(kk_raw, b + 1)
                if b < 2:
                    act.wait_ge(qk_stat, 7 + b)
                else:
                    act.wait_ge(kk_stat, b - 1)
                nc.scalar.activation(sq[:, b % 2, :], kkT[:, b, :], ACT.Square).then_inc(kk_sqr, 1)
            act.wait_ge(qk_var, 1)
            nc.scalar.activation(stat[0:16, :], stat[0:16, :], ACT.Sqrt, scale=qk_fold[:, 0:1]).then_inc(qk_rstd, 1)
            act.wait_ge(kk_stat, NB)
            nc.scalar.activation(stat_kk, ps[0:8, 5, :], ACT.Sqrt).then_inc(kk_norm, 1)
            act.wait_ge(proj_v, 15)
            nc.scalar.activation(loT[:, 0, :], loT[:, 0, :], ACT.Tanh).then_inc(lo_done, 1)
            nc.scalar.activation(loT[:, 2, :], loT[:, 2, :], ACT.Sigmoid).then_inc(lo_done, 1)
            act.wait_ge(lam_sum, 1)
            nc.scalar.activation(lam_e[:], lam_e[:], ACT.Exp).then_inc(lam_exp, 1)

            def evacuate(u):
                act.wait_ge(mixT_mm, u + 1)
                if u >= 2:
                    act.wait_ge(o_mm, u - 1)
                nc.scalar.activation(mixT[:, u % 2, :], ps[:, 4 + u % 2, :], ACT.Copy).then_inc(mixT_done, 1)

            def head_out(h):
                act.wait_ge(o_mm, NT * (h + 1))
                bank = ps[:, 6 + h % 2, :]
                nc.scalar.activation(sq_o[:, h, :], bank, ACT.Square).then_inc(o_sqr, 1)
                nc.scalar.activation(attT[:, h, :], bank, ACT.Copy, scale=sub_g[:, 0:1]).then_inc(o_copy, 1)

            act.wait_ge(ld_lam, 32)
            for u in range(UN):
                act.wait_ge(s_max, u + 1)
                for cmp in range(2):
                    pr = probs[:, 2 * (u % 2) + cmp, :]
                    nc.scalar.activation(pr, pr, ACT.Exp, bias=nmx[:, u % 2, cmp:cmp + 1],
                                         accum_out=den[:, u % 2, cmp:cmp + 1]).then_inc(s_exp, 1)
                if u >= 1:
                    evacuate(u - 1)
                if u % NT == 1 and u >= NT:
                    head_out(u // NT - 1)
            evacuate(UN - 1)
            head_out(DA - 1)
            act.wait_ge(o_var, 1)
            nc.scalar.activation(stat_o, stat_o, ACT.Sqrt, scale=(1.0 - LAMBDA0) ** 2).then_inc(o_rstd, 1)


            act.wait_ge(ld_rw, RW_LOADS)
            act.wait_ge(o_done, DA)
            with act.Fori(0, NB) as i:
                nc.scalar.activation(v_fix, pair_of(8, i), ACT.Copy).then_inc(v_fixed, 1)
                for d, r in enumerate(dirs):
                    act.wait_ge(mm[d], upto(STEPS, "decay", i))
                    nc.scalar.activation(r.sg, ps[:, 4 * d, :], ACT.Sigmoid, bias=w0_col[:, d, bass.ds(i, 1)]).then_inc(by_act[d], 1)
                    act.wait_ge(mm[d], upto(STEPS, "iclr", i))
                    nc.scalar.activation(r.a, ps[:, 4 * d + 2, :], ACT.Sigmoid, bias=a0_col[:, d, bass.ds(i, 1)]).then_inc(by_act[d], 1)
                act.wait_ge(vt_mm, i + 1)
                nc.scalar.activation(vt_u[:, 0, :], ps[:, 7, :], ACT.Copy).then_inc(vt_done, 1)
                for d, r in enumerate(dirs):
                    act.wait_ge(cum_done, 2 * i + d + 1)
                    nc.scalar.activation(r.pinc, r.cum, ACT.Exp, scale=-DECAY).then_inc(exps, 1)
                    nc.scalar.activation(r.pinv, r.cum, ACT.Exp, scale=DECAY).then_inc(exps, 1)
                    act.wait_ge(feat_p, 8 * i + 4 * d + 1)
                    nc.scalar.activation(r.pexc, r.pexc, ACT.Exp, scale=-DECAY).then_inc(exps, 1)

                def take(name, dst, scale=1.0, width=1):
                    for d, r in enumerate(dirs):
                        b = bank_of(d, name)
                        act.wait_ge(mm[d], upto(STEPS, name, i))
                        src = ps[:, b:b + width, :].rearrange("p b n -> p (b n)").rearrange("p (c n) -> p c n", c=NC)
                        nc.scalar.activation(dst(d, r), src, ACT.Copy, scale=scale).then_inc(by_act[d], 1)

                take("alpha_t", lambda d, r: r.rhs[:, :, 0:CH])
                take("beta_t", lambda d, r: r.beta_t)
                take("kappa_t", lambda d, r: r.kappa_t)
                take("mv", lambda d, r: r.rhs[:, :, CH:2 * CH])
                for k in range(1, LEVELS):
                    take(f"w{k}", lambda d, r: r.w)
                take("gh", lambda d, r: r.gh, scale=-1.0, width=2)
                take("psi", lambda d, r: by_chunk(pair_of(31 + d, i * 2)))
                for d in range(2):
                    act.wait_ge(mm[d], (i + 1) * len(STEPS))
                    act.wait_ge(by_dve[d], (i + 1) * len(DVE_STEPS))
            for b in range(NB):
                act.wait_ge(centred, b + 1)
                nc.scalar.activation(tmp2[:, b, :], YT[:, b, :], ACT.Square).then_inc(y_sqr, 1)
            act.wait_ge(y_var, 1)
            nc.scalar.activation(stat_y, stat_y, ACT.Sqrt).then_inc(y_rstd, 1)

            act.wait_ge(rw_out, NB)
            nc.scalar.activation(silu_rows, silu_c[:].unsqueeze(2).to_broadcast([P, KD, P]), ACT.Copy).then_inc(sr_done, 1)
            for g in range(4):
                act.wait_ge(keysT_mm, g + 1)
                nc.scalar.activation(keysT[:, 4 * g:4 * g + 4, :].rearrange("p b n -> p (b n)"), ps[:, 6 + g % 2, :], ACT.Copy).then_inc(keysT_done, 1)
            for t in range(NT):
                act.wait_ge(x1_done, 2 * t + 2)
                nc.scalar.activation(h2[:, t, :], x1[:, t, :], ACT.Square, accum_out=sumsq[:, t:t + 1]).then_inc(ss2, 1)
            act.wait_ge(rv2, 1)
            nc.scalar.activation(rstd[:], rstd[:], ACT.Sqrt).then_inc(rstd2, 1)
            for j in range(KD):
                act.wait_ge(h2T_mm, j + 1)
                nc.scalar.activation(h2T[:, j, :], ps[:, 6 + j % 2, :], ACT.Copy).then_inc(h2T_done, 1)
            for b in range(2 * PH):
                act.wait_ge(q_mm, b + 1)
                if b >= 4:
                    act.wait_ge(sc_mm, b - 3)
                nc.scalar.activation(qT[:, b % 4, :], ps[:, b % 4, :], ACT.Copy).then_inc(q_done, 1)

            def fix_scores(u):
                nc.scalar.activation(sc, scores_all[:, bass.ds(u * (2 * NKEY), 2 * NKEY)], ACT.Copy).then_inc(sc_fixed, 1)

            def gate_exp(u):
                act.wait_ge(neg_done, u + 1)
                nc.scalar.activation(g_exp_t[:], top[:, 2, :], ACT.Exp, bias=neg_top[:, 0:1], accum_out=g_den[:]).then_inc(g_exp, 1)

            act.wait_ge(sc_done, 2 * PH)
            with act.Fori(0, 2) as u:
                fix_scores(u)
                gate_exp(u)
            with act.Fori(0, PH * NT) as u:
                fix_scores(u + 2)
                for g in range(4):
                    act.wait_ge(u_free, u * TOPK + (U_SLOTS + 4 * g + 4))
                    nc.scalar.activation(gelu16[:, 4 * g:4 * g + 4], act16[:, 4 * g:4 * g + 4], ACT.Gelu).then_inc(gelu_done, 1)
                    if g == 1:
                        gate_exp(u + 2)
                    act.wait_ge(w_done, u * 4 + (g + 1))
                    for s in range(4 * g, 4 * g + 4):
                        act.wait_ge(v_free, u * TOPK + (s + 1))
                        nc.scalar.activation(diag[:, s % V_SLOTS, :], ident[:], ACT.Copy, scale=w16[:, s:s + 1]).then_inc(diags, 1)

        @block.tensor
        def _(pe):
            pe.wait_ge(silu_done, 1)
            for n in range(8):
                pe.wait_ge(ld_w[n % 4], 16 * (n // 4 + 1))
                w = strip(n)
                for h in range(2):
                    for k in range(KD):
                        last = nc.tensor.matmul(ps[:, 7, 2 * n + h:2 * n + h + 1], w[:, k, h * P:(h + 1) * P],
                                                silu_c[:, k:k + 1], start=(k == 0), stop=(k == KD - 1))
                last.then_inc(w_used, 1)
            pe.wait_ge(consts, CONSTS)
            pe.wait_ge(xs_done, NT)
            for j in range(KD):
                if j >= 4:
                    pe.wait_ge(hT_done, j - 3)
                for t in range(NT):
                    last = nc.tensor.transpose(ps[:, j % 4, t * P:(t + 1) * P], xs_rows[:, t, j * P:(j + 1) * P], ident[:])
                last.then_inc(xT_mm, 1)

            pe.wait_ge(hT_done, KD)

            def project(b, n, col):
                if col == 0:
                    pe.wait_ge(ld_w[n % 4], 16 * (n // 4 + 1))
                if b >= 4:
                    pe.wait_ge(proj_v, b - 3)
                w = strip(n)
                for k in range(KD):
                    last = nc.tensor.matmul(ps[:, b % 4, :], w[:, k, col:col + P], hT[:, k, :],
                                            start=(k == 0), stop=(k == KD - 1))
                last.then_inc(proj_mm, 1)

            pe.wait_ge(sel_done, 4)

            def qk_statistics(b):
                pe.wait_ge(qk_sqr, b + 1)
                nc.tensor.matmul(ps[0:16, 4, :], sel[:, b, :], sq[:, b % 2, :], start=(b == 0), stop=(b == 7)).then_inc(qk_stat, 1)

            for b, (n, col) in enumerate(rw_blocks):
                project(b, n, col)
            for n in (16, 17):
                pe.wait_ge(ld_w[n % 4], 16 * (n // 4 + 1))
            for t in range(NT):
                for i in range(2):
                    for k in range(KD):
                        last = nc.tensor.matmul(ps[:, 4 + t, 256 * i:256 * i + 256], hT[:, k, t * P:(t + 1) * P],
                                                strip(16 + i)[:, k, :], start=(k == 0), stop=(k == KD - 1))
                last.then_inc(v_mm, 1)
            pe.wait_ge(v_done, NT)
            for b, (n, col) in enumerate(qk_blocks):
                project(15 + b, n, col)
                if b >= 1:
                    qk_statistics(b - 1)
            qk_statistics(7)
            for b in range(NB):
                pe.wait_ge(kk_sqr, b + 1)
                nc.tensor.matmul(ps[0:8, 5, :], sel[:, b, 0:8], sq[:, b % 2, :], start=(b == 0), stop=(b == NB - 1)).then_inc(kk_stat, 1)
            pe.wait_ge(proj_v, 23)
            pe.wait_ge(qk_rstd, 1)
            for b in range(8):
                if b >= 4:
                    pe.wait_ge(qk_done, b - 3)
                nc.tensor.matmul(ps[:, b % 4, :], selT[:, b, :], stat[:], start=True, stop=True).then_inc(qk_bc, 1)
            pe.wait_ge(kk_inv, 1)
            for b in range(NB):
                pe.wait_ge(qk_done, b + 5)
                nc.tensor.matmul(ps[:, b, :], selT[0:8, b, :], stat_kk, start=True, stop=True).then_inc(kk_bc, 1)

            def scores(u):
                h, qt = u // NT, u % NT
                if u < 2:
                    pe.wait_ge(kk_done, NB)
                else:
                    pe.wait_ge(s_max, u - 1)
                for cmp in range(2):
                    r = slice(HD * cmp, HD * cmp + HD)
                    last = nc.tensor.matmul(ps[:, 2 * (u % 2) + cmp, :], qkT[r, h, qt * P:(qt + 1) * P], qkT[r, DA + h, :],
                                            start=True, stop=True)
                last.then_inc(s_mm, 1)

            def transpose_mix(u):
                pe.wait_ge(mixed, u + 1)
                if u >= 2:
                    pe.wait_ge(mixT_done, u - 1)
                for kt in range(NT):
                    last = nc.tensor.transpose(ps[:, 4 + u % 2, kt * P:(kt + 1) * P], mix[:, u % 2, kt * P:(kt + 1) * P], ident[:])
                last.then_inc(mixT_mm, 1)

            def values(u):
                h, qt = u // NT, u % NT
                pe.wait_ge(mixT_done, u + 1)
                if h >= 2 and qt == 0:
                    pe.wait_ge(o_copy, h - 1)
                for kt in range(NT):
                    last = nc.tensor.matmul(ps[:, 6 + h % 2, qt * P:(qt + 1) * P], vA[:, kt, h * P:(h + 1) * P],
                                            mixT[:, u % 2, kt * P:(kt + 1) * P], start=(kt == 0), stop=(kt == NT - 1))
                last.then_inc(o_mm, 1)

            scores(0)
            for u in range(UN):
                if u + 1 < UN:
                    scores(u + 1)
                transpose_mix(u)
                if u >= 1:
                    values(u - 1)
            values(UN - 1)
            pe.wait_ge(o_copy, DA)
            pe.wait_ge(s_max, UN)
            for h in range(DA):
                last = nc.tensor.matmul(ps[0:DA, 0, :], selh[:, h, :], sq_o[:, h, :], start=(h == 0), stop=(h == DA - 1))
            last.then_inc(o_stat, 1)
            pe.wait_ge(o_rstd, 1)
            for h in range(DA):
                nc.tensor.matmul(ps[:, 1 + h, :], selhT[:, h, :], stat_o, start=True, stop=True).then_inc(o_bc, 1)


            def each(d, name, *terms):
                b0 = bank_of(d, name)
                pe.nop(nofuse=True)
                for ch in range(NC):
                    for n, (lhs, rhs) in enumerate(terms):
                        for h in range(2):
                            r = slice(HD * h, HD * h + HD)
                            right = rhs(r, ch)
                            w = right.shape[-1]
                            col = ch * w
                            last = nc.tensor.matmul(ps[r, b0 + col // 512, col % 512:col % 512 + w], lhs(r, ch), right,
                                                    start=(n == 0), stop=(n == len(terms) - 1))
                return last

            def at(ap, c0=0, w=CH):
                return lambda r, ch: ap[r, ch, c0:c0 + w]

            def half_ident(r, ch):
                return ident[r, r]

            pe.wait_ge(o_done, DA)
            pe.wait_ge(lo_done, 2)
            pe.wait_ge(masks_done, 1)
            with pe.Fori(0, NB) as i:
                pe.wait_ge(pair_w, 2 * i + 2)
                for name, w, slot in (("decay", w2_pair, 0), ("iclr", a2_pair, 1)):
                    for d in range(2):
                        r = slice(HD * d, HD * d + HD)
                        nc.tensor.matmul(ps[:, bank_of(d, name), :], w[r, :], loT[r, slot, :], start=True, stop=True).then_inc(mm[d], 1)
                pe.wait_ge(v_fixed, i + 1)
                pe.nop(nofuse=True)
                for ch in range(NC):
                    for h in range(2):
                        r = slice(HD * h, HD * h + HD)
                        last = nc.tensor.matmul(ps[r, 7, ch * CH:(ch + 1) * CH], v_fix[r, ch * CH:(ch + 1) * CH], ident[r, r],
                                                start=True, stop=True)
                last.then_inc(vt_mm, 1)
                for d, r in enumerate(dirs):
                    pe.wait_ge(feat_v, 10 * i + 5 * d + 3)
                    pe.wait_ge(by_act[d], upto(ACT_STEPS, "decay", i))
                    each(d, "alpha_t", (at(r.ar), half_ident)).then_inc(mm[d], 1)
                for d, r in enumerate(dirs):
                    pe.wait_ge(feat_p, 8 * i + 4 * d + 4)
                    each(d, "beta_t", (at(by_chunk(r.hat_b)), half_ident)).then_inc(mm[d], 1)
                for d, r in enumerate(dirs):
                    pe.wait_ge(feat_v, 10 * i + 5 * d + 5)
                    pe.wait_ge(by_act[d], upto(ACT_STEPS, "alpha_t", i))
                    each(d, "kappa_t", (at(by_chunk(r.hat_k)), half_ident)).then_inc(mm[d], 1)
                pe.wait_ge(vt_done, i + 1)
                for d, r in enumerate(dirs):
                    pe.wait_ge(by_act[d], upto(ACT_STEPS, "beta_t", i))
                    each(d, "gram_b", (at(by_chunk(r.beta)), at(r.ar, 0, 2 * CH))).then_inc(mm[d], 1)
                for d, r in enumerate(dirs):
                    pe.wait_ge(by_act[d], upto(ACT_STEPS, "kappa_t", i))
                    each(d, "gram_k", (at(by_chunk(r.kappa)), at(r.ar, 0, 2 * CH))).then_inc(mm[d], 1)
                for d, r in enumerate(dirs):
                    pe.wait_ge(by_dve[d], upto(DVE_STEPS, "gram_k", i))
                    each(d, "mv", (at(r.mb), at(v_t))).then_inc(mm[d], 1)
                for d, r in enumerate(dirs):
                    pe.wait_ge(c_done[d], 7 * i + 1)
                    each(d, "w0", (at(r.c[0]), half_ident)).then_inc(mm[d], 1)
                for k in range(1, LEVELS):
                    for d, r in enumerate(dirs):
                        pe.wait_ge(c_done[d], 7 * i + 1 + k)
                        pe.wait_ge(by_dve[d], upto(DVE_STEPS, f"xt{k - 1}" if k > 1 else "w0", i))
                        pe.wait_ge(by_act[d], upto(ACT_STEPS, f"w{k - 1}" if k > 1 else "mv", i))
                        each(d, f"w{k}", (at(r.c[k % 2]), at(r.x))).then_inc(mm[d], 1)
                    for kind in ("x", "xt"):
                        if kind == "x" and k == LEVELS - 1:
                            continue
                        for d, r in enumerate(dirs):
                            pe.wait_ge(by_act[d], upto(ACT_STEPS, f"w{k}", i))
                            if kind == "x":
                                each(d, f"x{k}", (at(r.xt), at(r.w))).then_inc(mm[d], 1)
                            else:
                                each(d, f"xt{k}", (at(r.w), at(r.xt))).then_inc(mm[d], 1)
                for d, r in enumerate(dirs):
                    pe.wait_ge(by_dve[d], upto(DVE_STEPS, f"xt{LEVELS - 1}", i))
                    each(d, "gh", (at(r.xt), at(r.rhs, 0, 2 * CH))).then_inc(mm[d], 1)
                for d, r in enumerate(dirs):
                    pe.wait_ge(by_act[d], upto(ACT_STEPS, "gh", i))
                    each(d, "phi", (at(r.gh), at(r.beta_t))).then_inc(mm[d], 1)
                for d, r in enumerate(dirs):
                    each(d, "psi", (at(r.kappa_t), at(v_t)), (at(r.beta_t), at(r.gh, CH))).then_inc(mm[d], 1)
                for d, r in enumerate(dirs):
                    pe.wait_ge(by_dve[d], upto(DVE_STEPS, "phi", i))
                    each(d, "rho", (at(r.gh), at(r.la, CH))).then_inc(mm[d], 1)
                for d, r in enumerate(dirs):
                    pe.wait_ge(by_act[d], upto(ACT_STEPS, "psi", i))
                    each(d, "y", (at(v_t), at(r.mb, CH)), (at(r.gh, CH), at(r.la, CH))).then_inc(mm[d], 1)
                for d in range(2):
                    pe.wait_ge(by_dve[d], (i + 1) * len(DVE_STEPS))
                    pe.wait_ge(by_act[d], (i + 1) * len(ACT_STEPS))
            for st in range(1, NC - 1):
                pe.wait_ge(state_done, 2 * st)
                for q in range(2 * NB):
                    ch = st if q % 2 == 0 else NC - 1 - st
                    for h in range(2):
                        r = slice(HD * h, HD * h + HD)
                        last = nc.tensor.matmul(ps[r, st % 2, q * CH:(q + 1) * CH], PHI[r, q, ch * CH:(ch + 1) * CH],
                                                states[r, st, q * CH:(q + 1) * CH], start=True, stop=True)
                last.then_inc(state_mm, 1)
            pe.wait_ge(state_done, 2 * (NC - 1))
            for b in range(NB):
                for ch in range(NC):
                    terms = [(q, st) for q, st in ((2 * b, ch), (2 * b + 1, NC - 1 - ch)) if st > 0]
                    for n, (q, st) in enumerate(terms):
                        for h in range(2):
                            r = slice(HD * h, HD * h + HD)
                            last = nc.tensor.matmul(ps[r, 2 + b, ch * CH:(ch + 1) * CH], states[r, st, q * CH:(q + 1) * CH],
                                                    RP[r, q, ch * CH:(ch + 1) * CH], start=(n == 0), stop=(n == len(terms) - 1))
                last.then_inc(yst_mm, 1)
            for b in range(NB):
                pe.wait_ge(y_sum, b + 1)
                nc.tensor.matmul(ps[:, 2 + b, :], half_ones[:], YT[:, b, :], start=True, stop=True).then_inc(mean_mm, 1)
            for b in range(NB):
                pe.wait_ge(y_sqr, b + 1)
                last = nc.tensor.matmul(ps[0:8, 0, :], sel[:, b, 0:8], tmp2[:, b, :], start=(b == 0), stop=(b == NB - 1))
            last.then_inc(y_stat, 1)
            for b in range(NB):
                pe.wait_ge(rk_done, b + 1)
                if b >= 2:
                    pe.wait_ge(bon_done, b - 1)
                nc.tensor.matmul(ps[:, 6 + b % 2, :], half_ones[:], tmp[:, b, :], start=True, stop=True).then_inc(bon_mm, 1)
            pe.wait_ge(centred, NB)
            for b in range(NB):
                if b == 0:
                    pe.wait_ge(y_rstd, 1)
                nc.tensor.matmul(ps[:, 2 + b, :], selT[0:8, b, :], stat_y, start=True, stop=True).then_inc(y_bc, 1)
            for b in range(NB):
                if b < 2:
                    pe.wait_ge(bon_done, NB - 1 + b)
                else:
                    pe.wait_ge(rw_out, b - 1)
                nc.tensor.matmul(ps[:, 6 + b % 2, :], g2_sb[:, b * P:(b + 1) * P], loT[:, 2, :], start=True, stop=True).then_inc(gate_mm, 1)

            pe.wait_ge(rw_out, NB)
            pe.wait_ge(sr_done, 1)

            def mod_strip(n):
                pe.wait_ge(ld_w[n % 4], ring2_loaded(n))
                if n >= 2:
                    pe.wait_ge(rows_done, n - 1)
                for k in range(KD):
                    last = nc.tensor.matmul(ps[:, n % 2, 0:256], silu_rows[:, k, :], strip2(n)[:, k, :],
                                            start=(k == 0), stop=(k == KD - 1))
                last.then_inc(rows_mm, 1)

            for n in range(4):
                mod_strip(n)
            pe.wait_ge(ld_wo, 16)
            for t in range(NT):
                for n in range(2):
                    if 2 * t + n >= 4:
                        pe.wait_ge(wo_gated, 2 * t + n - 3)
                    for k in range(KD):
                        last = nc.tensor.matmul(ps[:, 2 + (2 * t + n) % 4, :], cat(k)[:, t * P:(t + 1) * P], wo[:, k, n * 512:(n + 1) * 512],
                                                start=(k == 0), stop=(k == KD - 1))
                    last.then_inc(wo_mm, 1)
            for n in range(4, 16):
                mod_strip(n)
            pe.wait_ge(ld_keys, 16)
            for g in range(4):
                if g >= 2:
                    pe.wait_ge(keysT_done, g - 1)
                for b in range(4):
                    last = nc.tensor.transpose(ps[:, 6 + g % 2, b * P:(b + 1) * P], keys_raw[:, 4 * g + b, :], ident[:])
                last.then_inc(keysT_mm, 1)
            pe.wait_ge(keysT_done, 4)
            pe.wait_ge(h2_done, NT)
            for j in range(KD):
                if j >= 2:
                    pe.wait_ge(h2T_done, j - 1)
                for t in range(NT):
                    last = nc.tensor.transpose(ps[:, 6 + j % 2, t * P:(t + 1) * P], h2[:, t, j * P:(j + 1) * P], ident[:])
                last.then_inc(h2T_mm, 1)
            pe.wait_ge(h2T_done, KD)

            def key_scores(b):
                pe.wait_ge(q_done, b + 1)
                if b >= 4:
                    pe.wait_ge(sc_done, b - 3)
                for t in range(NT):
                    last = nc.tensor.matmul(ps[:, 4 + b % 4, t * P:(t + 1) * P], qT[:, b % 4, t * P:(t + 1) * P], keysT[:, b, :],
                                            start=True, stop=True)
                last.then_inc(sc_mm, 1)

            for b in range(2 * PH):
                n = 16 + b // 2
                if b % 2 == 0:
                    pe.wait_ge(ld_w[n % 4], ring2_loaded(n))
                if b >= 4:
                    pe.wait_ge(q_done, b - 3)
                for k in range(KD):
                    last = nc.tensor.matmul(ps[:, b % 4, :], strip2(n)[:, k, P * (b % 2):P * (b % 2) + P], h2T[:, k, :],
                                            start=(k == 0), stop=(k == KD - 1))
                last.then_inc(q_mm, 1)
                if b >= 1:
                    key_scores(b - 1)
            key_scores(2 * PH - 1)

            pe.wait_ge(q_done, 2 * PH)
            with pe.Fori(0, NT) as t:
                for n in range(2):
                    nc.tensor.matmul(ps[:, n, :], zero_w[0:1, :], restart[0:1, :], start=True, stop=False)
                with pe.Fori(0, PH) as h:
                    for s in range(TOPK):
                        pe.wait_ge(diags, t * SLOTS + h * TOPK + (s + 1))
                        pe.wait_ge(ld_v[s % V_SLOTS], t * (PH * 32) + h * 32 + 16 * (s // V_SLOTS + 1))
                        for n in range(2):
                            last = nc.tensor.matmul(ps[:, n, :], diag[:, s % V_SLOTS, :], v_ring[:, s % V_SLOTS, n * 512:(n + 1) * 512],
                                                    start=False, stop=False)
                        last.then_inc(v_free, 1)
                for n in range(2):
                    last = nc.tensor.matmul(ps[:, n, :], zero_w[0:1, :], restart[0:1, :], start=False, stop=True)
                last.then_inc(tile_mm, 1)
                pe.wait_ge(o_gated, t * 2 + 2)

        @block.vector
        def _(dve):
            step = Tally(dve, dve_s)
            v = nc.vector
            dve.wait_ge(zeroed, 8)
            sel_flat = sel[:].rearrange("p b m -> p (b m)")
            for h in range(2):
                v.memset(sel_flat[HD * h:HD * h + HD, h:h + 127:18], 1.0).then_inc(sel_done, 1)
                v.memset(half_ones[HD * h:HD * h + HD, HD * h:HD * h + HD], 1.0).then_inc(sel_done, 1)
            dve.wait_ge(consts, CONSTS)
            step.link(v.scalar_tensor_tensor(bias_h[:, 0, :], bias_h[:, 0, :], -1.0, bias_h[:, 0, :], ALU.mult, ALU.min))
            for h in (3, 2, 1, 0):
                v.tensor_scalar(bias_h[:, h, :], bias_h[:, 0, :], 2.0 ** (-8.0 * (h + 1) / DA), None, ALU.mult).then_inc(bias_done, 1)
            step.link(v.tensor_scalar(s_idx[:], s_idx[:], CH - 1, None, ALU.bitwise_and))
            step(v.tensor_tensor(xor_idx[:], s_idx[:], t_idx[:], ALU.bitwise_xor))
            step(v.tensor_tensor(tri[:, 0, 0, :], s_idx[:], t_idx[:], ALU.is_lt))
            step(v.tensor_tensor(tri[:, 1, 0, :], s_idx[:], t_idx[:], ALU.is_gt))
            step(v.tensor_tensor(tri[:, 0, 1, :], s_idx[:], t_idx[:], ALU.is_le))
            step(v.tensor_tensor(tri[:, 1, 1, :], s_idx[:], t_idx[:], ALU.is_gt))
            step.link(v.tensor_tensor(eye[:], s_idx[:], t_idx[:], ALU.is_equal))
            for k in range(LEVELS):
                step.link(v.tensor_scalar(level[:, 1, k, :], xor_idx[:], float(2 ** k), None, ALU.is_ge))
                step.link(v.scalar_tensor_tensor(level[:, 1, k, :], xor_idx[:], float(2 ** (k + 1)), level[:, 1, k, :], ALU.is_lt, ALU.mult))
                step(v.tensor_tensor(level[:, 0, k, :], level[:, 1, k, :], tri[:, 0, 0, :], ALU.mult))
                last = v.tensor_tensor(level[:, 1, k, :], level[:, 1, k, :], tri[:, 1, 0, :], ALU.mult)
                if k < LEVELS - 1:
                    step(last)
            last.then_inc(masks_done, 1)
            dve.wait_ge(ss_done, NT)
            step.link(v.tensor_scalar(rstd[:], sumsq[:], 1.0 / D, NORM_EPS, ALU.mult, ALU.add))
            v.reciprocal(rstd[:], rstd[:]).then_inc(rv_done, 1)
            dve.wait_ge(ld_mu, 16 * 6)
            step.link(v.tensor_tensor(mu_self[:], mu[:, 0, :], mu[:, 1, :], ALU.add))
            v.tensor_scalar(mu_self[:], mu_self[:], -1.0, 1.0, ALU.mult, ALU.add).then_inc(mu_done, 1)
            dve.wait_ge(rstd_done, 1)
            for t in range(NT):
                v.tensor_scalar(xs_rows[:, t, :], x_rows[:, t, :], rstd[:, t:t + 1], None, ALU.mult).then_inc(xs_done, 1)
            dve.wait_ge(ld_par, 32)
            dve.wait_ge(w_used, 8)
            step.link(v.tensor_tensor(mod1[:], ps[:, 7, 0:16], ada_bc[:], ALU.add))
            v.scalar_tensor_tensor(mod1[:, 8:16], mod1[:, 8:16], 1.0, n1_col[:], ALU.add, ALU.mult).then_inc(mod1_done, 1)
            dve.wait_ge(ld_lam, 32)
            lam4 = lam[:].rearrange("p (a d) -> p a d", a=4)
            step.link(v.tensor_tensor(lam_p[:].rearrange("p (a d) -> p a d", a=2), lam4[:, 0:4:2, :], lam4[:, 1:4:2, :], ALU.mult))
            v.tensor_reduce(lam_e[:], lam_p[:].rearrange("p (a d) -> p a d", a=2), AX.X, ALU.add).then_inc(lam_sum, 1)
            dve.wait_ge(ld_rw, RW_LOADS)
            step(v.tensor_scalar(ka1_col[:], ka_col[:], -1.0, 1.0, ALU.mult, ALU.add))

            for b in range(15):
                dve.wait_ge(proj_a, b + 1)
                bank, dst = ps[:, b % 4, :], rw_dest(b)
                step.link(v.scalar_tensor_tensor(dst[:, 1:S], bank[:, 0:S - 1], mu[:, 0, b:b + 1], dst[:, 1:S], ALU.mult, ALU.add))
                v.scalar_tensor_tensor(dst[:, 0:S - 1], bank[:, 1:S], mu[:, 1, b:b + 1], dst[:, 0:S - 1], ALU.mult, ALU.add).then_inc(proj_v, 1)
            dve.wait_ge(proj_v, 15)
            for b in range(NB):
                v.tensor_scalar(kkT[:, b, :], kT[:, b, :], kk_col[:, b:b + 1], None, ALU.mult).then_inc(kk_raw, 1)
            for b in range(8):
                dve.wait_ge(qk_sqr, b + 1)
                v.tensor_scalar(qkT[:, b, :], ps[:, (15 + b) % 4, :], qk_gain[:, b // 4:b // 4 + 1], None, ALU.mult).then_inc(proj_v, 1)
            dve.wait_ge(qk_stat, 8)
            step.link(v.tensor_scalar(stat[:], ps[0:16, 4, :], 1.0 / HD, NORM_EPS, ALU.mult, ALU.add))
            v.reciprocal(stat[:], stat[:]).then_inc(qk_var, 1)
            dve.wait_ge(kk_norm, 1)
            step.link(v.tensor_scalar(stat_kk, stat_kk, 1e-12, None, ALU.max))
            v.reciprocal(stat_kk, stat_kk).then_inc(kk_inv, 1)
            for b in range(8):
                dve.wait_ge(qk_bc, b + 1)
                v.tensor_tensor(qkT[:, b, :], ps[:, b % 4, :], qkT[:, b, :], ALU.mult).then_inc(qk_done, 1)
            for b in range(NB):
                dve.wait_ge(kk_bc, b + 1)
                v.tensor_tensor(kkT[:, b, :], ps[:, b, :], kkT[:, b, :], ALU.mult).then_inc(kk_done, 1)
            dve.wait_ge(lam_exp, 1)
            step.link(v.tensor_tensor(neg_lam[:], lam_e[:, 1:2], lam_e[:, 0:1], ALU.subtract))
            step.link(v.tensor_scalar(neg_lam[:], neg_lam[:], -LAMBDA0, None, ALU.add))

            def maxima(u):
                h, qt, e = u // NT, u % NT, u % 2
                dve.wait_ge(s_mm, u + 1)
                first = 384 - qt * P
                for cmp in range(2):
                    step(v.tensor_tensor_reduce(out=probs[:, 2 * e + cmp, :], in0=ps[:, 2 * e + cmp, :],
                                                in1=bias_h[:, h, first:first + S], scale=1.0, scalar=LOWEST,
                                                op0=ALU.add, op1=ALU.max, accum_out=mx[:, e, cmp:cmp + 1]))
                step.eng.wait_ge(step.sem, step.n)
                v.tensor_scalar(nmx[:, e, :], mx[:, e, :], -1.0, None, ALU.mult).then_inc(s_max, 1)

            def mixture(u):
                e = u % 2
                dve.wait_ge(s_exp, 2 * u + 2)
                step.link(v.reciprocal(rden[:, e, :], den[:, e, :]))
                step(v.tensor_scalar(rden[:, e, 1:2], rden[:, e, 1:2], neg_lam[:, 0:1], None, ALU.mult))
                step.link(v.tensor_scalar(probs[:, 2 * e, :], probs[:, 2 * e, :], rden[:, e, 0:1], None, ALU.mult))
                if u >= 2:
                    dve.wait_ge(mixT_mm, u - 1)
                v.scalar_tensor_tensor(mix[:, e, :], probs[:, 2 * e + 1, :], rden[:, e, 1:2], probs[:, 2 * e, :],
                                       ALU.mult, ALU.add).then_inc(mixed, 1)

            dve.wait_ge(bias_done, DA)
            maxima(0)
            for u in range(UN):
                if u + 1 < UN:
                    maxima(u + 1)
                mixture(u)
            dve.wait_ge(o_stat, 1)
            step.link(v.tensor_scalar(stat_o, ps[0:DA, 0, :], 1.0 / P, NORM_EPS, ALU.mult, ALU.add))
            v.reciprocal(stat_o, stat_o).then_inc(o_var, 1)
            for h in range(DA):
                dve.wait_ge(o_bc, h + 1)
                v.tensor_tensor(attT[:, h, :], ps[:, 1 + h, :], attT[:, h, :], ALU.mult).then_inc(o_done, 1)


            with dve.Fori(0, NB) as i:
                for d, r in enumerate(dirs):
                    dve.wait_ge(by_act[d], upto(ACT_STEPS, "decay", i))
                    turn = (lambda ap: ap) if d == 0 else (lambda ap: ap[:, ::-1])
                    v.tensor_tensor_scan(turn(r.cum), restart[:], turn(r.sg), 0.0, ALU.mult, ALU.add).then_inc(cum_done, 1)
                for d, r in enumerate(dirs):
                    end = CH - 1 if d == 0 else 0
                    dve.wait_ge(by_act[d], upto(ACT_STEPS, "iclr", i))
                    v.tensor_scalar(r.kappa, r.a, ka_col[:, bass.ds(i, 1)], ka1_col[:, bass.ds(i, 1)], ALU.mult, ALU.add).then_inc(kap, 1)
                    dve.wait_ge(kap, 4 * i + 2 * d + 1)
                    v.tensor_tensor(r.kappa, r.kappa, pair_of(4, i), ALU.mult).then_inc(kap, 1)
                    dve.wait_ge(exps, 6 * i + 3 * d + 2)
                    v.tensor_copy(ptot[:, d, :].unsqueeze(2), by_chunk(r.pinc)[:, :, end:end + 1]).then_inc(feat_v, 1)
                    dve.wait_ge(kap, 4 * i + 2 * d + 2)
                    v.tensor_tensor(r.kappa, r.kappa, r.pinv, ALU.mult).then_inc(feat_v, 1)
                    dve.wait_ge(exps, 6 * i + 3 * d + 3)
                    v.tensor_tensor(r.ar[:, :, 0:CH], by_chunk(r.pexc), by_chunk(pair_of(12, i)), ALU.mult).then_inc(feat_v, 1)
                    v.tensor_tensor(r.ar[:, :, CH:2 * CH], by_chunk(r.pinc if d == 0 else r.pexc), by_chunk(pair_of(0, i)),
                                    ALU.mult).then_inc(feat_v, 1)
                    dve.wait_ge(feat_v, 10 * i + 5 * d + 2)
                    v.tensor_tensor(by_chunk(r.hat_k), by_chunk(r.kappa), ptot[:, d, :].unsqueeze(2).to_broadcast([P, NC, CH]),
                                    ALU.mult).then_inc(feat_v, 1)

                def banks(d, name, width=1):
                    b = bank_of(d, name)
                    return ps[:, b:b + width, :].rearrange("p b n -> p (b n)").rearrange("p (c n) -> p c n", c=NC)

                for name in ("gram_b", "gram_k"):
                    for d, r in enumerate(dirs):
                        dve.wait_ge(mm[d], upto(STEPS, name, i))
                        mask = tri[:, d, :, :].rearrange("p a t -> p (a t)").unsqueeze(1).to_broadcast([P, NC, 2 * CH])
                        v.tensor_tensor(r.la if name == "gram_b" else r.mb, banks(d, name, 2), mask, ALU.mult).then_inc(by_dve[d], 1)
                for d, r in enumerate(dirs):
                    eyes = eye[:].unsqueeze(1).to_broadcast([P, NC, CH])
                    dve.wait_ge(mm[d], upto(STEPS, "w0", i))
                    v.tensor_tensor(r.x, eyes, banks(d, "w0"), ALU.subtract).then_inc(x_one, 1)
                    v.tensor_tensor(r.xt, eyes, r.c[0], ALU.subtract).then_inc(by_dve[d], 1)
                for k in range(1, LEVELS):
                    for kind in ("x", "xt"):
                        if kind == "x" and k == LEVELS - 1:
                            continue
                        for d, r in enumerate(dirs):
                            dst = r.x if kind == "x" else r.xt
                            dve.wait_ge(mm[d], upto(STEPS, f"{kind}{k}", i))
                            if k == 1 and kind == "x":
                                dve.wait_ge(x_one, 2 * i + d + 1)
                            v.tensor_tensor(dst, dst, banks(d, f"{kind}{k}"), ALU.subtract).then_inc(by_dve[d], 1)
                for d, r in enumerate(dirs):
                    dve.wait_ge(c_done[d], 7 * i + 7)
                    dve.wait_ge(mm[d], upto(STEPS, "phi", i))
                    v.tensor_tensor(by_chunk(pair_of(23 + d, i * 2)), r.dg, banks(d, "phi"), ALU.add).then_inc(by_dve[d], 1)
                for d, r in enumerate(dirs):
                    dve.wait_ge(mm[d], upto(STEPS, "rho", i))
                    v.tensor_tensor(by_chunk(pair_of(39 + d, i * 2)), r.ar[:, :, CH:2 * CH], banks(d, "rho"), ALU.add).then_inc(by_dve[d], 1)
                dve.wait_ge(mm[0], upto(STEPS, "y", i))
                v.tensor_copy(by_chunk(pair_of(47, i)), banks(0, "y")).then_inc(by_dve[0], 1)
                dve.wait_ge(mm[1], upto(STEPS, "y", i))
                dve.wait_ge(by_dve[0], upto(DVE_STEPS, "y", i))
                v.tensor_tensor(by_chunk(pair_of(47, i)), by_chunk(pair_of(47, i)), banks(1, "y"), ALU.add).then_inc(by_dve[1], 1)
                for d in range(2):
                    dve.wait_ge(mm[d], (i + 1) * len(STEPS))
                    dve.wait_ge(by_act[d], (i + 1) * len(ACT_STEPS))
                    dve.wait_ge(by_dve[d], (i + 1) * len(DVE_STEPS))
                    dve.wait_ge(c_done[d], 7 * i + 7)


            def of_dir(ap, d):
                return ap.rearrange("p (b n) -> p b n", b=NB)[:, :, d * CH:(d + 1) * CH]

            psi = PSI.rearrange("p (b a) n -> p b a n", a=2)
            for st in range(NC - 1):
                for d in range(2):
                    ch = st if d == 0 else NC - 1 - st
                    dst, part = of_dir(states[:, st + 1, :], d), psi[:, :, d, ch * CH:(ch + 1) * CH]
                    if st == 0:
                        v.tensor_copy(dst, part).then_inc(state_done, 1)
                    else:
                        dve.wait_ge(state_mm, st)
                        v.tensor_tensor(dst, of_dir(ps[:, st % 2, :], d), part, ALU.add).then_inc(state_done, 1)
            for b in range(NB):
                v.scalar_tensor_tensor(tmp[:, b, :], rT[:, b, :], rk_col[:, b:b + 1], kT[:, b, :], ALU.mult, ALU.mult).then_inc(rk_done, 1)
            for b in range(NB):
                dve.wait_ge(yst_mm, b + 1)
                v.tensor_tensor(YT[:, b, :], YT[:, b, :], ps[:, 2 + b, :], ALU.add).then_inc(y_sum, 1)
            for b in range(NB):
                dve.wait_ge(y_sum, b + 1)
                dve.wait_ge(mean_mm, b + 1)
                v.scalar_tensor_tensor(YT[:, b, :], ps[:, 2 + b, :], -1.0 / HD, YT[:, b, :], ALU.mult, ALU.add).then_inc(centred, 1)
            dve.wait_ge(y_stat, 1)
            step.link(v.tensor_scalar(stat_y, ps[0:8, 0, :], 1.0 / HD, GN_EPS, ALU.mult, ALU.add))
            v.reciprocal(stat_y, stat_y).then_inc(y_var, 1)
            for b in range(NB):
                dve.wait_ge(bon_mm, b + 1)
                v.tensor_tensor(tmp[:, b, :], ps[:, 6 + b % 2, :], vT[:, b, :], ALU.mult).then_inc(bon_done, 1)
            dve.wait_ge(y_sqr, NB)
            for b in range(NB):
                dve.wait_ge(y_bc, b + 1)
                step.link(v.tensor_tensor(YT[:, b, :], YT[:, b, :], ps[:, 2 + b, :], ALU.mult))
                step.link(v.tensor_scalar(YT[:, b, :], YT[:, b, :], lg_col[:, b:b + 1], lb_col[:, b:b + 1], ALU.mult, ALU.add))
                dve.wait_ge(bon_done, b + 1)
                step.link(v.tensor_tensor(YT[:, b, :], YT[:, b, :], tmp[:, b, :], ALU.add))
                dve.wait_ge(gate_mm, b + 1)
                v.tensor_tensor(YT[:, b, :], YT[:, b, :], ps[:, 6 + b % 2, :], ALU.mult).then_inc(rw_out, 1)

            dve.wait_ge(ld_rows, 80)
            mod_flat = mod_rows.rearrange("p m d -> p (m d)")

            def mod_add(n):
                dve.wait_ge(rows_mm, n + 1)
                c0 = 256 * n
                v.tensor_tensor(mod_flat[:, c0:c0 + 256], mod_flat[:, c0:c0 + 256], ps[:, n % 2, 0:256], ALU.add).then_inc(rows_done, 1)

            for n in range(4):
                mod_add(n)
            dve.wait_ge(rows_done, 4)
            for t in range(NT):
                dve.wait_ge(ld_x[t], 32)
                for n in range(2):
                    g, cols = 2 * t + n, slice(512 * n, 512 * n + 512)
                    dve.wait_ge(wo_mm, g + 1)
                    v.tensor_tensor(h2[:, t, cols], ps[:, 2 + g % 4, :], gate1[:, cols], ALU.mult).then_inc(wo_gated, 1)
                    dve.wait_ge(wo_gated, g + 1)
                    v.tensor_tensor(x1[:, t, cols], x1[:, t, cols], h2[:, t, cols], ALU.add).then_inc(x1_done, 1)
            for n in range(4, 16):
                mod_add(n)
            dve.wait_ge(rows_done, 16)
            step(v.scalar_tensor_tensor(scale2, scale2, 1.0, n2_rows, ALU.add, ALU.mult))
            dve.wait_ge(ss2, NT)
            step.link(v.tensor_scalar(rstd[:], sumsq[:], 1.0 / D, NORM_EPS, ALU.mult, ALU.add))
            v.reciprocal(rstd[:], rstd[:]).then_inc(rv2, 1)
            dve.wait_ge(rstd2, 1)
            for t in range(NT):
                v.scalar_tensor_tensor(h2[:, t, :], x1[:, t, :], rstd[:, t:t + 1], scale2, ALU.mult, ALU.mult).then_inc(h2a, 1)
            for t in range(NT):
                dve.wait_ge(h2a, t + 1)
                v.tensor_tensor(h2[:, t, :], h2[:, t, :], shift2, ALU.add).then_inc(h2_done, 1)
            by_block = scores_all[:, 0:2 * PH * NT * NKEY].rearrange("p (t b n) -> p t b n", t=NT, b=2 * PH)
            for b in range(2 * PH):
                dve.wait_ge(sc_mm, b + 1)
                v.tensor_copy(by_block[:, :, b, :], ps[:, 4 + b % 4, :].rearrange("p (t n) -> p t n", t=NT)).then_inc(sc_done, 1)
            def choose(u):
                dve.wait_ge(sc_fixed, u + 1)

                def best16(srcs, cuts, rows, done):
                    n = len(srcs)

                    def inputs_at(k):
                        dve.wait_ge(best, u * CHOICE_OPS + k)

                    for i in range(n):
                        if done:
                            inputs_at(done)
                        dve.nop(nofuse=True)
                        v.max(top[:, rows + i, 0:8], srcs[i]).then_inc(best, 1)
                    for i in range(n):
                        inputs_at(done + i + 1)
                        dve.nop(nofuse=True)
                        v.max_index(top_i[:, rows + i, 0:8], top[:, rows + i, 0:8], srcs[i]).then_inc(best, 1)
                    for i in range(n):
                        v.match_replace(cuts[i], top[:, rows + i, 0:8], srcs[i], LOWEST).then_inc(best, 1)
                    for i in range(n):
                        inputs_at(done + 2 * n + i + 1)
                        dve.nop(nofuse=True)
                        v.max(top[:, rows + i, 8:16], cuts[i]).then_inc(best, 1)
                    for i in range(n):
                        inputs_at(done + 3 * n + i + 1)
                        dve.nop(nofuse=True)
                        v.max_index(top_i[:, rows + i, 8:16], top[:, rows + i, 8:16], cuts[i]).then_inc(best, 1)

                best16([sc[:, 0:NKEY], sc[:, NKEY:]], [sc_cut[:, 0:NKEY], sc_cut[:, NKEY:]], 0, 0)
                dve.wait_ge(best, u * CHOICE_OPS + 10)
                v.tensor_tensor(cand.rearrange("p (a b) -> p a b", a=TOPK), top[:, 0, :].unsqueeze(2).to_broadcast([P, TOPK, TOPK]),
                                top[:, 1, :].unsqueeze(1).to_broadcast([P, TOPK, TOPK]), ALU.add).then_inc(best, 1)
                best16([cand], [cand_cut], 2, 11)
                v.tensor_scalar(neg_top[:], top[:, 2, 0:1], -1.0, None, ALU.mult).then_inc(neg_done, 1)

            def resolve(u):
                base = lambda k: u * 7 + k
                places = top_i[:, 2, :].bitcast(I32)
                dve.wait_ge(best, u * CHOICE_OPS + CHOICE_OPS)
                v.tensor_scalar(ci_hi[:], places, 4, None, ALU.logical_shift_right).then_inc(math_s, 1)
                v.tensor_scalar(ci_lo[:], places, TOPK - 1, None, ALU.bitwise_and).then_inc(math_s, 1)
                for a, ci in enumerate((ci_hi, ci_lo)):
                    dve.wait_ge(math_s, base(a + 1))
                    v.tensor_tensor(pick[:, a], ci[:].unsqueeze(2).to_broadcast([P, TOPK, TOPK]),
                                    iota16i[:].unsqueeze(1).to_broadcast([P, TOPK, TOPK]), ALU.is_equal).then_inc(math_s, 1)
                for a in range(2):
                    dve.wait_ge(math_s, base(a + 3))
                    v.tensor_tensor(pick[:, a], pick[:, a], top_i[:, a, :].bitcast(I32).unsqueeze(1).to_broadcast([P, TOPK, TOPK]),
                                    ALU.mult).then_inc(math_s, 1)
                dve.wait_ge(math_s, base(6))
                v.tensor_reduce(e_half[:], pick, AX.X, ALU.add).then_inc(math_s, 1)
                dve.wait_ge(math_s, base(7))
                v.scalar_tensor_tensor(e_idx[:, bass.ds(u * TOPK, TOPK)], e_half[:, 0, :], float(NKEY), e_half[:, 1, :],
                                       ALU.mult, ALU.add).then_inc(e_done, 1)
                dve.wait_ge(g_exp, u + 1)
                dve.wait_ge(neg_done, u + 1)
                step_r(v.reciprocal(g_den[:], g_den[:]), u + 1)
                v.tensor_scalar(gates[:, bass.ds(u * TOPK, TOPK)], g_exp_t[:], g_den[:, 0:1], None, ALU.mult).then_inc(g_done, 1)

            def step_r(ins, n):
                ins.then_inc(g_rec, 1)
                dve.wait_ge(g_rec, n)

            with dve.Fori(0, 2) as u:
                choose(u)
                resolve(u)
            with dve.Fori(0, NT) as t:
                dve.wait_ge(h2_done, NT)
                v.tensor_copy(h2_fix, arena[:, bass.ds(t * 2 + 52, 2), :].rearrange("p u n -> p (u n)")).then_inc(h2_fixed, 1)
                with dve.Fori(0, PH) as h:
                    dve.wait_ge(h2_fixed, t + 1)
                    dve.wait_ge(g_done, t * PH + h + 1)

                    def weigh(g):
                        dve.wait_ge(gelu_done, t * (PH * 4) + h * 4 + (g + 1))
                        v.tensor_tensor(w16[:, 4 * g:4 * g + 4], gelu16[:, 4 * g:4 * g + 4],
                                        gates[:, bass.ds(t * SLOTS + h * TOPK + 4 * g, 4)], ALU.mult).then_inc(w_done, 1)

                    for g in range(4):
                        for b in range(U_SLOTS):
                            s = 4 * g + b
                            dve.wait_ge(ld_u[b], t * (PH * 64) + h * 64 + 16 * (g + 1))
                            dve.wait_ge(u_free, t * SLOTS + h * TOPK + (U_SLOTS + s - 1))
                            v.tensor_tensor_reduce(out=waste[:, s % 2, :], in0=u_ring[:, b, :], in1=h2_fix, scale=1.0, scalar=0.0,
                                                   op0=ALU.mult, op1=ALU.add, accum_out=act16[:, s:s + 1]).then_inc(u_free, 1)
                            if b == 0 and g > 0:
                                weigh(g - 1)
                        if g == 1:
                            choose(t * PH + h + 2)
                        if g == 2:
                            resolve(t * PH + h + 2)
                    weigh(3)
                dve.wait_ge(tile_mm, t + 1)
                for n in range(2):
                    cols = slice(512 * n, 512 * n + 512)
                    v.tensor_tensor(o_rows[:, cols], ps[:, n, :], gate2[:, cols], ALU.mult).then_inc(o_gated, 1)
                for n in range(2):
                    cols = slice(512 * n, 512 * n + 512)
                    dve.wait_ge(o_gated, t * 2 + (n + 1))
                    v.tensor_tensor(o_rows[:, cols], o_rows[:, cols], pair_of(n, t * 2), ALU.add).then_inc(o_sum, 1)
                dve.wait_ge(st_out, t * 16 + 16)


_INS = ["x", "c", "ada_w", "ada_b", "norm1_g", "w_in", "da_qnorm_g", "da_knorm_g", "da_lambda", "da_subln_g",
        "rw_shift_mu", "rw_w0", "rw_w2", "rw_a0", "rw_a2", "rw_g2", "rw_k_k", "rw_k_a", "rw_r_k", "rw_ln_g", "rw_ln_b",
        "w_out", "norm2_g", "peer_wq", "peer_keys", "peer_u", "peer_v"]
_FLAT = {"x", "ada_w", "w_in", "w_out", "peer_wq", "peer_u", "peer_v"}


def lay(**inputs):
    import numpy as np
    arrays = {}
    for name in _INS:
        a = np.ascontiguousarray(inputs[name])
        arrays[name] = a.reshape(a.shape[1:]) if name in _FLAT else a
    arrays["peer_keys"] = arrays["peer_keys"].reshape(2 * PH, NKEY, P)
    return arrays


def kernel(**inputs):
    import concourse.bacc as _bacc
    from concourse import mybir as _mybir
    from concourse.bass_utils import run_bass_kernel_spmd as _run

    nc = _bacc.Bacc("TRN2", target_bir_lowering=False, num_devices=1)
    laid = lay(**inputs)
    arrays, args = {}, []
    for name in _INS:
        a = laid[name]
        arrays[f"in_{name}_dram"] = a
        args.append(nc.dram_tensor(f"in_{name}_dram", a.shape, _mybir.dt.from_np(a.dtype), kind="ExternalInput").ap())
    out = nc.dram_tensor("out_0_dram", (S, D), F32, kind="ExternalOutput").ap()
    hymba_kernel(nc, *args, out)
    r = _run(nc, [arrays], core_ids=[0])
    return r.results[0]["out_0_dram"].reshape(1, S, D)
```

```python
import math
from contextlib import ExitStack

import concourse.bass as bass
from concourse import mybir

F32 = mybir.dt.float32
I32 = mybir.dt.int32
U32 = mybir.dt.uint32
ALU = mybir.AluOpType
ACT = mybir.ActivationFunctionType
AX = mybir.AxisListType

P = 128
D = 1024
S = 512
NT = S // P
KD = D // P
HD = 64
DA = 4
NB = 4
RW0 = 3 * 512
CH = 64
NC = S // CH
LEVELS = 6
PH = 8
TOPK = 16
NKEY = 128
SLOTS = PH * TOPK
U_SLOTS, V_SLOTS = 4, 8
CHOICE_OPS = 16
NORM_EPS = 1e-6
GN_EPS = 64e-5
DECAY = math.exp(-0.5)
LAMBDA0 = 0.8 - 0.6 * math.exp(0.0)
LOWEST = -3.0e38
UNIT = 512


class Tally:

    def __init__(self, eng, sem):
        self.eng, self.sem, self.n = eng, sem, 0

    def __call__(self, instruction):
        instruction.then_inc(self.sem, 1)
        self.n += 1

    def link(self, instruction):
        self(instruction)
        self.eng.wait_ge(self.sem, self.n)


STEPS = ["decay", "iclr", "alpha_t", "beta_t", "kappa_t", "gram_b", "gram_k", "mv"]
for _k in range(1, LEVELS):
    STEPS += [f"w{_k}", f"x{_k}" if _k < LEVELS - 1 else f"xt{_k}"]
STEPS += ["gh", "phi", "psi", "rho", "y"]
ACT_STEPS = ["decay", "iclr", "alpha_t", "beta_t", "kappa_t", "mv"] + [f"w{_k}" for _k in range(1, LEVELS)] + ["gh", "psi"]
DVE_STEPS = ["gram_b", "gram_k", "xt0", "x0"]
for _k in range(1, LEVELS - 1):
    DVE_STEPS += [f"x{_k}", f"xt{_k}"]
DVE_STEPS += [f"xt{LEVELS - 1}", "phi", "rho", "y"]


def upto(steps, name, i):
    return i * len(steps) + (steps.index(name) + 1)


def hymba_kernel(nc, x, c, ada_w, ada_b, norm1_g, w_in, da_qnorm_g, da_knorm_g, da_lambda, da_subln_g,
                 rw_shift_mu, rw_w0, rw_w2, rw_a0, rw_a2, rw_g2, rw_k_k, rw_k_a, rw_r_k, rw_ln_g, rw_ln_b,
                 w_out, norm2_g, peer_wq, peer_keys, peer_u, peer_v, out):
    with ExitStack() as ctx:
        def sb(name, shape, dt=F32):
            return ctx.enter_context(nc.sbuf_tensor(name, shape, dt))

        def sem(name):
            return ctx.enter_context(nc.semaphore(name))

        ident = sb("ident", [P, P])
        sel = sb("sel", [P, 8, 16])
        selT = sb("selT", [16, 8, P])
        selh = sb("selh", [P, DA, DA])
        selhT = sb("selhT", [DA, DA, P])
        ones = sb("ones", [P, P])
        half_ones = sb("half_ones", [P, P])
        qk_fold = sb("qk_fold", [16, 1])
        restart = sb("restart", [P, S])
        s_idx = sb("s_idx", [P, CH], I32)
        t_idx = sb("t_idx", [P, CH], I32)
        xor_idx = sb("xor_idx", [P, CH], I32)
        level = sb("level", [P, 2, LEVELS, CH])
        tri = sb("tri", [P, 2, 2, CH])
        eye = sb("eye", [P, CH])
        c_col = sb("c_col", [P, KD])
        silu_c = sb("silu_c", [P, KD])
        ada_bc = sb("ada_bc", [P, 16])
        ada_bc2 = sb("ada_bc2", [P, 32])
        n2_col = sb("n2_col", [P, KD])
        mod2 = sb("mod2", [P, 32])
        n1_col = sb("n1_col", [P, KD])
        mod1 = sb("mod1", [P, 16])
        qk_gain = sb("qk_gain", [P, 2])
        mu = sb("mu", [P, 2, 15])
        mu_self = sb("mu_self", [P, 15])
        sub_g = sb("sub_g", [P, 1])
        lam = sb("lam", [P, 4 * HD])
        lam_p = sb("lam_p", [P, 2 * HD])
        lam_e = sb("lam_e", [P, 2])
        neg_lam = sb("neg_lam", [P, 1])
        w0_col = sb("w0_col", [P, 2, NB])
        a0_col = sb("a0_col", [P, 2, NB])
        kk_col = sb("kk_col", [P, NB])
        ka_col = sb("ka_col", [P, NB])
        ka1_col = sb("ka1_col", [P, NB])
        rk_col = sb("rk_col", [P, NB])
        lg_col = sb("lg_col", [P, NB])
        lb_col = sb("lb_col", [P, NB])
        w2_sb = sb("w2_sb", [P, 512])
        a2_sb = sb("a2_sb", [P, 512])
        g2_sb = sb("g2_sb", [P, 512])
        w2_pair = sb("w2_pair", [P, P])
        a2_pair = sb("a2_pair", [P, P])
        sumsq = sb("sumsq", [P, NT])
        rstd = sb("rstd", [P, NT])
        stat = sb("stat", [16, S])
        mx = sb("mx", [P, 2, 2])
        nmx = sb("nmx", [P, 2, 2])
        den = sb("den", [P, 2, 2])
        rden = sb("rden", [P, 2, 2])
        ptot = sb("ptot", [P, 2, NC])

        top = sb("top", [P, 3, TOPK])
        top_i = sb("top_i", [P, 3, TOPK], U32)
        neg_top = sb("neg_top", [P, 1])
        ci_lo = sb("ci_lo", [P, TOPK], I32)
        ci_hi = sb("ci_hi", [P, TOPK], I32)
        e_half = sb("e_half", [P, 2, TOPK])
        g_exp_t = sb("g_exp_t", [P, TOPK])
        g_den = sb("g_den", [P, 1])
        iota16i = sb("iota16i", [P, TOPK], I32)
        idx_col = sb("idx_col", [P, TOPK], I32)
        act16 = sb("act16", [P, TOPK])
        gelu16 = sb("gelu16", [P, TOPK])
        w16 = sb("w16", [P, TOPK])
        zero_w = sb("zero_w", [P, P])

        NU = 87
        arena = sb("arena", [P, NU, UNIT])

        def units(u, n):
            return arena[:, u:u + n, :]

        rT, kT, vT, kkT = units(0, 4), units(4, 4), units(8, 4), units(12, 4)
        attT = units(16, 4)
        loT = units(20, 3)
        qkT = units(23, 8)
        vA = units(31, 4)
        hT = units(35, 8)
        ring = units(43, 16)
        xs = units(59, 8)
        xr = units(67, 8)
        sq = units(75, 2)
        sq_o = units(67, DA)
        stat_kk, stat_o = arena[0:8, 84, :], arena[0:DA, 85, :]
        bias = units(77, 7)
        bias_h = bias.rearrange("p u n -> p (u n)").rearrange("p (h n) -> p h n", h=DA)
        probs = units(59, 4)
        mix = units(63, 2)
        mixT = units(65, 2)
        PHI, PSI, RP, YT = units(23, 8), units(31, 8), units(39, 8), units(47, 4)
        vt_u = units(51, 1)
        dir_u = [52, 69]
        ps = ctx.enter_context(nc.psum_tensor("ps", [P, 8, 512], F32))

        def chunks(ap):
            return ap.rearrange("p u n -> p (u n)").rearrange("p (c n) -> p c n", c=NC)

        class Dir:

            def __init__(self, u):
                self.bk = units(u, 2)
                self.beta, self.kappa = arena[:, u, :], arena[:, u + 1, :]
                self.gh = chunks(units(u, 2))
                self.hat_b, self.hat_k = arena[:, u + 2, :], arena[:, u + 3, :]
                self.la = chunks(units(u + 2, 2))
                self.ar = units(u + 4, 2)
                self.alpha, self.rho = arena[:, u + 4, :], arena[:, u + 5, :]
                self.rhs = chunks(units(u + 6, 2))
                self.beta_t, self.kappa_t = chunks(units(u + 8, 1)), chunks(units(u + 9, 1))
                self.mb = chunks(units(u + 10, 2))
                t = u + 12
                self.dg = chunks(units(t, 1))
                self.sg, self.a, self.cum = arena[:, t, :], arena[:, t + 1, :], arena[:, t + 2, :]
                self.pinc, self.pinv, self.pexc = arena[:, t + 3, :], arena[:, t + 4, :], self.sgx(t)
                self.c = [chunks(units(t, 1)), chunks(units(t + 1, 1))]
                self.x, self.xt, self.w = chunks(units(t + 2, 1)), chunks(units(t + 3, 1)), chunks(units(t + 4, 1))

            def sgx(self, t):
                return arena[:, t, :]

        dirs = [Dir(u) for u in dir_u]
        x1 = units(0, 8).rearrange("p u n -> p (u n)").rearrange("p (t d) -> p t d", t=NT)
        mod_rows = units(8, 8).rearrange("p u n -> p (u n)").rearrange("p (m d) -> p m d", m=4)
        gate1, shift2, scale2, gate2 = (mod_rows[:, m, :] for m in range(4))
        col_diag = units(31, 8)
        ring2 = units(23, 16)
        h2T = units(39, 8)
        h2 = units(52, 8).rearrange("p u n -> p (u n)").rearrange("p (t d) -> p t d", t=NT)
        wo = units(69, 16).rearrange("p u n -> p (u n)").rearrange("p (k n) -> p k n", k=KD)
        keys_raw = units(60, 4).rearrange("p u n -> p (u n)").rearrange("p (b n) -> p b n", b=16)
        keysT = units(64, 4).rearrange("p u n -> p (u n)").rearrange("p (b n) -> p b n", b=16)
        qT = units(47, 4)
        scores_all = units(69, 17).rearrange("p u n -> p (u n)")
        gates = units(16, 2).rearrange("p u n -> p (u n)")
        e_idx = units(18, 2).rearrange("p u n -> p (u n)").bitcast(I32)
        sc, sc_cut = arena[:, 20, 0:256], arena[:, 20, 256:512]
        cand, cand_cut = arena[:, 21, 0:256], arena[:, 21, 256:512]
        pick = arena[:, 22, :].rearrange("p (a r m) -> p a r m", a=2, r=TOPK)
        v_ring = units(23, 16).rearrange("p u n -> p (u n)").rearrange("p (s d) -> p s d", s=V_SLOTS)
        u_ring = units(39, 8).rearrange("p u n -> p (u n)").rearrange("p (s d) -> p s d", s=U_SLOTS)
        o_rows = units(47, 2).rearrange("p u n -> p (u n)")
        diag = units(49, 2).rearrange("p u n -> p (u n)").rearrange("p (s m) -> p s m", s=V_SLOTS)
        h2_fix = units(8, 2).rearrange("p u n -> p (u n)")
        waste = units(10, 4).rearrange("p u n -> p (u n)").rearrange("p (s d) -> p s d", s=2)
        v_t = chunks(vt_u)
        v_fix = arena[:, 86, :]
        states = units(52, NC)
        tmp = units(60, 4)
        tmp2 = units(64, 4)
        stat_y = arena[0:8, 68, :]

        def pair_of(u, i, n=1):
            return arena[:, bass.ds(i + u, 1), :].rearrange("p a n -> p (a n)")

        def feature_banks(b):
            return ps[:, b:b + 2, 0:NC // 2 * CH].rearrange("p o (c n) -> p o c n", c=NC // 2)

        def odd_even(ap):
            return ap.rearrange("p (c o n) -> p o c n", c=NC // 2, o=2)

        def flat(ap):
            return ap.rearrange("p c n -> p (c n)")

        def by_chunk(ap):
            return ap.rearrange("p (c n) -> p c n", c=NC)

        ld_c = sem("ld_c"); ld_par = sem("ld_par"); ld_mu = sem("ld_mu"); ld_rw = sem("ld_rw"); ld_lam = sem("ld_lam")
        ld_x = [sem(f"ld_x{t}") for t in range(NT)]
        ld_w = [sem(f"ld_w{i}") for i in range(4)]
        w_used = sem("w_used")
        zeroed = sem("zeroed"); consts = sem("consts"); sel_done = sem("sel_done"); masks = sem("masks")
        silu_done = sem("silu_done"); mod1_done = sem("mod1_done"); mu_done = sem("mu_done")
        ss_done = sem("ss_done"); rv_done = sem("rv_done"); rstd_done = sem("rstd_done")
        xs_done = sem("xs_done"); xT_mm = sem("xT_mm"); hT_done = sem("hT_done")
        proj_mm = sem("proj_mm"); proj_a = sem("proj_a"); proj_v = sem("proj_v")
        qk_sqr = sem("qk_sqr"); qk_stat = sem("qk_stat")
        v_mm = sem("v_mm"); v_done = sem("v_done")
        qk_var = sem("qk_var"); qk_rstd = sem("qk_rstd"); qk_bc = sem("qk_bc"); qk_done = sem("qk_done")
        lo_done = sem("lo_done")
        kk_raw = sem("kk_raw"); kk_sqr = sem("kk_sqr"); kk_stat = sem("kk_stat")
        kk_norm = sem("kk_norm"); kk_inv = sem("kk_inv"); kk_bc = sem("kk_bc"); kk_done = sem("kk_done")
        bias_done = sem("bias_done"); lam_sum = sem("lam_sum"); lam_exp = sem("lam_exp")
        s_mm = sem("s_mm"); s_max = sem("s_max"); s_exp = sem("s_exp"); mixed = sem("mixed")
        mixT_mm = sem("mixT_mm"); mixT_done = sem("mixT_done"); o_mm = sem("o_mm"); o_copy = sem("o_copy"); o_sqr = sem("o_sqr")
        o_stat = sem("o_stat"); o_var = sem("o_var"); o_rstd = sem("o_rstd"); o_bc = sem("o_bc"); o_done = sem("o_done")
        dve_s = sem("dve_s"); 
        ld_wo = sem("ld_wo"); ld_keys = sem("ld_keys")
        spread = sem("spread"); rows_mm = sem("rows_mm"); rows_done = sem("rows_done"); 
        wo_mm = sem("wo_mm"); wo_gated = sem("wo_gated"); x1_done = sem("x1_done")
        ss2 = sem("ss2"); rv2 = sem("rv2"); rstd2 = sem("rstd2"); h2a = sem("h2a"); h2_done = sem("h2_done")
        h2T_mm = sem("h2T_mm"); h2T_done = sem("h2T_done"); keysT_mm = sem("keysT_mm"); keysT_done = sem("keysT_done")
        q_mm = sem("q_mm"); q_done = sem("q_done"); sc_mm = sem("sc_mm"); sc_done = sem("sc_done")
        sc_fixed = sem("sc_fixed"); best = sem("best"); neg_done = sem("neg_done"); g_exp = sem("g_exp"); math_s = sem("math_s")
        e_done = sem("e_done"); g_done = sem("g_done"); g_rec = sem("g_rec"); col_done = sem("col_done")
        ld_u = [sem(f"ld_u{n}") for n in range(U_SLOTS)]; ld_v = [sem(f"ld_v{n}") for n in range(V_SLOTS)]
        u_free = sem("u_free"); v_free = sem("v_free")
        h2_fixed = sem("h2_fixed"); gelu_done = sem("gelu_done"); w_done = sem("w_done"); diags = sem("diags")
        tile_mm = sem("tile_mm"); o_gated = sem("o_gated"); o_sum = sem("o_sum"); st_out = sem("st_out")
        masks_done = sem("masks_done"); v_fixed = sem("v_fixed"); vt_mm = sem("vt_mm"); vt_done = sem("vt_done")
        pair_w = sem("pair_w")
        mm = [sem(f"step_mm{d}") for d in range(2)]
        by_act = [sem(f"step_act{d}") for d in range(2)]
        by_dve = [sem(f"step_dve{d}") for d in range(2)]
        cum_done = sem("cum_done")
        exps = sem("exps")
        feat_v = sem("feat_v")
        feat_p = sem("feat_p")
        c_done = [sem(f"c_done{d}") for d in range(2)]
        kap = sem("kap")
        
        state_mm = sem("state_mm"); state_done = sem("state_done"); yst_mm = sem("yst_mm"); y_sum = sem("y_sum")
        mean_mm = sem("mean_mm"); centred = sem("centred"); y_sqr = sem("y_sqr"); y_stat = sem("y_stat"); y_var = sem("y_var")
        y_rstd = sem("y_rstd"); y_bc = sem("y_bc"); rk_done = sem("rk_done"); bon_mm = sem("bon_mm")
        bon_done = sem("bon_done"); gate_mm = sem("gate_mm"); rw_out = sem("rw_out")

        strips = [(ada_w, i * 256, 256) for i in range(8)]
        strips += [(w_in, RW0 + i * 256, 256 if i < 7 else 128) for i in range(8)]
        strips += [(w_in, 1024 + i * 256, 256) for i in range(2)]
        strips += [(w_in, i * 256, 256) for i in range(4)]
        strips += [(ada_w, 2048 + i * 256, 256) for i in range(16)]
        rw_blocks = [(8 + b // 2, P * (b % 2)) for b in range(15)]
        qk_blocks = [(18 + b // 2, P * (b % 2)) for b in range(8)]

        def strip(n):
            w = strips[n][2]
            flat = ring[:, 4 * (n % 4):4 * (n % 4) + 4, :].rearrange("p u n -> p (u n)")
            return flat[:, 0:KD * w].rearrange("p (k n) -> p k n", k=KD)

        def strip_read(eng, n):
            if n < 8:
                eng.wait_ge(w_used, n + 1)
            elif n < 16:
                eng.wait_ge(proj_mm, min(2 * (n - 8) + 2, 15))
            elif n < 18:
                eng.wait_ge(v_mm, NT)
            elif n < 22:
                eng.wait_ge(proj_mm, 15 + 2 * (n - 18) + 2)
            else:
                eng.wait_ge(w_used, 8 + n - 22 + 1)

        def rw_dest(b):
            return arena[:, b, :] if b < 12 else loT[:, b - 12, :]

        def strip2(n):
            return ring2[:, 4 * (n % 4):4 * (n % 4) + 4, :].rearrange("p u n -> p (u n)").rearrange("p (k n) -> p k n", k=KD)

        def ring2_loaded(n):
            first = len(strips[n % 4::4])
            return 16 * (first + n // 4 + 1)

        def cat(k):
            return attT[:, k, :] if k < 4 else YT[:, k - 4, :]

        UN = DA * NT
        x_rows = xr.rearrange("p u n -> p (u n)").rearrange("p (t d) -> p t d", t=NT)
        xs_rows = xs.rearrange("p u n -> p (u n)").rearrange("p (t d) -> p t d", t=NT)

        def bank_of(d, name):
            return 4 * d + 2 * (STEPS.index(name) % 2)

        CONSTS = 11
        RW_LOADS = 14 * 16

        block = ctx.enter_context(nc.Block())

        @block.sync
        def _(sp):
            sp.dma_start(c_col[:], c.rearrange("o (k p) -> p (o k)", p=P), allow_slow_non_contiguous=True).then_inc(ld_c, 16)

            def load_strip(n):
                src, c0, w = strips[n]
                if n >= 4:
                    strip_read(sp, n - 4)
                sp.dma_start(strip(n), src[:, c0:c0 + w].rearrange("(k p) n -> p k n", p=P)).then_inc(ld_w[n % 4], 16)

            for n in range(4):
                load_strip(n)
                sp.dma_start(x_rows[:, n, :], x[n * P:(n + 1) * P, :]).then_inc(ld_x[n], 16)
            for n in range(4, len(strips)):
                load_strip(n)
            for d in range(2):
                sp.wait_ge(mm[d], NB * len(STEPS))
                sp.wait_ge(by_dve[d], NB * len(DVE_STEPS))
                sp.wait_ge(by_act[d], NB * len(ACT_STEPS))
                sp.wait_ge(c_done[d], NB * 7)
            sp.dma_start(wo, w_out.rearrange("(k p) n -> p k n", p=P)).then_inc(ld_wo, 16)

            def load_ring2(n):
                if n >= 4:
                    sp.wait_ge(q_mm, 2 * (n - 4) + 2)
                sp.dma_start(strip2(n), peer_wq[:, 256 * n:256 * (n + 1)].rearrange("(k p) n -> p k n", p=P)).then_inc(ld_w[n % 4], 16)

            sp.wait_ge(rk_done, NB)
            for t in range(NT):
                sp.dma_start(x1[:, t, :], x[t * P:(t + 1) * P, :]).then_inc(ld_x[t], 16)
            sp.wait_ge(state_mm, NC - 2)
            for n in range(2):
                load_ring2(n)
            sp.wait_ge(rw_out, NB)
            sp.dma_start(keys_raw, peer_keys.rearrange("b n d -> n b d")).then_inc(ld_keys, 16)
            sp.wait_ge(rows_mm, 8)
            for n in range(2, 8):
                load_ring2(n)
            for t in range(NT):
                sp.wait_ge(o_sum, 2 * t + 2)
                sp.dma_start(out[t * P:(t + 1) * P, :], o_rows).then_inc(st_out, 16)
            sp.wait_ge(st_out, 16 * NT)

        @block.gpsimd
        def _(pool):
            slow = dict(allow_slow_non_contiguous=True)
            pool.dma_start(ada_bc[:], ada_b[0, 0:2048].rearrange("(j p) -> p j", p=P), **slow).then_inc(ld_par, 16)
            pool.dma_start(n1_col[:], norm1_g.rearrange("o (j p) -> p (o j)", p=P), **slow).then_inc(ld_par, 16)
            for d in range(2):
                pool.dma_start(mu[:, d, :], rw_shift_mu[0, d, :].rearrange("(j p) -> p j", p=P), **slow).then_inc(ld_mu, 16)
            for i, g in enumerate((da_qnorm_g, da_knorm_g)):
                for h in range(2):
                    pool.dma_start(qk_gain[HD * h:HD * h + HD, i:i + 1], g.rearrange("o d -> d o"), **slow).then_inc(ld_mu, 16)
            pool.memset(ident[:], 0.0).then_inc(zeroed, 1)
            pool.memset(sel[:], 0.0).then_inc(zeroed, 1)
            pool.memset(selT[:], 0.0).then_inc(zeroed, 1)
            pool.memset(half_ones[:], 0.0).then_inc(zeroed, 1)
            pool.memset(selh[:], 0.0).then_inc(zeroed, 1)
            pool.memset(selhT[:], 0.0).then_inc(zeroed, 1)
            pool.memset(qk_fold[:], 1.0).then_inc(zeroed, 1)
            pool.memset(restart[:], 1.0).then_inc(zeroed, 1)
            pool.memset(zero_w[:], 0.0).then_inc(zeroed, 1)
            pool.wait_ge(zeroed, 9)
            pool.affine_select(out=ident[:], in_=ident[:], compare_op=ALU.not_equal, fill=1.0, base=0,
                               pattern=[[-1, P]], channel_multiplier=1).then_inc(consts, 1)
            split = selT[:].rearrange("m b (h p) -> m b h p", h=2)
            pool.affine_select(out=split, in_=split, compare_op=ALU.not_equal, fill=1.0, base=0,
                               pattern=[[-2, 8], [-1, 2], [0, 64]], channel_multiplier=1).then_inc(consts, 1)
            pool.affine_select(out=selhT[:], in_=selhT[:], compare_op=ALU.not_equal, fill=1.0, base=0,
                               pattern=[[-1, DA], [0, P]], channel_multiplier=1).then_inc(consts, 1)
            pool.memset(ones[:], 1.0).then_inc(consts, 1)
            pool.memset(selh[:].rearrange("p h m -> p (h m)")[:, 0:DA * DA:DA + 1], 1.0).then_inc(consts, 1)
            pool.memset(qk_fold[0:8, :], 1.0 / HD).then_inc(consts, 1)
            pool.memset(restart[:, 0:S:CH], 0.0).then_inc(consts, 1)
            pool.iota(s_idx[:], [[0, CH]], base=0, channel_multiplier=1).then_inc(consts, 1)
            pool.iota(t_idx[:], [[1, CH]], base=0, channel_multiplier=0).then_inc(consts, 1)
            pool.iota(iota16i[:], [[1, TOPK]], base=0, channel_multiplier=0).then_inc(consts, 1)
            pool.iota(bias_h[:, 0, :], [[-1, 896]], base=384, channel_multiplier=1,
                      allow_small_or_imprecise_dtypes=True).then_inc(consts, 1)
            pool.dma_start(lam[:], da_lambda.rearrange("o a d -> o (a d)").to_broadcast([P, 4 * HD]), **slow).then_inc(ld_lam, 16)
            pool.dma_start(sub_g[:], da_subln_g.rearrange("o d -> d o"), **slow).then_inc(ld_lam, 16)
            for d in range(2):
                pool.dma_start(w0_col[:, d, :], rw_w0[0, d, :].rearrange("(j p) -> p j", p=P), **slow).then_inc(ld_rw, 16)
                pool.dma_start(a0_col[:, d, :], rw_a0[0, d, :].rearrange("(j p) -> p j", p=P), **slow).then_inc(ld_rw, 16)
            for col, src in ((kk_col, rw_k_k), (ka_col, rw_k_a), (lg_col, rw_ln_g), (lb_col, rw_ln_b),
                             (rk_col, rw_r_k.rearrange("o h d -> o (h d)"))):
                pool.dma_start(col[:], src.rearrange("o (j p) -> p (o j)", p=P), **slow).then_inc(ld_rw, 16)
            pool.dma_start(ada_bc2[:], ada_b[0, 2048:6144].rearrange("(j p) -> p j", p=P), **slow).then_inc(ld_rw, 16)
            pool.dma_start(n2_col[:], norm2_g.rearrange("o (j p) -> p (o j)", p=P), **slow).then_inc(ld_rw, 16)
            pool.dma_start(w2_sb[:], rw_w2.rearrange("o d r n -> (o d r) n")).then_inc(ld_rw, 16)
            pool.dma_start(a2_sb[:], rw_a2.rearrange("o d r n -> (o d r) n")).then_inc(ld_rw, 16)
            pool.dma_start(g2_sb[:], rw_g2.rearrange("o r n -> (o r) n")).then_inc(ld_rw, 16)


            pool.wait_ge(ld_rw, RW_LOADS)
            pool.wait_ge(masks_done, 1)
            pool.wait_ge(o_done, DA)
            with pool.Fori(0, NB) as i:
                for fixed, src in ((w2_pair, w2_sb), (a2_pair, a2_sb)):
                    pool.tensor_copy(fixed[:], src[:, bass.ds(i * P, P)]).then_inc(pair_w, 1)
                for d, r in enumerate(dirs):
                    pool.wait_ge(cum_done, 2 * i + d + 1)
                    pool.tensor_tensor(r.pexc, r.cum, r.sg, ALU.subtract).then_inc(feat_p, 1)
                    pool.wait_ge(by_act[d], upto(ACT_STEPS, "iclr", i))
                    pool.nop(nofuse=True)
                    pool.tensor_tensor(r.beta, pair_of(12, i), r.a, ALU.mult).then_inc(feat_p, 1)
                    pool.wait_ge(exps, 6 * i + 3 * d + 2)
                    pool.wait_ge(feat_p, 8 * i + 4 * d + 2)
                    pool.tensor_tensor(r.beta, r.beta, r.pinv, ALU.mult).then_inc(feat_p, 1)
                    pool.wait_ge(feat_v, 10 * i + 5 * d + 1)
                    pool.wait_ge(feat_p, 8 * i + 4 * d + 3)
                    pool.tensor_tensor(by_chunk(r.hat_b), by_chunk(r.beta), ptot[:, d, :].unsqueeze(2).to_broadcast([P, NC, CH]),
                                       ALU.mult).then_inc(feat_p, 1)
                for k in range(LEVELS):
                    for d, r in enumerate(dirs):
                        pool.wait_ge(by_dve[d], upto(DVE_STEPS, "gram_b", i) if k < 2 else upto(DVE_STEPS, "xt0", i))
                        if k >= 3:
                            pool.wait_ge(mm[d], upto(STEPS, f"w{k - 2}", i))
                        pool.tensor_tensor(r.c[k % 2], r.la[:, :, 0:CH],
                                           level[:, d, k, :].unsqueeze(1).to_broadcast([P, NC, CH]), ALU.mult).then_inc(c_done[d], 1)
                for d, r in enumerate(dirs):
                    pool.wait_ge(mm[d], upto(STEPS, "w4", i))
                    pool.tensor_tensor(r.dg, eye[:].unsqueeze(1).to_broadcast([P, NC, CH]),
                                       ptot[:, d, :].unsqueeze(2).to_broadcast([P, NC, CH]), ALU.mult).then_inc(c_done[d], 1)
                for d in range(2):
                    pool.wait_ge(mm[d], (i + 1) * len(STEPS))
                    pool.wait_ge(by_dve[d], (i + 1) * len(DVE_STEPS))
                    pool.wait_ge(by_act[d], (i + 1) * len(ACT_STEPS))


            pool.wait_ge(e_done, 1)
            pool.wait_ge(h2_fixed, 1)
            pool.memset(w16[:], 0.0).then_inc(v_free, V_SLOTS)
            pool.memset(act16[:], 0.0).then_inc(u_free, U_SLOTS)
            pool.tensor_copy(idx_col[:, 0:1], e_idx[:, 0:1]).then_inc(col_done, 1)
            with pool.Fori(0, PH * NT) as u:
                for s in range(TOPK):
                    pool.wait_ge(col_done, u * TOPK + (s + 1))
                    pool.wait_ge(u_free, u * TOPK + (s + 1))
                    pool.wait_ge(v_free, u * TOPK + (s + 1))
                    if s == TOPK - 1:
                        pool.wait_ge(e_done, u + 2)
                    nxt = (s + 1) % TOPK
                    pool.tensor_copy(idx_col[:, nxt:nxt + 1], e_idx[:, bass.ds(u * TOPK + (s + 1), 1)]).then_inc(col_done, 1)
                    pool.indirect_dma_start(u_ring[:, s % U_SLOTS, :], None, peer_u,
                                            bass.IndirectOffsetOnAxis(idx_col[:, s:s + 1], 0)).then_inc(ld_u[s % U_SLOTS], 16)
                    pool.indirect_dma_start(v_ring[:, s % V_SLOTS, :], None, peer_v,
                                            bass.IndirectOffsetOnAxis(idx_col[:, s:s + 1], 0)).then_inc(ld_v[s % V_SLOTS], 16)

        @block.scalar
        def _(act):
            act.wait_ge(ld_c, 16)
            nc.scalar.activation(silu_c[:], c_col[:], ACT.Silu).then_inc(silu_done, 1)
            for t in range(NT):
                act.wait_ge(ld_x[t], 16)
                nc.scalar.activation(xs_rows[:, t, :], x_rows[:, t, :], ACT.Square, accum_out=sumsq[:, t:t + 1]).then_inc(ss_done, 1)
            act.wait_ge(rv_done, 1)
            nc.scalar.activation(rstd[:], rstd[:], ACT.Sqrt).then_inc(rstd_done, 1)
            act.wait_ge(mod1_done, 1)
            for j in range(KD):
                act.wait_ge(xT_mm, j + 1)
                nc.scalar.activation(hT[:, j, :], ps[:, j % 4, :], ACT.Identity, bias=mod1[:, j:j + 1],
                                     scale=mod1[:, 8 + j:9 + j]).then_inc(hT_done, 1)
            act.wait_ge(mu_done, 1)
            for b in range(15):
                act.wait_ge(proj_mm, b + 1)
                nc.scalar.activation(rw_dest(b), ps[:, b % 4, :], ACT.Copy, scale=mu_self[:, b:b + 1]).then_inc(proj_a, 1)
            for t in range(NT):
                act.wait_ge(v_mm, t + 1)
                nc.scalar.activation(vA[:, t, :], ps[:, 4 + t, :], ACT.Copy).then_inc(v_done, 1)
            for b in range(8):
                act.wait_ge(proj_mm, 16 + b)
                if b >= 2:
                    act.wait_ge(qk_stat, b - 1)
                nc.scalar.activation(sq[:, b % 2, :], ps[:, (15 + b) % 4, :], ACT.Square).then_inc(qk_sqr, 1)
            for b in range(NB):
                act.wait_ge(kk_raw, b + 1)
                if b < 2:
                    act.wait_ge(qk_stat, 7 + b)
                else:
                    act.wait_ge(kk_stat, b - 1)
                nc.scalar.activation(sq[:, b % 2, :], kkT[:, b, :], ACT.Square).then_inc(kk_sqr, 1)
            act.wait_ge(qk_var, 1)
            nc.scalar.activation(stat[0:16, :], stat[0:16, :], ACT.Sqrt, scale=qk_fold[:, 0:1]).then_inc(qk_rstd, 1)
            act.wait_ge(kk_stat, NB)
            nc.scalar.activation(stat_kk, ps[0:8, 5, :], ACT.Sqrt).then_inc(kk_norm, 1)
            act.wait_ge(proj_v, 15)
            nc.scalar.activation(loT[:, 0, :], loT[:, 0, :], ACT.Tanh).then_inc(lo_done, 1)
            nc.scalar.activation(loT[:, 2, :], loT[:, 2, :], ACT.Sigmoid).then_inc(lo_done, 1)
            act.wait_ge(lam_sum, 1)
            nc.scalar.activation(lam_e[:], lam_e[:], ACT.Exp).then_inc(lam_exp, 1)

            def evacuate(u):
                act.wait_ge(mixT_mm, u + 1)
                if u >= 2:
                    act.wait_ge(o_mm, u - 1)
                nc.scalar.activation(mixT[:, u % 2, :], ps[:, 4 + u % 2, :], ACT.Copy).then_inc(mixT_done, 1)

            def head_out(h):
                act.wait_ge(o_mm, NT * (h + 1))
                bank = ps[:, 6, :]
                nc.scalar.activation(sq_o[:, h, :], bank, ACT.Square).then_inc(o_sqr, 1)
                nc.scalar.activation(attT[:, h, :], bank, ACT.Copy, scale=sub_g[:, 0:1]).then_inc(o_copy, 1)

            act.wait_ge(ld_lam, 32)
            for u in range(UN):
                act.wait_ge(s_max, u + 1)
                for cmp in range(2):
                    pr = probs[:, 2 * (u % 2) + cmp, :]
                    nc.scalar.activation(pr, pr, ACT.Exp, bias=nmx[:, u % 2, cmp:cmp + 1],
                                         accum_out=den[:, u % 2, cmp:cmp + 1]).then_inc(s_exp, 1)
                if u >= 1:
                    evacuate(u - 1)
                if u % NT == 0 and u >= NT:
                    head_out(u // NT - 1)
            evacuate(UN - 1)
            head_out(DA - 1)
            act.wait_ge(o_var, 1)
            nc.scalar.activation(stat_o, stat_o, ACT.Sqrt, scale=(1.0 - LAMBDA0) ** 2).then_inc(o_rstd, 1)


            act.wait_ge(ld_rw, RW_LOADS)
            act.wait_ge(o_done, DA)
            with act.Fori(0, NB) as i:
                nc.scalar.activation(v_fix, pair_of(8, i), ACT.Copy).then_inc(v_fixed, 1)
                for d, r in enumerate(dirs):
                    act.wait_ge(mm[d], upto(STEPS, "decay", i))
                    nc.scalar.activation(r.sg, ps[:, 4 * d, :], ACT.Sigmoid, bias=w0_col[:, d, bass.ds(i, 1)]).then_inc(by_act[d], 1)
                    act.wait_ge(mm[d], upto(STEPS, "iclr", i))
                    nc.scalar.activation(r.a, ps[:, 4 * d + 2, :], ACT.Sigmoid, bias=a0_col[:, d, bass.ds(i, 1)]).then_inc(by_act[d], 1)
                act.wait_ge(vt_mm, i + 1)
                nc.scalar.activation(vt_u[:, 0, :], ps[:, 7, :], ACT.Copy).then_inc(vt_done, 1)
                for d, r in enumerate(dirs):
                    act.wait_ge(cum_done, 2 * i + d + 1)
                    nc.scalar.activation(r.pinc, r.cum, ACT.Exp, scale=-DECAY).then_inc(exps, 1)
                    nc.scalar.activation(r.pinv, r.cum, ACT.Exp, scale=DECAY).then_inc(exps, 1)
                    act.wait_ge(feat_p, 8 * i + 4 * d + 1)
                    nc.scalar.activation(r.pexc, r.pexc, ACT.Exp, scale=-DECAY).then_inc(exps, 1)

                def take(name, dst, scale=1.0, width=1):
                    for d, r in enumerate(dirs):
                        b = bank_of(d, name)
                        act.wait_ge(mm[d], upto(STEPS, name, i))
                        src = ps[:, b:b + width, :].rearrange("p b n -> p (b n)").rearrange("p (c n) -> p c n", c=NC)
                        nc.scalar.activation(dst(d, r), src, ACT.Copy, scale=scale).then_inc(by_act[d], 1)

                take("alpha_t", lambda d, r: r.rhs[:, :, 0:CH])
                take("beta_t", lambda d, r: r.beta_t)
                take("kappa_t", lambda d, r: r.kappa_t)
                take("mv", lambda d, r: r.rhs[:, :, CH:2 * CH])
                for k in range(1, LEVELS):
                    take(f"w{k}", lambda d, r: r.w)
                take("gh", lambda d, r: r.gh, scale=-1.0, width=2)
                for d, r in enumerate(dirs):
                    act.wait_ge(mm[d], upto(STEPS, "psi", i))
                    nc.scalar.activation(odd_even(pair_of(31 + d, i * 2)), feature_banks(bank_of(d, "psi")), ACT.Copy).then_inc(by_act[d], 1)
                for d in range(2):
                    act.wait_ge(mm[d], (i + 1) * len(STEPS))
                    act.wait_ge(by_dve[d], (i + 1) * len(DVE_STEPS))
            for b in range(NB):
                act.wait_ge(centred, b + 1)
                nc.scalar.activation(tmp2[:, b, :], YT[:, b, :], ACT.Square).then_inc(y_sqr, 1)
            act.wait_ge(y_var, 1)
            nc.scalar.activation(stat_y, stat_y, ACT.Sqrt).then_inc(y_rstd, 1)

            act.wait_ge(bon_done, NB)
            for g in range(8):
                act.wait_ge(rows_mm, g + 1)
                nc.scalar.activation(mod_rows.rearrange("p m d -> p (m d)")[:, 512 * g:512 * g + 512], ps[:, g % 2, :], ACT.Copy).then_inc(rows_done, 1)
            for g in range(4):
                act.wait_ge(keysT_mm, g + 1)
                nc.scalar.activation(keysT[:, 4 * g:4 * g + 4, :].rearrange("p b n -> p (b n)"), ps[:, 6 + g % 2, :], ACT.Copy).then_inc(keysT_done, 1)
            for t in range(NT):
                act.wait_ge(x1_done, 2 * t + 2)
                nc.scalar.activation(h2[:, t, :], x1[:, t, :], ACT.Square, accum_out=sumsq[:, t:t + 1]).then_inc(ss2, 1)
            act.wait_ge(rv2, 1)
            nc.scalar.activation(rstd[:], rstd[:], ACT.Sqrt).then_inc(rstd2, 1)
            for j in range(KD):
                act.wait_ge(h2T_mm, j + 1)
                nc.scalar.activation(h2T[:, j, :], ps[:, 6 + j % 2, :], ACT.Copy).then_inc(h2T_done, 1)
            for b in range(2 * PH):
                act.wait_ge(q_mm, b + 1)
                if b >= 4:
                    act.wait_ge(sc_mm, b - 3)
                nc.scalar.activation(qT[:, b % 4, :], ps[:, b % 4, :], ACT.Copy).then_inc(q_done, 1)

            def fix_scores(u):
                nc.scalar.activation(sc, scores_all[:, bass.ds(u * (2 * NKEY), 2 * NKEY)], ACT.Copy).then_inc(sc_fixed, 1)

            def gate_exp(u):
                act.wait_ge(neg_done, u + 1)
                nc.scalar.activation(g_exp_t[:], top[:, 2, :], ACT.Exp, bias=neg_top[:, 0:1], accum_out=g_den[:]).then_inc(g_exp, 1)

            act.wait_ge(sc_done, 2 * PH)
            with act.Fori(0, 2) as u:
                fix_scores(u)
                gate_exp(u)
            with act.Fori(0, PH * NT) as u:
                fix_scores(u + 2)
                for g in range(4):
                    act.wait_ge(u_free, u * TOPK + (U_SLOTS + 4 * g + 4))
                    nc.scalar.activation(gelu16[:, 4 * g:4 * g + 4], act16[:, 4 * g:4 * g + 4], ACT.Gelu).then_inc(gelu_done, 1)
                    if g == 1:
                        gate_exp(u + 2)
                    act.wait_ge(w_done, u * 4 + (g + 1))
                    for s in range(4 * g, 4 * g + 4):
                        act.wait_ge(v_free, u * TOPK + (s + 1))
                        nc.scalar.activation(diag[:, s % V_SLOTS, :], ident[:], ACT.Copy, scale=w16[:, s:s + 1]).then_inc(diags, 1)

        @block.tensor
        def _(pe):
            pe.wait_ge(silu_done, 1)
            for n in range(8):
                pe.wait_ge(ld_w[n % 4], 16 * (n // 4 + 1))
                w = strip(n)
                for h in range(2):
                    for k in range(KD):
                        last = nc.tensor.matmul(ps[:, 7, 2 * n + h:2 * n + h + 1], w[:, k, h * P:(h + 1) * P],
                                                silu_c[:, k:k + 1], start=(k == 0), stop=(k == KD - 1))
                last.then_inc(w_used, 1)
            pe.wait_ge(consts, CONSTS)
            pe.wait_ge(xs_done, NT)
            for j in range(KD):
                if j >= 4:
                    pe.wait_ge(hT_done, j - 3)
                for t in range(NT):
                    last = nc.tensor.transpose(ps[:, j % 4, t * P:(t + 1) * P], xs_rows[:, t, j * P:(j + 1) * P], ident[:])
                last.then_inc(xT_mm, 1)

            pe.wait_ge(hT_done, KD)

            def project(b, n, col):
                if col == 0:
                    pe.wait_ge(ld_w[n % 4], 16 * (n // 4 + 1))
                if b >= 4:
                    pe.wait_ge(proj_v, b - 3)
                w = strip(n)
                for k in range(KD):
                    last = nc.tensor.matmul(ps[:, b % 4, :], w[:, k, col:col + P], hT[:, k, :],
                                            start=(k == 0), stop=(k == KD - 1))
                last.then_inc(proj_mm, 1)

            pe.wait_ge(sel_done, 4)

            def qk_statistics(b):
                pe.wait_ge(qk_sqr, b + 1)
                nc.tensor.matmul(ps[0:16, 4, :], sel[:, b, :], sq[:, b % 2, :], start=(b == 0), stop=(b == 7)).then_inc(qk_stat, 1)

            for b, (n, col) in enumerate(rw_blocks):
                project(b, n, col)
            for n in (16, 17):
                pe.wait_ge(ld_w[n % 4], 16 * (n // 4 + 1))
            for t in range(NT):
                for i in range(2):
                    for k in range(KD):
                        last = nc.tensor.matmul(ps[:, 4 + t, 256 * i:256 * i + 256], hT[:, k, t * P:(t + 1) * P],
                                                strip(16 + i)[:, k, :], start=(k == 0), stop=(k == KD - 1))
                last.then_inc(v_mm, 1)
            pe.wait_ge(v_done, NT)
            for b, (n, col) in enumerate(qk_blocks):
                project(15 + b, n, col)
                if b >= 1:
                    qk_statistics(b - 1)
            qk_statistics(7)
            for b in range(NB):
                pe.wait_ge(kk_sqr, b + 1)
                nc.tensor.matmul(ps[0:8, 5, :], sel[:, b, 0:8], sq[:, b % 2, :], start=(b == 0), stop=(b == NB - 1)).then_inc(kk_stat, 1)
            pe.wait_ge(proj_v, 23)
            pe.wait_ge(qk_rstd, 1)
            for b in range(8):
                if b >= 4:
                    pe.wait_ge(qk_done, b - 3)
                nc.tensor.matmul(ps[:, b % 4, :], selT[:, b, :], stat[:], start=True, stop=True).then_inc(qk_bc, 1)
            pe.wait_ge(kk_inv, 1)
            for b in range(NB):
                pe.wait_ge(qk_done, b + 5)
                nc.tensor.matmul(ps[:, b, :], selT[0:8, b, :], stat_kk, start=True, stop=True).then_inc(kk_bc, 1)

            def scores(u):
                h, qt = u // NT, u % NT
                if u < 2:
                    pe.wait_ge(kk_done, NB)
                else:
                    pe.wait_ge(s_max, u - 1)
                for cmp in range(2):
                    r = slice(HD * cmp, HD * cmp + HD)
                    last = nc.tensor.matmul(ps[:, 2 * (u % 2) + cmp, :], qkT[r, h, qt * P:(qt + 1) * P], qkT[r, DA + h, :],
                                            start=True, stop=True)
                last.then_inc(s_mm, 1)

            def transpose_mix(u):
                pe.wait_ge(mixed, u + 1)
                if u >= 2:
                    pe.wait_ge(mixT_done, u - 1)
                for kt in range(NT):
                    last = nc.tensor.transpose(ps[:, 4 + u % 2, kt * P:(kt + 1) * P], mix[:, u % 2, kt * P:(kt + 1) * P], ident[:])
                last.then_inc(mixT_mm, 1)

            def values(u):
                h, qt = u // NT, u % NT
                pe.wait_ge(mixT_done, u + 1)
                if h >= 1 and qt == 0:
                    pe.wait_ge(o_copy, h)
                for kt in range(NT):
                    last = nc.tensor.matmul(ps[:, 6, qt * P:(qt + 1) * P], vA[:, kt, h * P:(h + 1) * P],
                                            mixT[:, u % 2, kt * P:(kt + 1) * P], start=(kt == 0), stop=(kt == NT - 1))
                last.then_inc(o_mm, 1)

            def second_modulation(u):
                n = 22 + u
                pe.wait_ge(ld_w[n % 4], 16 * (n // 4 + 1))
                w = strip(n)
                for half in range(2):
                    for k in range(KD):
                        last = nc.tensor.matmul(ps[:, 7, 2 * u + half:2 * u + half + 1], w[:, k, half * P:(half + 1) * P],
                                                silu_c[:, k:k + 1], start=(k == 0), stop=(k == KD - 1))
                last.then_inc(w_used, 1)

            scores(0)
            scores(1)
            for u in range(UN):
                transpose_mix(u)
                if u >= 1:
                    values(u - 1)
                if u + 2 < UN:
                    scores(u + 2)
                second_modulation(u)
            values(UN - 1)
            pe.wait_ge(o_copy, DA)
            pe.wait_ge(s_max, UN)
            for h in range(DA):
                last = nc.tensor.matmul(ps[0:DA, 0, :], selh[:, h, :], sq_o[:, h, :], start=(h == 0), stop=(h == DA - 1))
            last.then_inc(o_stat, 1)
            pe.wait_ge(o_rstd, 1)
            for h in range(DA):
                nc.tensor.matmul(ps[:, 1 + h, :], selhT[:, h, :], stat_o, start=True, stop=True).then_inc(o_bc, 1)


            def place(major, ch, h):
                half, block = (h, ch) if major == "features" else (ch % 2, NC // 2 * h + ch // 2)
                return slice(HD * half, HD * half + HD), block

            def each(d, name, source, result, *terms):
                b0 = bank_of(d, name)
                pe.nop(nofuse=True)
                apart = [[(0, 0), (0, 1)], [(1, 0), (1, 1)]] if source == result else [[(0, 0), (1, 1)], [(0, 1), (1, 0)]]
                for ch2 in range(0, NC, 2):
                    for two in apart:
                        for n, (lhs, rhs) in enumerate(terms):
                            for h, odd in two:
                                r, block = place(source, ch2 + odd, h)
                                o, o_block = place(result, ch2 + odd, h)
                                right = rhs(r, block)
                                w = right.shape[-1] * (2 if len(right.shape) == 3 else 1)
                                col = o_block * w if result == T else 512 * odd + ch2 // 2 * w
                                into = ps[o, b0 + col // 512, col % 512:col % 512 + w]
                                if len(right.shape) == 3:
                                    into = into.rearrange("p (a n) -> p a n", a=2)
                                last = nc.tensor.matmul(into, lhs(r, block), right,
                                                        start=(n == 0), stop=(n == len(terms) - 1))
                return last

            def turned(bank, rows):
                for ch2 in range(NC // 2):
                    last = nc.tensor.transpose(by_head(ps[:, bank, :], ch2), rows[:, ch2 * P:(ch2 + 1) * P], ident[:])
                return last

            def by_head(bank, ch2):
                return bank.rearrange("p (h c n) -> p h c n", h=2, c=NC // 2)[:, :, ch2, :]

            def at(ap, c0=0, w=CH):
                return lambda r, block: ap[r, block, c0:c0 + w]

            def both(ap):
                return lambda r, block: ap[r, :, block * CH:(block + 1) * CH]

            F, T = "features", "tokens"
            pe.wait_ge(o_done, DA)
            pe.wait_ge(lo_done, 2)
            pe.wait_ge(masks_done, 1)
            with pe.Fori(0, NB) as i:
                pe.wait_ge(pair_w, 2 * i + 2)
                for name, w, slot in (("decay", w2_pair, 0), ("iclr", a2_pair, 1)):
                    for d in range(2):
                        r = slice(HD * d, HD * d + HD)
                        nc.tensor.matmul(ps[:, bank_of(d, name), :], w[r, :], loT[r, slot, :], start=True, stop=True).then_inc(mm[d], 1)
                pe.wait_ge(v_fixed, i + 1)
                turned(7, v_fix).then_inc(vt_mm, 1)
                for d, r in enumerate(dirs):
                    pe.wait_ge(feat_v, 10 * i + 5 * d + 3)
                    pe.wait_ge(by_act[d], upto(ACT_STEPS, "decay", i))
                    turned(bank_of(d, "alpha_t"), r.alpha).then_inc(mm[d], 1)
                for d, r in enumerate(dirs):
                    pe.wait_ge(feat_p, 8 * i + 4 * d + 4)
                    turned(bank_of(d, "beta_t"), r.hat_b).then_inc(mm[d], 1)
                for d, r in enumerate(dirs):
                    pe.wait_ge(feat_v, 10 * i + 5 * d + 5)
                    pe.wait_ge(by_act[d], upto(ACT_STEPS, "alpha_t", i))
                    turned(bank_of(d, "kappa_t"), r.hat_k).then_inc(mm[d], 1)
                pe.wait_ge(vt_done, i + 1)
                for d, r in enumerate(dirs):
                    pe.wait_ge(by_act[d], upto(ACT_STEPS, "beta_t", i))
                    each(d, "gram_b", F, T, (at(by_chunk(r.beta)), both(r.ar))).then_inc(mm[d], 1)
                for d, r in enumerate(dirs):
                    pe.wait_ge(by_act[d], upto(ACT_STEPS, "kappa_t", i))
                    each(d, "gram_k", F, T, (at(by_chunk(r.kappa)), both(r.ar))).then_inc(mm[d], 1)
                for d, r in enumerate(dirs):
                    pe.wait_ge(by_dve[d], upto(DVE_STEPS, "gram_k", i))
                    each(d, "mv", T, T, (at(r.mb), at(v_t))).then_inc(mm[d], 1)
                for k in range(1, LEVELS):
                    for d, r in enumerate(dirs):
                        pe.wait_ge(c_done[d], 7 * i + 1 + k)
                        pe.wait_ge(by_dve[d], upto(DVE_STEPS, f"x{k - 1}", i))
                        pe.wait_ge(by_act[d], upto(ACT_STEPS, f"w{k - 1}" if k > 1 else "mv", i))
                        each(d, f"w{k}", T, T, (at(r.c[k % 2]), at(r.x))).then_inc(mm[d], 1)
                    for d, r in enumerate(dirs):
                        pe.wait_ge(by_dve[d], upto(DVE_STEPS, f"xt{k - 1}", i))
                        pe.wait_ge(by_act[d], upto(ACT_STEPS, f"w{k}", i))
                        if k < LEVELS - 1:
                            each(d, f"x{k}", T, T, (at(r.xt), at(r.w))).then_inc(mm[d], 1)
                        else:
                            each(d, f"xt{k}", T, T, (at(r.w), at(r.xt))).then_inc(mm[d], 1)
                for d, r in enumerate(dirs):
                    pe.wait_ge(by_dve[d], upto(DVE_STEPS, f"xt{LEVELS - 1}", i))
                    each(d, "gh", T, T, (at(r.xt), at(r.rhs, 0, 2 * CH))).then_inc(mm[d], 1)
                for d, r in enumerate(dirs):
                    pe.wait_ge(by_act[d], upto(ACT_STEPS, "gh", i))
                    each(d, "phi", T, F, (at(r.gh), at(r.beta_t))).then_inc(mm[d], 1)
                for d, r in enumerate(dirs):
                    each(d, "psi", T, F, (at(r.kappa_t), at(v_t)), (at(r.beta_t), at(r.gh, CH))).then_inc(mm[d], 1)
                for d, r in enumerate(dirs):
                    pe.wait_ge(by_dve[d], upto(DVE_STEPS, "phi", i))
                    each(d, "rho", T, F, (at(r.gh), at(r.la, CH))).then_inc(mm[d], 1)
                for d, r in enumerate(dirs):
                    pe.wait_ge(by_act[d], upto(ACT_STEPS, "psi", i))
                    each(d, "y", T, F, (at(v_t), at(r.mb, CH)), (at(r.gh, CH), at(r.la, CH))).then_inc(mm[d], 1)
                for d in range(2):
                    pe.wait_ge(by_dve[d], (i + 1) * len(DVE_STEPS))
                    pe.wait_ge(by_act[d], (i + 1) * len(ACT_STEPS))
            for st in range(1, NC - 1):
                pe.wait_ge(state_done, 2 * st)
                for q in range(2 * NB):
                    ch = st if q % 2 == 0 else NC - 1 - st
                    for h in range(2):
                        r = slice(HD * h, HD * h + HD)
                        last = nc.tensor.matmul(ps[r, st % 2, q * CH:(q + 1) * CH], PHI[r, q, ch * CH:(ch + 1) * CH],
                                                states[r, st, q * CH:(q + 1) * CH], start=True, stop=True)
                last.then_inc(state_mm, 1)
            pe.wait_ge(state_done, 2 * (NC - 1))
            for b in range(NB):
                for ch in range(NC):
                    terms = [(q, st) for q, st in ((2 * b, ch), (2 * b + 1, NC - 1 - ch)) if st > 0]
                    for n, (q, st) in enumerate(terms):
                        for h in range(2):
                            r = slice(HD * h, HD * h + HD)
                            last = nc.tensor.matmul(ps[r, 2 + b, ch * CH:(ch + 1) * CH], states[r, st, q * CH:(q + 1) * CH],
                                                    RP[r, q, ch * CH:(ch + 1) * CH], start=(n == 0), stop=(n == len(terms) - 1))
                last.then_inc(yst_mm, 1)
            for b in range(NB):
                pe.wait_ge(y_sum, b + 1)
                nc.tensor.matmul(ps[:, 2 + b, :], half_ones[:], YT[:, b, :], start=True, stop=True).then_inc(mean_mm, 1)
            for b in range(NB):
                pe.wait_ge(y_sqr, b + 1)
                last = nc.tensor.matmul(ps[0:8, 0, :], sel[:, b, 0:8], tmp2[:, b, :], start=(b == 0), stop=(b == NB - 1))
            last.then_inc(y_stat, 1)
            for b in range(NB):
                pe.wait_ge(rk_done, b + 1)
                if b >= 2:
                    pe.wait_ge(bon_done, b - 1)
                nc.tensor.matmul(ps[:, 6 + b % 2, :], half_ones[:], tmp[:, b, :], start=True, stop=True).then_inc(bon_mm, 1)
            pe.wait_ge(centred, NB)
            for b in range(NB):
                if b == 0:
                    pe.wait_ge(y_rstd, 1)
                nc.tensor.matmul(ps[:, 2 + b, :], selT[0:8, b, :], stat_y, start=True, stop=True).then_inc(y_bc, 1)
            for b in range(NB):
                if b < 2:
                    pe.wait_ge(bon_done, NB - 1 + b)
                else:
                    pe.wait_ge(rw_out, b - 1)
                nc.tensor.matmul(ps[:, 6 + b % 2, :], g2_sb[:, b * P:(b + 1) * P], loT[:, 2, :], start=True, stop=True).then_inc(gate_mm, 1)

            for g in range(8):
                pe.wait_ge(spread, g + 1)
                if g >= 2:
                    pe.wait_ge(rows_done, g - 1)
                nc.tensor.matmul(ps[:, g % 2, :], ones[:], col_diag[:, g, :], start=True, stop=True).then_inc(rows_mm, 1)
            pe.wait_ge(rw_out, NB)
            pe.wait_ge(ld_wo, 16)
            for t in range(NT):
                for n in range(2):
                    if 2 * t + n >= 4:
                        pe.wait_ge(wo_gated, 2 * t + n - 3)
                    for k in range(KD):
                        last = nc.tensor.matmul(ps[:, 2 + (2 * t + n) % 4, :], cat(k)[:, t * P:(t + 1) * P], wo[:, k, n * 512:(n + 1) * 512],
                                                start=(k == 0), stop=(k == KD - 1))
                    last.then_inc(wo_mm, 1)
            pe.wait_ge(ld_keys, 16)
            for g in range(4):
                if g >= 2:
                    pe.wait_ge(keysT_done, g - 1)
                for b in range(4):
                    last = nc.tensor.transpose(ps[:, 6 + g % 2, b * P:(b + 1) * P], keys_raw[:, 4 * g + b, :], ident[:])
                last.then_inc(keysT_mm, 1)
            pe.wait_ge(keysT_done, 4)
            pe.wait_ge(h2_done, NT)
            for j in range(KD):
                if j >= 2:
                    pe.wait_ge(h2T_done, j - 1)
                for t in range(NT):
                    last = nc.tensor.transpose(ps[:, 6 + j % 2, t * P:(t + 1) * P], h2[:, t, j * P:(j + 1) * P], ident[:])
                last.then_inc(h2T_mm, 1)
            pe.wait_ge(h2T_done, KD)

            def key_scores(b):
                pe.wait_ge(q_done, b + 1)
                if b >= 4:
                    pe.wait_ge(sc_done, b - 3)
                for t in range(NT):
                    last = nc.tensor.matmul(ps[:, 4 + b % 4, t * P:(t + 1) * P], qT[:, b % 4, t * P:(t + 1) * P], keysT[:, b, :],
                                            start=True, stop=True)
                last.then_inc(sc_mm, 1)

            for b in range(2 * PH):
                n = b // 2
                if b % 2 == 0:
                    pe.wait_ge(ld_w[n % 4], ring2_loaded(n))
                if b >= 4:
                    pe.wait_ge(q_done, b - 3)
                for k in range(KD):
                    last = nc.tensor.matmul(ps[:, b % 4, :], strip2(n)[:, k, P * (b % 2):P * (b % 2) + P], h2T[:, k, :],
                                            start=(k == 0), stop=(k == KD - 1))
                last.then_inc(q_mm, 1)
                if b >= 1:
                    key_scores(b - 1)
            key_scores(2 * PH - 1)

            pe.wait_ge(q_done, 2 * PH)
            with pe.Fori(0, NT) as t:
                for n in range(2):
                    nc.tensor.matmul(ps[:, n, :], zero_w[0:1, :], restart[0:1, :], start=True, stop=False)
                with pe.Fori(0, PH) as h:
                    for s in range(TOPK):
                        pe.wait_ge(diags, t * SLOTS + h * TOPK + (s + 1))
                        pe.wait_ge(ld_v[s % V_SLOTS], t * (PH * 32) + h * 32 + 16 * (s // V_SLOTS + 1))
                        for n in range(2):
                            last = nc.tensor.matmul(ps[:, n, :], diag[:, s % V_SLOTS, :], v_ring[:, s % V_SLOTS, n * 512:(n + 1) * 512],
                                                    start=False, stop=False)
                        last.then_inc(v_free, 1)
                for n in range(2):
                    last = nc.tensor.matmul(ps[:, n, :], zero_w[0:1, :], restart[0:1, :], start=False, stop=True)
                last.then_inc(tile_mm, 1)
                pe.wait_ge(o_gated, t * 2 + 2)

        @block.vector
        def _(dve):
            step = Tally(dve, dve_s)
            v = nc.vector
            dve.wait_ge(zeroed, 8)
            sel_flat = sel[:].rearrange("p b m -> p (b m)")
            for h in range(2):
                v.memset(sel_flat[HD * h:HD * h + HD, h:h + 127:18], 1.0).then_inc(sel_done, 1)
                v.memset(half_ones[HD * h:HD * h + HD, HD * h:HD * h + HD], 1.0).then_inc(sel_done, 1)
            dve.wait_ge(consts, CONSTS)
            step.link(v.scalar_tensor_tensor(bias_h[:, 0, :], bias_h[:, 0, :], -1.0, bias_h[:, 0, :], ALU.mult, ALU.min))
            for h in (3, 2, 1, 0):
                v.tensor_scalar(bias_h[:, h, :], bias_h[:, 0, :], 2.0 ** (-8.0 * (h + 1) / DA), None, ALU.mult).then_inc(bias_done, 1)
            step.link(v.tensor_scalar(s_idx[:], s_idx[:], CH - 1, None, ALU.bitwise_and))
            step(v.tensor_tensor(xor_idx[:], s_idx[:], t_idx[:], ALU.bitwise_xor))
            step(v.tensor_tensor(tri[:, 0, 0, :], s_idx[:], t_idx[:], ALU.is_lt))
            step(v.tensor_tensor(tri[:, 1, 0, :], s_idx[:], t_idx[:], ALU.is_gt))
            step(v.tensor_tensor(tri[:, 0, 1, :], s_idx[:], t_idx[:], ALU.is_le))
            step(v.tensor_tensor(tri[:, 1, 1, :], s_idx[:], t_idx[:], ALU.is_gt))
            step.link(v.tensor_tensor(eye[:], s_idx[:], t_idx[:], ALU.is_equal))
            for k in range(LEVELS):
                step.link(v.tensor_scalar(level[:, 1, k, :], xor_idx[:], float(2 ** k), None, ALU.is_ge))
                step.link(v.scalar_tensor_tensor(level[:, 1, k, :], xor_idx[:], float(2 ** (k + 1)), level[:, 1, k, :], ALU.is_lt, ALU.mult))
                step(v.tensor_tensor(level[:, 0, k, :], level[:, 1, k, :], tri[:, 0, 0, :], ALU.mult))
                last = v.tensor_tensor(level[:, 1, k, :], level[:, 1, k, :], tri[:, 1, 0, :], ALU.mult)
                if k < LEVELS - 1:
                    step(last)
            last.then_inc(masks_done, 1)
            dve.wait_ge(ss_done, NT)
            step.link(v.tensor_scalar(rstd[:], sumsq[:], 1.0 / D, NORM_EPS, ALU.mult, ALU.add))
            v.reciprocal(rstd[:], rstd[:]).then_inc(rv_done, 1)
            dve.wait_ge(ld_mu, 16 * 6)
            step.link(v.tensor_tensor(mu_self[:], mu[:, 0, :], mu[:, 1, :], ALU.add))
            v.tensor_scalar(mu_self[:], mu_self[:], -1.0, 1.0, ALU.mult, ALU.add).then_inc(mu_done, 1)
            dve.wait_ge(rstd_done, 1)
            for t in range(NT):
                v.tensor_scalar(xs_rows[:, t, :], x_rows[:, t, :], rstd[:, t:t + 1], None, ALU.mult).then_inc(xs_done, 1)
            dve.wait_ge(ld_par, 32)
            dve.wait_ge(w_used, 8)
            step.link(v.tensor_tensor(mod1[:], ps[:, 7, 0:16], ada_bc[:], ALU.add))
            v.scalar_tensor_tensor(mod1[:, 8:16], mod1[:, 8:16], 1.0, n1_col[:], ALU.add, ALU.mult).then_inc(mod1_done, 1)
            dve.wait_ge(ld_lam, 32)
            lam4 = lam[:].rearrange("p (a d) -> p a d", a=4)
            step.link(v.tensor_tensor(lam_p[:].rearrange("p (a d) -> p a d", a=2), lam4[:, 0:4:2, :], lam4[:, 1:4:2, :], ALU.mult))
            v.tensor_reduce(lam_e[:], lam_p[:].rearrange("p (a d) -> p a d", a=2), AX.X, ALU.add).then_inc(lam_sum, 1)
            dve.wait_ge(ld_rw, RW_LOADS)
            step(v.tensor_scalar(ka1_col[:], ka_col[:], -1.0, 1.0, ALU.mult, ALU.add))

            for b in range(15):
                dve.wait_ge(proj_a, b + 1)
                bank, dst = ps[:, b % 4, :], rw_dest(b)
                step.link(v.scalar_tensor_tensor(dst[:, 1:S], bank[:, 0:S - 1], mu[:, 0, b:b + 1], dst[:, 1:S], ALU.mult, ALU.add))
                v.scalar_tensor_tensor(dst[:, 0:S - 1], bank[:, 1:S], mu[:, 1, b:b + 1], dst[:, 0:S - 1], ALU.mult, ALU.add).then_inc(proj_v, 1)
            dve.wait_ge(proj_v, 15)
            for b in range(NB):
                v.tensor_scalar(kkT[:, b, :], kT[:, b, :], kk_col[:, b:b + 1], None, ALU.mult).then_inc(kk_raw, 1)
            for b in range(8):
                dve.wait_ge(qk_sqr, b + 1)
                v.tensor_scalar(qkT[:, b, :], ps[:, (15 + b) % 4, :], qk_gain[:, b // 4:b // 4 + 1], None, ALU.mult).then_inc(proj_v, 1)
            dve.wait_ge(qk_stat, 8)
            step.link(v.tensor_scalar(stat[:], ps[0:16, 4, :], 1.0 / HD, NORM_EPS, ALU.mult, ALU.add))
            v.reciprocal(stat[:], stat[:]).then_inc(qk_var, 1)
            dve.wait_ge(kk_norm, 1)
            step.link(v.tensor_scalar(stat_kk, stat_kk, 1e-12, None, ALU.max))
            v.reciprocal(stat_kk, stat_kk).then_inc(kk_inv, 1)
            for b in range(8):
                dve.wait_ge(qk_bc, b + 1)
                v.tensor_tensor(qkT[:, b, :], ps[:, b % 4, :], qkT[:, b, :], ALU.mult).then_inc(qk_done, 1)
            for b in range(NB):
                dve.wait_ge(kk_bc, b + 1)
                v.tensor_tensor(kkT[:, b, :], ps[:, b, :], kkT[:, b, :], ALU.mult).then_inc(kk_done, 1)
            dve.wait_ge(lam_exp, 1)
            step.link(v.tensor_tensor(neg_lam[:], lam_e[:, 1:2], lam_e[:, 0:1], ALU.subtract))
            step.link(v.tensor_scalar(neg_lam[:], neg_lam[:], -LAMBDA0, None, ALU.add))

            def maxima(u):
                h, qt, e = u // NT, u % NT, u % 2
                dve.wait_ge(s_mm, u + 1)
                first = 384 - qt * P
                for cmp in range(2):
                    step(v.tensor_tensor_reduce(out=probs[:, 2 * e + cmp, :], in0=ps[:, 2 * e + cmp, :],
                                                in1=bias_h[:, h, first:first + S], scale=1.0, scalar=LOWEST,
                                                op0=ALU.add, op1=ALU.max, accum_out=mx[:, e, cmp:cmp + 1]))
                step.eng.wait_ge(step.sem, step.n)
                v.tensor_scalar(nmx[:, e, :], mx[:, e, :], -1.0, None, ALU.mult).then_inc(s_max, 1)

            def mixture(u):
                e = u % 2
                dve.wait_ge(s_exp, 2 * u + 2)
                step.link(v.reciprocal(rden[:, e, :], den[:, e, :]))
                step(v.tensor_scalar(rden[:, e, 1:2], rden[:, e, 1:2], neg_lam[:, 0:1], None, ALU.mult))
                step.link(v.tensor_scalar(probs[:, 2 * e, :], probs[:, 2 * e, :], rden[:, e, 0:1], None, ALU.mult))
                if u >= 2:
                    dve.wait_ge(mixT_mm, u - 1)
                v.scalar_tensor_tensor(mix[:, e, :], probs[:, 2 * e + 1, :], rden[:, e, 1:2], probs[:, 2 * e, :],
                                       ALU.mult, ALU.add).then_inc(mixed, 1)

            dve.wait_ge(bias_done, DA)
            maxima(0)
            maxima(1)
            for u in range(UN):
                mixture(u)
                if u + 2 < UN:
                    maxima(u + 2)
            dve.wait_ge(o_stat, 1)
            step.link(v.tensor_scalar(stat_o, ps[0:DA, 0, :], 1.0 / P, NORM_EPS, ALU.mult, ALU.add))
            v.reciprocal(stat_o, stat_o).then_inc(o_var, 1)
            dve.wait_ge(w_used, 8 + 16)
            step.link(v.tensor_tensor(mod2[:], ps[:, 7, 0:32], ada_bc2[:], ALU.add))
            step.link(v.scalar_tensor_tensor(mod2[:, 16:24], mod2[:, 16:24], 1.0, n2_col[:], ALU.add, ALU.mult))
            for h in range(DA):
                dve.wait_ge(o_bc, h + 1)
                v.tensor_tensor(attT[:, h, :], ps[:, 1 + h, :], attT[:, h, :], ALU.mult).then_inc(o_done, 1)


            with dve.Fori(0, NB) as i:
                for d, r in enumerate(dirs):
                    dve.wait_ge(by_act[d], upto(ACT_STEPS, "decay", i))
                    turn = (lambda ap: ap) if d == 0 else (lambda ap: ap[:, ::-1])
                    v.tensor_tensor_scan(turn(r.cum), restart[:], turn(r.sg), 0.0, ALU.mult, ALU.add).then_inc(cum_done, 1)
                for d, r in enumerate(dirs):
                    end = CH - 1 if d == 0 else 0
                    dve.wait_ge(by_act[d], upto(ACT_STEPS, "iclr", i))
                    v.tensor_scalar(r.kappa, r.a, ka_col[:, bass.ds(i, 1)], ka1_col[:, bass.ds(i, 1)], ALU.mult, ALU.add).then_inc(kap, 1)
                    dve.wait_ge(kap, 4 * i + 2 * d + 1)
                    v.tensor_tensor(r.kappa, r.kappa, pair_of(4, i), ALU.mult).then_inc(kap, 1)
                    dve.wait_ge(exps, 6 * i + 3 * d + 2)
                    v.tensor_copy(ptot[:, d, :].unsqueeze(2), by_chunk(r.pinc)[:, :, end:end + 1]).then_inc(feat_v, 1)
                    dve.wait_ge(kap, 4 * i + 2 * d + 2)
                    v.tensor_tensor(r.kappa, r.kappa, r.pinv, ALU.mult).then_inc(feat_v, 1)
                    dve.wait_ge(exps, 6 * i + 3 * d + 3)
                    v.tensor_tensor(r.alpha, r.pexc, pair_of(12, i), ALU.mult).then_inc(feat_v, 1)
                    v.tensor_tensor(r.rho, r.pinc if d == 0 else r.pexc, pair_of(0, i), ALU.mult).then_inc(feat_v, 1)
                    dve.wait_ge(feat_v, 10 * i + 5 * d + 2)
                    v.tensor_tensor(by_chunk(r.hat_k), by_chunk(r.kappa), ptot[:, d, :].unsqueeze(2).to_broadcast([P, NC, CH]),
                                    ALU.mult).then_inc(feat_v, 1)

                def banks(d, name, width=1):
                    b = bank_of(d, name)
                    return ps[:, b:b + width, :].rearrange("p b n -> p (b n)").rearrange("p (c n) -> p c n", c=NC)

                for name in ("gram_b", "gram_k"):
                    for d, r in enumerate(dirs):
                        dve.wait_ge(mm[d], upto(STEPS, name, i))
                        mask = tri[:, d, :, :].rearrange("p a t -> p (a t)").unsqueeze(1).to_broadcast([P, NC, 2 * CH])
                        v.tensor_tensor(r.la if name == "gram_b" else r.mb, banks(d, name, 2), mask, ALU.mult).then_inc(by_dve[d], 1)
                for d, r in enumerate(dirs):
                    dve.wait_ge(c_done[d], 7 * i + 1)
                    v.tensor_tensor(r.xt, eye[:].unsqueeze(1).to_broadcast([P, NC, CH]), r.c[0], ALU.subtract).then_inc(by_dve[d], 1)
                for d, r in enumerate(dirs):
                    dve.wait_ge(by_dve[d], upto(DVE_STEPS, "xt0", i))
                    v.transpose(flat(r.x), flat(r.xt)).then_inc(by_dve[d], 1)
                for k in range(1, LEVELS - 1):
                    for d, r in enumerate(dirs):
                        dve.wait_ge(mm[d], upto(STEPS, f"x{k}", i))
                        v.tensor_tensor(r.x, r.x, banks(d, f"x{k}"), ALU.subtract).then_inc(by_dve[d], 1)
                    for d, r in enumerate(dirs):
                        dve.wait_ge(by_dve[d], upto(DVE_STEPS, f"x{k}", i))
                        v.transpose(flat(r.xt), flat(r.x)).then_inc(by_dve[d], 1)
                for d, r in enumerate(dirs):
                    dve.wait_ge(mm[d], upto(STEPS, f"xt{LEVELS - 1}", i))
                    v.tensor_tensor(r.xt, r.xt, banks(d, f"xt{LEVELS - 1}"), ALU.subtract).then_inc(by_dve[d], 1)
                for d, r in enumerate(dirs):
                    dve.wait_ge(c_done[d], 7 * i + 7)
                    dve.wait_ge(mm[d], upto(STEPS, "phi", i))
                    v.tensor_tensor(odd_even(pair_of(23 + d, i * 2)), odd_even(flat(r.dg)), feature_banks(bank_of(d, "phi")), ALU.add).then_inc(by_dve[d], 1)
                for d, r in enumerate(dirs):
                    dve.wait_ge(mm[d], upto(STEPS, "rho", i))
                    v.tensor_tensor(odd_even(pair_of(39 + d, i * 2)), odd_even(r.rho),
                                    feature_banks(bank_of(d, "rho")), ALU.add).then_inc(by_dve[d], 1)
                dve.wait_ge(mm[0], upto(STEPS, "y", i))
                v.tensor_copy(odd_even(pair_of(47, i)), feature_banks(bank_of(0, "y"))).then_inc(by_dve[0], 1)
                dve.wait_ge(mm[1], upto(STEPS, "y", i))
                dve.wait_ge(by_dve[0], upto(DVE_STEPS, "y", i))
                v.tensor_tensor(odd_even(pair_of(47, i)), odd_even(pair_of(47, i)), feature_banks(bank_of(1, "y")), ALU.add).then_inc(by_dve[1], 1)
                for d in range(2):
                    dve.wait_ge(mm[d], (i + 1) * len(STEPS))
                    dve.wait_ge(by_act[d], (i + 1) * len(ACT_STEPS))
                    dve.wait_ge(by_dve[d], (i + 1) * len(DVE_STEPS))
                    dve.wait_ge(c_done[d], 7 * i + 7)


            def of_dir(ap, d):
                return ap.rearrange("p (b n) -> p b n", b=NB)[:, :, d * CH:(d + 1) * CH]

            psi = PSI.rearrange("p (b a) n -> p b a n", a=2)
            for st in range(NC - 1):
                for d in range(2):
                    ch = st if d == 0 else NC - 1 - st
                    dst, part = of_dir(states[:, st + 1, :], d), psi[:, :, d, ch * CH:(ch + 1) * CH]
                    if st == 0:
                        v.tensor_copy(dst, part).then_inc(state_done, 1)
                    else:
                        dve.wait_ge(state_mm, st)
                        v.tensor_tensor(dst, of_dir(ps[:, st % 2, :], d), part, ALU.add).then_inc(state_done, 1)
            dve.wait_ge(state_done, 2 * (NC - 1))
            for g in range(8):
                v.tensor_tensor(col_diag[:, g, :].rearrange("p (c n) -> p c n", c=4), ident[:].unsqueeze(1).to_broadcast([P, 4, P]),
                                mod2[:, 4 * g:4 * g + 4].unsqueeze(2).to_broadcast([P, 4, P]), ALU.mult).then_inc(spread, 1)
            for b in range(NB):
                v.scalar_tensor_tensor(tmp[:, b, :], rT[:, b, :], rk_col[:, b:b + 1], kT[:, b, :], ALU.mult, ALU.mult).then_inc(rk_done, 1)
            for b in range(NB):
                dve.wait_ge(yst_mm, b + 1)
                v.tensor_tensor(YT[:, b, :], YT[:, b, :], ps[:, 2 + b, :], ALU.add).then_inc(y_sum, 1)
            for b in range(NB):
                dve.wait_ge(y_sum, b + 1)
                dve.wait_ge(mean_mm, b + 1)
                v.scalar_tensor_tensor(YT[:, b, :], ps[:, 2 + b, :], -1.0 / HD, YT[:, b, :], ALU.mult, ALU.add).then_inc(centred, 1)
            dve.wait_ge(y_stat, 1)
            step.link(v.tensor_scalar(stat_y, ps[0:8, 0, :], 1.0 / HD, GN_EPS, ALU.mult, ALU.add))
            v.reciprocal(stat_y, stat_y).then_inc(y_var, 1)
            for b in range(NB):
                dve.wait_ge(bon_mm, b + 1)
                v.tensor_tensor(tmp[:, b, :], ps[:, 6 + b % 2, :], vT[:, b, :], ALU.mult).then_inc(bon_done, 1)
            dve.wait_ge(y_sqr, NB)
            for b in range(NB):
                dve.wait_ge(y_bc, b + 1)
                step.link(v.tensor_tensor(YT[:, b, :], YT[:, b, :], ps[:, 2 + b, :], ALU.mult))
                step.link(v.tensor_scalar(YT[:, b, :], YT[:, b, :], lg_col[:, b:b + 1], lb_col[:, b:b + 1], ALU.mult, ALU.add))
                dve.wait_ge(bon_done, b + 1)
                step.link(v.tensor_tensor(YT[:, b, :], YT[:, b, :], tmp[:, b, :], ALU.add))
                dve.wait_ge(gate_mm, b + 1)
                v.tensor_tensor(YT[:, b, :], YT[:, b, :], ps[:, 6 + b % 2, :], ALU.mult).then_inc(rw_out, 1)

            dve.wait_ge(rows_done, 2)
            for t in range(NT):
                dve.wait_ge(ld_x[t], 32)
                for n in range(2):
                    g, cols = 2 * t + n, slice(512 * n, 512 * n + 512)
                    dve.wait_ge(wo_mm, g + 1)
                    v.tensor_tensor(h2[:, t, cols], ps[:, 2 + g % 4, :], gate1[:, cols], ALU.mult).then_inc(wo_gated, 1)
                    dve.wait_ge(wo_gated, g + 1)
                    v.tensor_tensor(x1[:, t, cols], x1[:, t, cols], h2[:, t, cols], ALU.add).then_inc(x1_done, 1)
            dve.wait_ge(ss2, NT)
            step.link(v.tensor_scalar(rstd[:], sumsq[:], 1.0 / D, NORM_EPS, ALU.mult, ALU.add))
            v.reciprocal(rstd[:], rstd[:]).then_inc(rv2, 1)
            dve.wait_ge(rstd2, 1)
            dve.wait_ge(rows_done, 8)
            for t in range(NT):
                v.scalar_tensor_tensor(h2[:, t, :], x1[:, t, :], rstd[:, t:t + 1], scale2, ALU.mult, ALU.mult).then_inc(h2a, 1)
            for t in range(NT):
                dve.wait_ge(h2a, t + 1)
                v.tensor_tensor(h2[:, t, :], h2[:, t, :], shift2, ALU.add).then_inc(h2_done, 1)
            by_block = scores_all[:, 0:2 * PH * NT * NKEY].rearrange("p (t b n) -> p t b n", t=NT, b=2 * PH)
            for b in range(2 * PH):
                dve.wait_ge(sc_mm, b + 1)
                v.tensor_copy(by_block[:, :, b, :], ps[:, 4 + b % 4, :].rearrange("p (t n) -> p t n", t=NT)).then_inc(sc_done, 1)
            def choose(u):
                dve.wait_ge(sc_fixed, u + 1)

                def best16(srcs, cuts, rows, done):
                    n = len(srcs)

                    def inputs_at(k):
                        dve.wait_ge(best, u * CHOICE_OPS + k)

                    for i in range(n):
                        if done:
                            inputs_at(done)
                        dve.nop(nofuse=True)
                        v.max(top[:, rows + i, 0:8], srcs[i]).then_inc(best, 1)
                    for i in range(n):
                        inputs_at(done + i + 1)
                        dve.nop(nofuse=True)
                        v.max_index(top_i[:, rows + i, 0:8], top[:, rows + i, 0:8], srcs[i]).then_inc(best, 1)
                    for i in range(n):
                        v.match_replace(cuts[i], top[:, rows + i, 0:8], srcs[i], LOWEST).then_inc(best, 1)
                    for i in range(n):
                        inputs_at(done + 2 * n + i + 1)
                        dve.nop(nofuse=True)
                        v.max(top[:, rows + i, 8:16], cuts[i]).then_inc(best, 1)
                    for i in range(n):
                        inputs_at(done + 3 * n + i + 1)
                        dve.nop(nofuse=True)
                        v.max_index(top_i[:, rows + i, 8:16], top[:, rows + i, 8:16], cuts[i]).then_inc(best, 1)

                best16([sc[:, 0:NKEY], sc[:, NKEY:]], [sc_cut[:, 0:NKEY], sc_cut[:, NKEY:]], 0, 0)
                dve.wait_ge(best, u * CHOICE_OPS + 10)
                v.tensor_tensor(cand.rearrange("p (a b) -> p a b", a=TOPK), top[:, 0, :].unsqueeze(2).to_broadcast([P, TOPK, TOPK]),
                                top[:, 1, :].unsqueeze(1).to_broadcast([P, TOPK, TOPK]), ALU.add).then_inc(best, 1)
                best16([cand], [cand_cut], 2, 11)
                v.tensor_scalar(neg_top[:], top[:, 2, 0:1], -1.0, None, ALU.mult).then_inc(neg_done, 1)

            def resolve(u):
                base = lambda k: u * 7 + k
                places = top_i[:, 2, :].bitcast(I32)
                dve.wait_ge(best, u * CHOICE_OPS + CHOICE_OPS)
                v.tensor_scalar(ci_hi[:], places, 4, None, ALU.logical_shift_right).then_inc(math_s, 1)
                v.tensor_scalar(ci_lo[:], places, TOPK - 1, None, ALU.bitwise_and).then_inc(math_s, 1)
                for a, ci in enumerate((ci_hi, ci_lo)):
                    dve.wait_ge(math_s, base(a + 1))
                    v.tensor_tensor(pick[:, a], ci[:].unsqueeze(2).to_broadcast([P, TOPK, TOPK]),
                                    iota16i[:].unsqueeze(1).to_broadcast([P, TOPK, TOPK]), ALU.is_equal).then_inc(math_s, 1)
                for a in range(2):
                    dve.wait_ge(math_s, base(a + 3))
                    v.tensor_tensor(pick[:, a], pick[:, a], top_i[:, a, :].bitcast(I32).unsqueeze(1).to_broadcast([P, TOPK, TOPK]),
                                    ALU.mult).then_inc(math_s, 1)
                dve.wait_ge(math_s, base(6))
                v.tensor_reduce(e_half[:], pick, AX.X, ALU.add).then_inc(math_s, 1)
                dve.wait_ge(math_s, base(7))
                v.scalar_tensor_tensor(e_idx[:, bass.ds(u * TOPK, TOPK)], e_half[:, 0, :], float(NKEY), e_half[:, 1, :],
                                       ALU.mult, ALU.add).then_inc(e_done, 1)
                dve.wait_ge(g_exp, u + 1)
                dve.wait_ge(neg_done, u + 1)
                step_r(v.reciprocal(g_den[:], g_den[:]), u + 1)
                v.tensor_scalar(gates[:, bass.ds(u * TOPK, TOPK)], g_exp_t[:], g_den[:, 0:1], None, ALU.mult).then_inc(g_done, 1)

            def step_r(ins, n):
                ins.then_inc(g_rec, 1)
                dve.wait_ge(g_rec, n)

            with dve.Fori(0, 2) as u:
                choose(u)
                resolve(u)
            with dve.Fori(0, NT) as t:
                dve.wait_ge(h2_done, NT)
                v.tensor_copy(h2_fix, arena[:, bass.ds(t * 2 + 52, 2), :].rearrange("p u n -> p (u n)")).then_inc(h2_fixed, 1)
                with dve.Fori(0, PH) as h:
                    dve.wait_ge(h2_fixed, t + 1)
                    dve.wait_ge(g_done, t * PH + h + 1)

                    def weigh(g):
                        dve.wait_ge(gelu_done, t * (PH * 4) + h * 4 + (g + 1))
                        v.tensor_tensor(w16[:, 4 * g:4 * g + 4], gelu16[:, 4 * g:4 * g + 4],
                                        gates[:, bass.ds(t * SLOTS + h * TOPK + 4 * g, 4)], ALU.mult).then_inc(w_done, 1)

                    for g in range(4):
                        for b in range(U_SLOTS):
                            s = 4 * g + b
                            dve.wait_ge(ld_u[b], t * (PH * 64) + h * 64 + 16 * (g + 1))
                            dve.wait_ge(u_free, t * SLOTS + h * TOPK + (U_SLOTS + s - 1))
                            v.tensor_tensor_reduce(out=waste[:, s % 2, :], in0=u_ring[:, b, :], in1=h2_fix, scale=1.0, scalar=0.0,
                                                   op0=ALU.mult, op1=ALU.add, accum_out=act16[:, s:s + 1]).then_inc(u_free, 1)
                            if b == 0 and g > 0:
                                weigh(g - 1)
                        if g == 1:
                            choose(t * PH + h + 2)
                        if g == 2:
                            resolve(t * PH + h + 2)
                    weigh(3)
                dve.wait_ge(tile_mm, t + 1)
                for n in range(2):
                    cols = slice(512 * n, 512 * n + 512)
                    v.tensor_tensor(o_rows[:, cols], ps[:, n, :], gate2[:, cols], ALU.mult).then_inc(o_gated, 1)
                for n in range(2):
                    cols = slice(512 * n, 512 * n + 512)
                    dve.wait_ge(o_gated, t * 2 + (n + 1))
                    v.tensor_tensor(o_rows[:, cols], o_rows[:, cols], pair_of(n, t * 2), ALU.add).then_inc(o_sum, 1)
                dve.wait_ge(st_out, t * 16 + 16)


_INS = ["x", "c", "ada_w", "ada_b", "norm1_g", "w_in", "da_qnorm_g", "da_knorm_g", "da_lambda", "da_subln_g",
        "rw_shift_mu", "rw_w0", "rw_w2", "rw_a0", "rw_a2", "rw_g2", "rw_k_k", "rw_k_a", "rw_r_k", "rw_ln_g", "rw_ln_b",
        "w_out", "norm2_g", "peer_wq", "peer_keys", "peer_u", "peer_v"]
_FLAT = {"x", "ada_w", "w_in", "w_out", "peer_wq", "peer_u", "peer_v"}


def lay(**inputs):
    import numpy as np
    arrays = {}
    for name in _INS:
        a = np.ascontiguousarray(inputs[name])
        arrays[name] = a.reshape(a.shape[1:]) if name in _FLAT else a
    arrays["peer_keys"] = arrays["peer_keys"].reshape(2 * PH, NKEY, P)
    return arrays


def kernel(**inputs):
    import concourse.bacc as _bacc
    from concourse import mybir as _mybir
    from concourse.bass_utils import run_bass_kernel_spmd as _run

    nc = _bacc.Bacc("TRN2", target_bir_lowering=False, num_devices=1)
    laid = lay(**inputs)
    arrays, args = {}, []
    for name in _INS:
        a = laid[name]
        arrays[f"in_{name}_dram"] = a
        args.append(nc.dram_tensor(f"in_{name}_dram", a.shape, _mybir.dt.from_np(a.dtype), kind="ExternalInput").ap())
    out = nc.dram_tensor("out_0_dram", (S, D), F32, kind="ExternalOutput").ap()
    hymba_kernel(nc, *args, out)
    r = _run(nc, [arrays], core_ids=[0])
    return r.results[0]["out_0_dram"].reshape(1, S, D)
```

```python
import math
from contextlib import ExitStack

import concourse.bass as bass
from concourse import mybir

F32 = mybir.dt.float32
I32 = mybir.dt.int32
U32 = mybir.dt.uint32
ALU = mybir.AluOpType
ACT = mybir.ActivationFunctionType
AX = mybir.AxisListType

P = 128
D = 1024
S = 512
NT = S // P
KD = D // P
HD = 64
DA = 4
NB = 4
RW0 = 3 * 512
CH = 64
NC = S // CH
LEVELS = 6
PH = 8
TOPK = 16
NKEY = 128
UNITS = PH * NT
U_SLOTS, V_SLOTS = 4, 8
CHOICE_OPS = 16
NORM_EPS = 1e-6
GN_EPS = 64e-5
DECAY = math.exp(-0.5)
LAMBDA0 = 0.8 - 0.6 * math.exp(0.0)
LOWEST = -3.0e38
UNIT = 512


class Tally:

    def __init__(self, eng, sem):
        self.eng, self.sem, self.n = eng, sem, 0

    def __call__(self, instruction):
        instruction.then_inc(self.sem, 1)
        self.n += 1

    def link(self, instruction):
        self(instruction)
        self.eng.wait_ge(self.sem, self.n)


STEPS = ["decay", "iclr", "alpha_t", "beta_t", "kappa_t", "gram_b", "gram_k", "mv"]
for _k in range(1, LEVELS):
    STEPS += [f"w{_k}", f"x{_k}" if _k < LEVELS - 1 else f"xt{_k}"]
STEPS += ["gh", "phi", "psi", "rho", "y"]
ACT_STEPS = ["decay", "iclr", "alpha_t", "beta_t", "kappa_t", "mv"] + [f"w{_k}" for _k in range(1, LEVELS)] + ["gh", "psi"]
DVE_STEPS = ["gram_b", "gram_k", "xt0", "x0"]
for _k in range(1, LEVELS - 1):
    DVE_STEPS += [f"x{_k}", f"xt{_k}"]
DVE_STEPS += [f"xt{LEVELS - 1}", "phi", "rho", "y"]


def upto(steps, name, i):
    return i * len(steps) + (steps.index(name) + 1)


def hymba_kernel(nc, x, c, ada_w, ada_b, norm1_g, w_in, da_qnorm_g, da_knorm_g, da_lambda, da_subln_g,
                 rw_shift_mu, rw_w0, rw_w2, rw_a0, rw_a2, rw_g2, rw_k_k, rw_k_a, rw_r_k, rw_ln_g, rw_ln_b,
                 w_out, norm2_g, peer_wq, peer_keys, peer_u, peer_v, out):
    with ExitStack() as ctx:
        def sb(name, shape, dt=F32):
            return ctx.enter_context(nc.sbuf_tensor(name, shape, dt))

        def sem(name):
            return ctx.enter_context(nc.semaphore(name))

        ident = sb("ident", [P, P])
        sel = sb("sel", [P, 8, 16])
        selT = sb("selT", [16, 8, P])
        selh = sb("selh", [P, DA, DA])
        selhT = sb("selhT", [DA, DA, P])
        ones = sb("ones", [P, P])
        half_ones = sb("half_ones", [P, P])
        qk_fold = sb("qk_fold", [16, 1])
        restart = sb("restart", [P, S])
        s_idx = sb("s_idx", [P, CH], I32)
        t_idx = sb("t_idx", [P, CH], I32)
        xor_idx = sb("xor_idx", [P, CH], I32)
        level = sb("level", [P, 2, LEVELS, CH])
        tri = sb("tri", [P, 2, 2, CH])
        eye = sb("eye", [P, CH])
        c_col = sb("c_col", [P, KD])
        silu_c = sb("silu_c", [P, KD])
        ada_bc = sb("ada_bc", [P, 16])
        ada_bc2 = sb("ada_bc2", [P, 32])
        n2_col = sb("n2_col", [P, KD])
        mod2 = sb("mod2", [P, 32])
        n1_col = sb("n1_col", [P, KD])
        mod1 = sb("mod1", [P, 16])
        qk_gain = sb("qk_gain", [P, 2])
        mu = sb("mu", [P, 2, 15])
        mu_self = sb("mu_self", [P, 15])
        sub_g = sb("sub_g", [P, 1])
        lam = sb("lam", [P, 4 * HD])
        lam_p = sb("lam_p", [P, 2 * HD])
        lam_e = sb("lam_e", [P, 2])
        neg_lam = sb("neg_lam", [P, 1])
        w0_col = sb("w0_col", [P, 2, NB])
        a0_col = sb("a0_col", [P, 2, NB])
        kk_col = sb("kk_col", [P, NB])
        ka_col = sb("ka_col", [P, NB])
        ka1_col = sb("ka1_col", [P, NB])
        rk_col = sb("rk_col", [P, NB])
        lg_col = sb("lg_col", [P, NB])
        lb_col = sb("lb_col", [P, NB])
        w2_sb = sb("w2_sb", [P, 512])
        a2_sb = sb("a2_sb", [P, 512])
        g2_sb = sb("g2_sb", [P, 512])
        w2_pair = sb("w2_pair", [P, P])
        a2_pair = sb("a2_pair", [P, P])
        sumsq = sb("sumsq", [P, NT])
        rstd = sb("rstd", [P, NT])
        stat = sb("stat", [16, S])
        mx = sb("mx", [P, 2, 2])
        nmx = sb("nmx", [P, 2, 2])
        den = sb("den", [P, 2, 2])
        rden = sb("rden", [P, 2, 2])
        ptot = sb("ptot", [P, 2, NC])

        top = sb("top", [P, 3, TOPK])
        top_i = sb("top_i", [P, 3, TOPK], U32)
        neg_top = sb("neg_top", [P, 1])
        ci_lo = sb("ci_lo", [P, TOPK], I32)
        ci_hi = sb("ci_hi", [P, TOPK], I32)
        e_half = sb("e_half", [P, 2, TOPK])
        g_exp_t = sb("g_exp_t", [P, TOPK])
        g_den = sb("g_den", [P, 1])
        iota16i = sb("iota16i", [P, TOPK], I32)
        idx_col = sb("idx_col", [P, TOPK], I32)
        act16 = sb("act16", [P, TOPK])
        gelu16 = sb("gelu16", [P, TOPK])
        w16 = sb("w16", [P, TOPK])
        zero_w = sb("zero_w", [P, P])

        NU = 87
        arena = sb("arena", [P, NU, UNIT])

        def units(u, n):
            return arena[:, u:u + n, :]

        rT, kT, vT, kkT = units(0, 4), units(4, 4), units(8, 4), units(12, 4)
        attT = units(16, 4)
        loT = units(20, 3)
        qkT = units(23, 8)
        vA = units(31, 4)
        hT = units(35, 8)
        ring = units(43, 16)
        xs = units(59, 8)
        xr = units(67, 8)
        sq = units(75, 2)
        sq_o = units(67, DA)
        stat_kk, stat_o = arena[0:8, 84, :], arena[0:DA, 85, :]
        mod_acc = units(71, 4).rearrange("p u n -> p (u n)").rearrange("p (s n) -> p s n", s=8)
        bias = units(77, 7)
        bias_h = bias.rearrange("p u n -> p (u n)").rearrange("p (h n) -> p h n", h=DA)
        probs = units(59, 4)
        mix = units(63, 2)
        mixT = units(65, 2)
        PHI, PSI, RP, YT = units(23, 8), units(31, 8), units(39, 8), units(47, 4)
        vt_u = units(51, 1)
        dir_u = [52, 69]
        ps = ctx.enter_context(nc.psum_tensor("ps", [P, 8, 512], F32))

        def chunks(ap):
            return ap.rearrange("p u n -> p (u n)").rearrange("p (c n) -> p c n", c=NC)

        class Dir:

            def __init__(self, u):
                self.bk = units(u, 2)
                self.beta, self.kappa = arena[:, u, :], arena[:, u + 1, :]
                self.gh = chunks(units(u, 2))
                self.hat_b, self.hat_k = arena[:, u + 2, :], arena[:, u + 3, :]
                self.la = chunks(units(u + 2, 2))
                self.ar = units(u + 4, 2)
                self.alpha, self.rho = arena[:, u + 4, :], arena[:, u + 5, :]
                self.rhs = chunks(units(u + 6, 2))
                self.beta_t, self.kappa_t = chunks(units(u + 8, 1)), chunks(units(u + 9, 1))
                self.mb = chunks(units(u + 10, 2))
                t = u + 12
                self.dg = chunks(units(t, 1))
                self.sg, self.a, self.cum = arena[:, t, :], arena[:, t + 1, :], arena[:, t + 2, :]
                self.pinc, self.pinv, self.pexc = arena[:, t + 3, :], arena[:, t + 4, :], self.sgx(t)
                self.c = [chunks(units(t, 1)), chunks(units(t + 1, 1))]
                self.x, self.xt, self.w = chunks(units(t + 2, 1)), chunks(units(t + 3, 1)), chunks(units(t + 4, 1))

            def sgx(self, t):
                return arena[:, t, :]

        dirs = [Dir(u) for u in dir_u]
        x1 = units(0, 8).rearrange("p u n -> p (u n)").rearrange("p (t d) -> p t d", t=NT)
        mod_rows = units(8, 8).rearrange("p u n -> p (u n)").rearrange("p (m d) -> p m d", m=4)
        gate1, shift2, scale2, gate2 = (mod_rows[:, m, :] for m in range(4))
        col_diag = units(31, 8)
        h2T = units(69, 8)
        wq_strip = units(81, 4).rearrange("p u n -> p (u n)").rearrange("p (k n) -> p k n", k=KD)
        h2 = units(52, 8).rearrange("p u n -> p (u n)").rearrange("p (t d) -> p t d", t=NT)
        wo = units(69, 16).rearrange("p u n -> p (u n)").rearrange("p (k n) -> p k n", k=KD)
        keys_raw = units(60, 4).rearrange("p u n -> p (u n)").rearrange("p (b n) -> p b n", b=16)
        keysT = units(64, 4).rearrange("p u n -> p (u n)").rearrange("p (b n) -> p b n", b=16)
        qT = units(77, 2)
        scores = units(79, 2).rearrange("p u n -> p (u n)").rearrange("p (t a n) -> p t a n", t=NT, a=2)
        gates = units(16, 2).rearrange("p u n -> p (u n)")
        e_idx = units(18, 2).rearrange("p u n -> p (u n)").bitcast(I32)
        sc_cut = arena[:, 20, 0:256]
        cand, cand_cut = arena[:, 21, 0:256], arena[:, 21, 256:512]
        pick = arena[:, 22, :].rearrange("p (a r m) -> p a r m", a=2, r=TOPK)
        v_ring = units(23, 16).rearrange("p u n -> p (u n)").rearrange("p (s d) -> p s d", s=V_SLOTS)
        u_ring = units(39, 8).rearrange("p u n -> p (u n)").rearrange("p (s d) -> p s d", s=U_SLOTS)
        gated = units(8, 2)
        diag = units(49, 2).rearrange("p u n -> p (u n)").rearrange("p (s m) -> p s m", s=V_SLOTS)
        waste = units(10, 4).rearrange("p u n -> p (u n)").rearrange("p (s d) -> p s d", s=2)
        v_t = chunks(vt_u)
        v_fix = arena[:, 86, :]
        states = units(52, NC)
        tmp = units(60, 4)
        tmp2 = units(64, 4)
        stat_y = arena[0:8, 68, :]

        def pair_of(u, i, n=1):
            return arena[:, bass.ds(i + u, 1), :].rearrange("p a n -> p (a n)")

        def feature_banks(b):
            return ps[:, b:b + 2, 0:NC // 2 * CH].rearrange("p o (c n) -> p o c n", c=NC // 2)

        def odd_even(ap):
            return ap.rearrange("p (c o n) -> p o c n", c=NC // 2, o=2)

        def flat(ap):
            return ap.rearrange("p c n -> p (c n)")

        def by_chunk(ap):
            return ap.rearrange("p (c n) -> p c n", c=NC)

        ld_c = sem("ld_c"); ld_par = sem("ld_par"); ld_mu = sem("ld_mu"); ld_rw = sem("ld_rw"); ld_lam = sem("ld_lam")
        ld_x = [sem(f"ld_x{t}") for t in range(NT)]
        ld_w = [sem(f"ld_w{i}") for i in range(4)]
        w_used = sem("w_used")
        zeroed = sem("zeroed"); consts = sem("consts"); sel_done = sem("sel_done"); masks = sem("masks")
        silu_done = sem("silu_done"); mod1_done = sem("mod1_done"); mu_done = sem("mu_done")
        ss_done = sem("ss_done"); rv_done = sem("rv_done"); rstd_done = sem("rstd_done")
        xs_done = sem("xs_done"); xT_mm = sem("xT_mm"); hT_done = sem("hT_done")
        proj_mm = sem("proj_mm"); proj_a = sem("proj_a"); proj_v = sem("proj_v")
        qk_sqr = sem("qk_sqr"); qk_stat = sem("qk_stat")
        v_mm = sem("v_mm"); v_done = sem("v_done")
        qk_var = sem("qk_var"); qk_rstd = sem("qk_rstd"); qk_bc = sem("qk_bc"); qk_done = sem("qk_done")
        lo_done = sem("lo_done")
        kk_raw = sem("kk_raw"); kk_sqr = sem("kk_sqr"); kk_stat = sem("kk_stat")
        kk_norm = sem("kk_norm"); kk_inv = sem("kk_inv"); kk_bc = sem("kk_bc"); kk_done = sem("kk_done")
        bias_done = sem("bias_done"); lam_sum = sem("lam_sum"); lam_exp = sem("lam_exp")
        s_mm = sem("s_mm"); s_max = sem("s_max"); s_exp = sem("s_exp"); mixed = sem("mixed")
        mixT_mm = sem("mixT_mm"); mixT_done = sem("mixT_done"); o_mm = sem("o_mm"); o_copy = sem("o_copy"); o_sqr = sem("o_sqr")
        o_stat = sem("o_stat"); o_var = sem("o_var"); o_rstd = sem("o_rstd"); o_bc = sem("o_bc"); o_done = sem("o_done")
        dve_s = sem("dve_s"); pool_s = sem("pool_s")
        ld_wo = sem("ld_wo"); ld_keys = sem("ld_keys"); ld_wq = sem("ld_wq")
        spread = sem("spread"); rows_mm = sem("rows_mm"); rows_done = sem("rows_done")
        wo_mm = sem("wo_mm"); wo_gated = sem("wo_gated"); x1_done = sem("x1_done")
        ss2 = sem("ss2"); rv2 = sem("rv2"); rstd2 = sem("rstd2"); h2a = sem("h2a"); h2_done = sem("h2_done")
        h2T_mm = sem("h2T_mm"); h2T_done = sem("h2T_done"); keysT_mm = sem("keysT_mm"); keysT_done = sem("keysT_done")
        q_mm = sem("q_mm"); q_done = sem("q_done"); sc_mm = sem("sc_mm"); sc_done = sem("sc_done")
        best = sem("best"); neg_done = sem("neg_done"); g_exp = sem("g_exp"); math_s = sem("math_s")
        e_done = sem("e_done"); g_done = sem("g_done"); g_rec = sem("g_rec"); col_done = sem("col_done")
        ld_u = [sem(f"ld_u{n}") for n in range(U_SLOTS)]; ld_v = [sem(f"ld_v{n}") for n in range(V_SLOTS)]
        u_free = sem("u_free"); v_free = sem("v_free")
        gelu_done = sem("gelu_done"); w_done = sem("w_done"); diags = sem("diags")
        o_gated = sem("o_gated"); o_sum = sem("o_sum"); st_out = sem("st_out")
        masks_done = sem("masks_done"); v_fixed = sem("v_fixed"); vt_mm = sem("vt_mm"); vt_done = sem("vt_done")
        pair_w = sem("pair_w")
        mm = [sem(f"step_mm{d}") for d in range(2)]
        by_act = [sem(f"step_act{d}") for d in range(2)]
        by_dve = [sem(f"step_dve{d}") for d in range(2)]
        cum_done = sem("cum_done")
        exps = sem("exps")
        feat_v = sem("feat_v")
        feat_p = sem("feat_p")
        c_done = [sem(f"c_done{d}") for d in range(2)]
        kap = sem("kap")
        state_mm = sem("state_mm"); state_done = sem("state_done"); yst_mm = sem("yst_mm"); y_sum = sem("y_sum")
        mean_mm = sem("mean_mm"); centred = sem("centred"); y_sqr = sem("y_sqr"); y_stat = sem("y_stat"); y_var = sem("y_var")
        y_rstd = sem("y_rstd"); y_bc = sem("y_bc"); rk_done = sem("rk_done"); mod_part = [sem(f"mod_part{n}") for n in range(2)]; mod_sum = sem("mod_sum"); bon_mm = sem("bon_mm")
        bon_done = sem("bon_done"); gate_mm = sem("gate_mm"); rw_out = sem("rw_out")

        strips = [(ada_w, i * 256, 256) for i in range(8)]
        strips += [(w_in, RW0 + i * 256, 256 if i < 7 else 128) for i in range(8)]
        strips += [(w_in, 1024 + i * 256, 256) for i in range(2)]
        strips += [(w_in, i * 256, 256) for i in range(4)]
        strips += [(ada_w, 2048 + i * 256, 256) for i in range(16)]
        rw_blocks = [(8 + b // 2, P * (b % 2)) for b in range(15)]
        qk_blocks = [(18 + b // 2, P * (b % 2)) for b in range(8)]

        def strip(n):
            w = strips[n][2]
            flat = ring[:, 4 * (n % 4):4 * (n % 4) + 4, :].rearrange("p u n -> p (u n)")
            return flat[:, 0:KD * w].rearrange("p (k n) -> p k n", k=KD)

        def part_done(eng, u):
            if u % 4 == 0:
                eng.wait_ge(mod_part[0], u // 4 + 1)
            else:
                eng.wait_ge(mod_part[1], u - u // 4)

        def strip_read(eng, n):
            if n < 8:
                eng.wait_ge(w_used, n + 1)
            elif n < 16:
                eng.wait_ge(proj_mm, min(2 * (n - 8) + 2, 15))
            elif n < 18:
                eng.wait_ge(v_mm, NT)
            elif n < 22:
                eng.wait_ge(proj_mm, 15 + 2 * (n - 18) + 2)
            else:
                part_done(eng, n - 22)

        def rw_dest(b):
            return arena[:, b, :] if b < 12 else loT[:, b - 12, :]

        def cat(k):
            return attT[:, k, :] if k < 4 else YT[:, k - 4, :]

        UN = DA * NT
        x_rows = xr.rearrange("p u n -> p (u n)").rearrange("p (t d) -> p t d", t=NT)
        xs_rows = xs.rearrange("p u n -> p (u n)").rearrange("p (t d) -> p t d", t=NT)

        def bank_of(d, name):
            return 4 * d + 2 * (STEPS.index(name) % 2)

        CONSTS = 11
        RW_LOADS = 14 * 16

        block = ctx.enter_context(nc.Block())

        @block.sync
        def _(sp):
            sp.dma_start(c_col[:], c.rearrange("o (k p) -> p (o k)", p=P), allow_slow_non_contiguous=True).then_inc(ld_c, 16)

            def load_strip(n):
                src, c0, w = strips[n]
                if n >= 4:
                    strip_read(sp, n - 4)
                sp.dma_start(strip(n), src[:, c0:c0 + w].rearrange("(k p) n -> p k n", p=P)).then_inc(ld_w[n % 4], 16)

            for n in range(4):
                load_strip(n)
                sp.dma_start(x_rows[:, n, :], x[n * P:(n + 1) * P, :]).then_inc(ld_x[n], 16)
            for n in range(4, len(strips)):
                load_strip(n)
            for d in range(2):
                sp.wait_ge(mm[d], NB * len(STEPS))
                sp.wait_ge(by_dve[d], NB * len(DVE_STEPS))
                sp.wait_ge(by_act[d], NB * len(ACT_STEPS))
                sp.wait_ge(c_done[d], NB * 7)
            sp.dma_start(wo, w_out.rearrange("(k p) n -> p k n", p=P)).then_inc(ld_wo, 16)
            sp.wait_ge(rk_done, NB)
            for t in range(NT):
                sp.dma_start(x1[:, t, :], x[t * P:(t + 1) * P, :]).then_inc(ld_x[t], 16)
            sp.wait_ge(rw_out, NB)
            sp.dma_start(keys_raw, peer_keys.rearrange("b n d -> n b d")).then_inc(ld_keys, 16)
            sp.wait_ge(wo_mm, 2 * NT)
            for h in range(PH):
                if h > 0:
                    sp.wait_ge(q_mm, 2 * h)
                sp.dma_start(wq_strip, peer_wq[:, 256 * h:256 * (h + 1)].rearrange("(k p) n -> p k n", p=P)).then_inc(ld_wq, 16)
            for t in range(NT):
                sp.wait_ge(o_sum, 2 * (NT * (PH - 1) + t + 2))
                sp.dma_start(out[t * P:(t + 1) * P, :], x1[:, t, :]).then_inc(st_out, 16)
            sp.wait_ge(st_out, 16 * NT)

        @block.gpsimd
        def _(pool):
            slow = dict(allow_slow_non_contiguous=True)
            pool.dma_start(ada_bc[:], ada_b[0, 0:2048].rearrange("(j p) -> p j", p=P), **slow).then_inc(ld_par, 16)
            pool.dma_start(n1_col[:], norm1_g.rearrange("o (j p) -> p (o j)", p=P), **slow).then_inc(ld_par, 16)
            for d in range(2):
                pool.dma_start(mu[:, d, :], rw_shift_mu[0, d, :].rearrange("(j p) -> p j", p=P), **slow).then_inc(ld_mu, 16)
            for i, g in enumerate((da_qnorm_g, da_knorm_g)):
                for h in range(2):
                    pool.dma_start(qk_gain[HD * h:HD * h + HD, i:i + 1], g.rearrange("o d -> d o"), **slow).then_inc(ld_mu, 16)
            pool.memset(ident[:], 0.0).then_inc(zeroed, 1)
            pool.memset(sel[:], 0.0).then_inc(zeroed, 1)
            pool.memset(selT[:], 0.0).then_inc(zeroed, 1)
            pool.memset(half_ones[:], 0.0).then_inc(zeroed, 1)
            pool.memset(selh[:], 0.0).then_inc(zeroed, 1)
            pool.memset(selhT[:], 0.0).then_inc(zeroed, 1)
            pool.memset(qk_fold[:], 1.0).then_inc(zeroed, 1)
            pool.memset(restart[:], 1.0).then_inc(zeroed, 1)
            pool.memset(zero_w[:], 0.0).then_inc(zeroed, 1)
            pool.wait_ge(zeroed, 9)
            pool.affine_select(out=ident[:], in_=ident[:], compare_op=ALU.not_equal, fill=1.0, base=0,
                               pattern=[[-1, P]], channel_multiplier=1).then_inc(consts, 1)
            split = selT[:].rearrange("m b (h p) -> m b h p", h=2)
            pool.affine_select(out=split, in_=split, compare_op=ALU.not_equal, fill=1.0, base=0,
                               pattern=[[-2, 8], [-1, 2], [0, 64]], channel_multiplier=1).then_inc(consts, 1)
            pool.affine_select(out=selhT[:], in_=selhT[:], compare_op=ALU.not_equal, fill=1.0, base=0,
                               pattern=[[-1, DA], [0, P]], channel_multiplier=1).then_inc(consts, 1)
            pool.memset(ones[:], 1.0).then_inc(consts, 1)
            pool.memset(selh[:].rearrange("p h m -> p (h m)")[:, 0:DA * DA:DA + 1], 1.0).then_inc(consts, 1)
            pool.memset(qk_fold[0:8, :], 1.0 / HD).then_inc(consts, 1)
            pool.memset(restart[:, 0:S:CH], 0.0).then_inc(consts, 1)
            pool.iota(s_idx[:], [[0, CH]], base=0, channel_multiplier=1).then_inc(consts, 1)
            pool.iota(t_idx[:], [[1, CH]], base=0, channel_multiplier=0).then_inc(consts, 1)
            pool.iota(iota16i[:], [[1, TOPK]], base=0, channel_multiplier=0).then_inc(consts, 1)
            pool.iota(bias_h[:, 0, :], [[-1, 896]], base=384, channel_multiplier=1,
                      allow_small_or_imprecise_dtypes=True).then_inc(consts, 1)
            pool.dma_start(lam[:], da_lambda.rearrange("o a d -> o (a d)").to_broadcast([P, 4 * HD]), **slow).then_inc(ld_lam, 16)
            pool.dma_start(sub_g[:], da_subln_g.rearrange("o d -> d o"), **slow).then_inc(ld_lam, 16)
            for d in range(2):
                pool.dma_start(w0_col[:, d, :], rw_w0[0, d, :].rearrange("(j p) -> p j", p=P), **slow).then_inc(ld_rw, 16)
                pool.dma_start(a0_col[:, d, :], rw_a0[0, d, :].rearrange("(j p) -> p j", p=P), **slow).then_inc(ld_rw, 16)
            for col, src in ((kk_col, rw_k_k), (ka_col, rw_k_a), (lg_col, rw_ln_g), (lb_col, rw_ln_b),
                             (rk_col, rw_r_k.rearrange("o h d -> o (h d)"))):
                pool.dma_start(col[:], src.rearrange("o (j p) -> p (o j)", p=P), **slow).then_inc(ld_rw, 16)
            pool.dma_start(ada_bc2[:], ada_b[0, 2048:6144].rearrange("(j p) -> p j", p=P), **slow).then_inc(ld_rw, 16)
            pool.dma_start(n2_col[:], norm2_g.rearrange("o (j p) -> p (o j)", p=P), **slow).then_inc(ld_rw, 16)
            pool.dma_start(w2_sb[:], rw_w2.rearrange("o d r n -> (o d r) n")).then_inc(ld_rw, 16)
            pool.dma_start(a2_sb[:], rw_a2.rearrange("o d r n -> (o d r) n")).then_inc(ld_rw, 16)
            pool.dma_start(g2_sb[:], rw_g2.rearrange("o r n -> (o r) n")).then_inc(ld_rw, 16)


            step = Tally(pool, pool_s)
            pool.wait_ge(silu_done, 1)
            pool.wait_ge(xs_done, NT)
            for u in range(16):
                if u % 4 == 0:
                    continue
                n = 22 + u
                pool.wait_ge(ld_w[n % 4], 16 * (n // 4 + 1))
                w = strip(n)
                step.link(pool.tensor_tensor(w, w, silu_c[:].unsqueeze(2).to_broadcast([P, KD, 256]), ALU.mult))
                for half in (4, 2):
                    step.link(pool.tensor_tensor(w[:, 0:half, :], w[:, 0:half, :], w[:, half:2 * half, :], ALU.add))
                if u >= 8:
                    pool.wait_ge(mod_sum, u - 7)
                pool.tensor_tensor(mod_acc[:, u % 8, :], w[:, 0, :], w[:, 1, :], ALU.add).then_inc(mod_part[1], 1)

            pool.wait_ge(ld_rw, RW_LOADS)
            pool.wait_ge(masks_done, 1)
            pool.wait_ge(o_done, DA)
            with pool.Fori(0, NB) as i:
                for fixed, src in ((w2_pair, w2_sb), (a2_pair, a2_sb)):
                    pool.tensor_copy(fixed[:], src[:, bass.ds(i * P, P)]).then_inc(pair_w, 1)
                for d, r in enumerate(dirs):
                    pool.wait_ge(cum_done, 2 * i + d + 1)
                    pool.tensor_tensor(r.pexc, r.cum, r.sg, ALU.subtract).then_inc(feat_p, 1)
                    pool.wait_ge(by_act[d], upto(ACT_STEPS, "iclr", i))
                    pool.nop(nofuse=True)
                    pool.tensor_tensor(r.beta, pair_of(12, i), r.a, ALU.mult).then_inc(feat_p, 1)
                    pool.wait_ge(exps, 6 * i + 3 * d + 2)
                    pool.wait_ge(feat_p, 8 * i + 4 * d + 2)
                    pool.tensor_tensor(r.beta, r.beta, r.pinv, ALU.mult).then_inc(feat_p, 1)
                    pool.wait_ge(feat_v, 10 * i + 5 * d + 1)
                    pool.wait_ge(feat_p, 8 * i + 4 * d + 3)
                    pool.tensor_tensor(by_chunk(r.hat_b), by_chunk(r.beta), ptot[:, d, :].unsqueeze(2).to_broadcast([P, NC, CH]),
                                       ALU.mult).then_inc(feat_p, 1)
                for k in range(LEVELS):
                    for d, r in enumerate(dirs):
                        pool.wait_ge(by_dve[d], upto(DVE_STEPS, "gram_b", i) if k < 2 else upto(DVE_STEPS, "xt0", i))
                        if k >= 3:
                            pool.wait_ge(mm[d], upto(STEPS, f"w{k - 2}", i))
                        pool.tensor_tensor(r.c[k % 2], r.la[:, :, 0:CH],
                                           level[:, d, k, :].unsqueeze(1).to_broadcast([P, NC, CH]), ALU.mult).then_inc(c_done[d], 1)
                for d, r in enumerate(dirs):
                    pool.wait_ge(mm[d], upto(STEPS, "w4", i))
                    pool.tensor_tensor(r.dg, eye[:].unsqueeze(1).to_broadcast([P, NC, CH]),
                                       ptot[:, d, :].unsqueeze(2).to_broadcast([P, NC, CH]), ALU.mult).then_inc(c_done[d], 1)
                for d in range(2):
                    pool.wait_ge(mm[d], (i + 1) * len(STEPS))
                    pool.wait_ge(by_dve[d], (i + 1) * len(DVE_STEPS))
                    pool.wait_ge(by_act[d], (i + 1) * len(ACT_STEPS))


            pool.wait_ge(e_done, 1)
            pool.memset(w16[:], 0.0).then_inc(v_free, V_SLOTS)
            pool.memset(act16[:], 0.0).then_inc(u_free, U_SLOTS)
            pool.tensor_copy(idx_col[:, 0:1], e_idx[:, 0:1]).then_inc(col_done, 1)
            with pool.Fori(0, UNITS) as u:
                for s in range(TOPK):
                    pool.wait_ge(col_done, u * TOPK + (s + 1))
                    pool.wait_ge(u_free, u * TOPK + (s + 1))
                    pool.wait_ge(v_free, u * TOPK + (s + 1))
                    if s == TOPK - 1:
                        pool.wait_ge(e_done, u + 2)
                    nxt = (s + 1) % TOPK
                    pool.tensor_copy(idx_col[:, nxt:nxt + 1], e_idx[:, bass.ds(u * TOPK + (s + 1), 1)]).then_inc(col_done, 1)
                    pool.indirect_dma_start(u_ring[:, s % U_SLOTS, :], None, peer_u,
                                            bass.IndirectOffsetOnAxis(idx_col[:, s:s + 1], 0)).then_inc(ld_u[s % U_SLOTS], 16)
                    pool.indirect_dma_start(v_ring[:, s % V_SLOTS, :], None, peer_v,
                                            bass.IndirectOffsetOnAxis(idx_col[:, s:s + 1], 0)).then_inc(ld_v[s % V_SLOTS], 16)

        @block.scalar
        def _(act):
            act.wait_ge(ld_c, 16)
            nc.scalar.activation(silu_c[:], c_col[:], ACT.Silu).then_inc(silu_done, 1)
            for t in range(NT):
                act.wait_ge(ld_x[t], 16)
                nc.scalar.activation(xs_rows[:, t, :], x_rows[:, t, :], ACT.Square, accum_out=sumsq[:, t:t + 1]).then_inc(ss_done, 1)
            act.wait_ge(rv_done, 1)
            nc.scalar.activation(rstd[:], rstd[:], ACT.Sqrt).then_inc(rstd_done, 1)
            act.wait_ge(mod1_done, 1)
            for j in range(KD):
                act.wait_ge(xT_mm, j + 1)
                nc.scalar.activation(hT[:, j, :], ps[:, j % 4, :], ACT.Identity, bias=mod1[:, j:j + 1],
                                     scale=mod1[:, 8 + j:9 + j]).then_inc(hT_done, 1)
            act.wait_ge(mu_done, 1)
            for b in range(15):
                act.wait_ge(proj_mm, b + 1)
                nc.scalar.activation(rw_dest(b), ps[:, b % 4, :], ACT.Copy, scale=mu_self[:, b:b + 1]).then_inc(proj_a, 1)
            for t in range(NT):
                act.wait_ge(v_mm, t + 1)
                nc.scalar.activation(vA[:, t, :], ps[:, 4 + t, :], ACT.Copy).then_inc(v_done, 1)
            for b in range(8):
                act.wait_ge(proj_mm, 16 + b)
                if b >= 2:
                    act.wait_ge(qk_stat, b - 1)
                nc.scalar.activation(sq[:, b % 2, :], ps[:, (15 + b) % 4, :], ACT.Square).then_inc(qk_sqr, 1)
            for b in range(NB):
                act.wait_ge(kk_raw, b + 1)
                if b < 2:
                    act.wait_ge(qk_stat, 7 + b)
                else:
                    act.wait_ge(kk_stat, b - 1)
                nc.scalar.activation(sq[:, b % 2, :], kkT[:, b, :], ACT.Square).then_inc(kk_sqr, 1)
            act.wait_ge(qk_var, 1)
            nc.scalar.activation(stat[0:16, :], stat[0:16, :], ACT.Sqrt, scale=qk_fold[:, 0:1]).then_inc(qk_rstd, 1)
            act.wait_ge(kk_stat, NB)
            nc.scalar.activation(stat_kk, ps[0:8, 5, :], ACT.Sqrt).then_inc(kk_norm, 1)
            act.wait_ge(proj_v, 15)
            nc.scalar.activation(loT[:, 0, :], loT[:, 0, :], ACT.Tanh).then_inc(lo_done, 1)
            nc.scalar.activation(loT[:, 2, :], loT[:, 2, :], ACT.Sigmoid).then_inc(lo_done, 1)
            act.wait_ge(lam_sum, 1)
            nc.scalar.activation(lam_e[:], lam_e[:], ACT.Exp).then_inc(lam_exp, 1)

            def evacuate(u):
                act.wait_ge(mixT_mm, u + 1)
                if u >= 2:
                    act.wait_ge(o_mm, u - 1)
                nc.scalar.activation(mixT[:, u % 2, :], ps[:, 4 + u % 2, :], ACT.Copy).then_inc(mixT_done, 1)

            def head_out(h):
                act.wait_ge(o_mm, NT * (h + 1))
                bank = ps[:, 6, :]
                nc.scalar.activation(sq_o[:, h, :], bank, ACT.Square).then_inc(o_sqr, 1)
                nc.scalar.activation(attT[:, h, :], bank, ACT.Copy, scale=sub_g[:, 0:1]).then_inc(o_copy, 1)

            act.wait_ge(ld_lam, 32)
            for u in range(UN):
                act.wait_ge(s_max, u + 1)
                for cmp in range(2):
                    pr = probs[:, 2 * (u % 2) + cmp, :]
                    nc.scalar.activation(pr, pr, ACT.Exp, bias=nmx[:, u % 2, cmp:cmp + 1],
                                         accum_out=den[:, u % 2, cmp:cmp + 1]).then_inc(s_exp, 1)
                if u % NT == 1 and u >= NT:
                    head_out(u // NT - 1)
                if u >= 1:
                    evacuate(u - 1)
            evacuate(UN - 1)
            head_out(DA - 1)
            act.wait_ge(o_var, 1)
            nc.scalar.activation(stat_o, stat_o, ACT.Sqrt, scale=(1.0 - LAMBDA0) ** 2).then_inc(o_rstd, 1)


            act.wait_ge(ld_rw, RW_LOADS)
            act.wait_ge(o_done, DA)
            with act.Fori(0, NB) as i:
                nc.scalar.activation(v_fix, pair_of(8, i), ACT.Copy).then_inc(v_fixed, 1)
                for d, r in enumerate(dirs):
                    act.wait_ge(mm[d], upto(STEPS, "decay", i))
                    nc.scalar.activation(r.sg, ps[:, 4 * d, :], ACT.Sigmoid, bias=w0_col[:, d, bass.ds(i, 1)]).then_inc(by_act[d], 1)
                    act.wait_ge(mm[d], upto(STEPS, "iclr", i))
                    nc.scalar.activation(r.a, ps[:, 4 * d + 2, :], ACT.Sigmoid, bias=a0_col[:, d, bass.ds(i, 1)]).then_inc(by_act[d], 1)
                act.wait_ge(vt_mm, i + 1)
                nc.scalar.activation(vt_u[:, 0, :], ps[:, 7, :], ACT.Copy).then_inc(vt_done, 1)
                for d, r in enumerate(dirs):
                    act.wait_ge(cum_done, 2 * i + d + 1)
                    nc.scalar.activation(r.pinc, r.cum, ACT.Exp, scale=-DECAY).then_inc(exps, 1)
                    nc.scalar.activation(r.pinv, r.cum, ACT.Exp, scale=DECAY).then_inc(exps, 1)
                    act.wait_ge(feat_p, 8 * i + 4 * d + 1)
                    nc.scalar.activation(r.pexc, r.pexc, ACT.Exp, scale=-DECAY).then_inc(exps, 1)

                def take(name, dst, scale=1.0, width=1):
                    for d, r in enumerate(dirs):
                        b = bank_of(d, name)
                        act.wait_ge(mm[d], upto(STEPS, name, i))
                        src = ps[:, b:b + width, :].rearrange("p b n -> p (b n)").rearrange("p (c n) -> p c n", c=NC)
                        nc.scalar.activation(dst(d, r), src, ACT.Copy, scale=scale).then_inc(by_act[d], 1)

                take("alpha_t", lambda d, r: r.rhs[:, :, 0:CH])
                take("beta_t", lambda d, r: r.beta_t)
                take("kappa_t", lambda d, r: r.kappa_t)
                take("mv", lambda d, r: r.rhs[:, :, CH:2 * CH])
                for k in range(1, LEVELS):
                    take(f"w{k}", lambda d, r: r.w)
                take("gh", lambda d, r: r.gh, scale=-1.0, width=2)
                for d, r in enumerate(dirs):
                    act.wait_ge(mm[d], upto(STEPS, "psi", i))
                    nc.scalar.activation(odd_even(pair_of(31 + d, i * 2)), feature_banks(bank_of(d, "psi")), ACT.Copy).then_inc(by_act[d], 1)
                for d in range(2):
                    act.wait_ge(mm[d], (i + 1) * len(STEPS))
                    act.wait_ge(by_dve[d], (i + 1) * len(DVE_STEPS))
            for b in range(NB):
                act.wait_ge(centred, b + 1)
                nc.scalar.activation(tmp2[:, b, :], YT[:, b, :], ACT.Square).then_inc(y_sqr, 1)
            act.wait_ge(y_var, 1)
            nc.scalar.activation(stat_y, stat_y, ACT.Sqrt).then_inc(y_rstd, 1)

            act.wait_ge(bon_done, NB)
            for g in range(8):
                act.wait_ge(rows_mm, g + 1)
                nc.scalar.activation(mod_rows.rearrange("p m d -> p (m d)")[:, 512 * g:512 * g + 512], ps[:, g % 2, :], ACT.Copy).then_inc(rows_done, 1)
            def take_h2T(t):
                for m in (2 * t, 2 * t + 1):
                    act.wait_ge(h2T_mm, m + 1)
                    nc.scalar.activation(h2T[:, 4 * (m % 2):4 * (m % 2) + 4, t * P:(t + 1) * P],
                                         ps[:, 6 + m % 2, :].rearrange("p (j n) -> p j n", j=4), ACT.Copy).then_inc(h2T_done, 1)

            for t in range(NT):
                act.wait_ge(x1_done, 2 * t + 2)
                nc.scalar.activation(h2[:, t, :], x1[:, t, :], ACT.Square, accum_out=sumsq[:, t:t + 1]).then_inc(ss2, 1)
                act.wait_ge(rv2, t + 1)
                nc.scalar.activation(rstd[:, t:t + 1], rstd[:, t:t + 1], ACT.Sqrt).then_inc(rstd2, 1)
            for g in range(4):
                act.wait_ge(keysT_mm, g + 1)
                nc.scalar.activation(keysT[:, 4 * g:4 * g + 4, :].rearrange("p b n -> p (b n)"), ps[:, g % 2, :], ACT.Copy).then_inc(keysT_done, 1)
            for t in range(NT):
                take_h2T(t)

            def take_query(h, a):
                act.wait_ge(q_mm, h * 2 + (a + 1))
                nc.scalar.activation(qT[:, a, :], ps[:, 4 + a, :], ACT.Copy).then_inc(q_done, 1)

            def take_scores(h, a):
                act.wait_ge(sc_mm, h * 2 + (a + 1))
                nc.scalar.activation(scores[:, :, a, :], ps[:, 6 + a, :].rearrange("p (t n) -> p t n", t=NT), ACT.Copy).then_inc(sc_done, 1)

            def gate_exp(u):
                act.wait_ge(neg_done, u + 1)
                nc.scalar.activation(g_exp_t[:], top[:, 2, :], ACT.Exp, bias=neg_top[:, 0:1], accum_out=g_den[:]).then_inc(g_exp, 1)

            def expert_turn(h, t, last_head):
                u = h * NT + t
                for g in range(4):
                    act.wait_ge(u_free, u * TOPK + (U_SLOTS + 4 * g + 4))
                    nc.scalar.activation(gelu16[:, 4 * g:4 * g + 4], act16[:, 4 * g:4 * g + 4], ACT.Gelu).then_inc(gelu_done, 1)
                    if g == 1 and not (last_head and t >= 2):
                        gate_exp(u + 2)
                    act.wait_ge(w_done, u * 4 + (g + 1))
                    for s in range(4 * g, 4 * g + 4):
                        act.wait_ge(v_free, u * TOPK + (s + 1))
                        nc.scalar.activation(diag[:, s % V_SLOTS, :], ident[:], ACT.Copy, scale=w16[:, s:s + 1]).then_inc(diags, 1)
                    if not last_head:
                        if t < 2 and g == 1:
                            take_query(h + 1, t)
                        if t == 1 and g == 3:
                            act.wait_ge(best, h * (NT * CHOICE_OPS) + NT * CHOICE_OPS)
                            take_scores(h + 1, 0)
                        if t == 2 and g == 0:
                            take_scores(h + 1, 1)

            for a in range(2):
                take_query(0, a)
            for a in range(2):
                take_scores(0, a)
            for u in range(2):
                gate_exp(u)
            with act.Fori(0, PH - 1) as h:
                for t in range(NT):
                    expert_turn(h, t, False)
            for t in range(NT):
                expert_turn(PH - 1, t, True)

        @block.tensor
        def _(pe):
            pe.wait_ge(silu_done, 1)
            for n in range(8):
                pe.wait_ge(ld_w[n % 4], 16 * (n // 4 + 1))
                w = strip(n)
                for h in range(2):
                    for k in range(KD):
                        last = nc.tensor.matmul(ps[:, 7, 2 * n + h:2 * n + h + 1], w[:, k, h * P:(h + 1) * P],
                                                silu_c[:, k:k + 1], start=(k == 0), stop=(k == KD - 1))
                last.then_inc(w_used, 1)
            pe.wait_ge(consts, CONSTS)
            pe.wait_ge(xs_done, NT)
            for j in range(KD):
                if j >= 4:
                    pe.wait_ge(hT_done, j - 3)
                for t in range(NT):
                    last = nc.tensor.transpose(ps[:, j % 4, t * P:(t + 1) * P], xs_rows[:, t, j * P:(j + 1) * P], ident[:])
                last.then_inc(xT_mm, 1)

            pe.wait_ge(hT_done, KD)

            def project(b, n, col):
                if col == 0:
                    pe.wait_ge(ld_w[n % 4], 16 * (n // 4 + 1))
                if b >= 4:
                    pe.wait_ge(proj_v, b - 3)
                w = strip(n)
                for k in range(KD):
                    last = nc.tensor.matmul(ps[:, b % 4, :], w[:, k, col:col + P], hT[:, k, :],
                                            start=(k == 0), stop=(k == KD - 1))
                last.then_inc(proj_mm, 1)

            pe.wait_ge(sel_done, 4)

            def qk_statistics(b):
                pe.wait_ge(qk_sqr, b + 1)
                nc.tensor.matmul(ps[0:16, 4, :], sel[:, b, :], sq[:, b % 2, :], start=(b == 0), stop=(b == 7)).then_inc(qk_stat, 1)

            for b, (n, col) in enumerate(rw_blocks):
                project(b, n, col)
            for n in (16, 17):
                pe.wait_ge(ld_w[n % 4], 16 * (n // 4 + 1))
            for t in range(NT):
                for i in range(2):
                    for k in range(KD):
                        last = nc.tensor.matmul(ps[:, 4 + t, 256 * i:256 * i + 256], hT[:, k, t * P:(t + 1) * P],
                                                strip(16 + i)[:, k, :], start=(k == 0), stop=(k == KD - 1))
                last.then_inc(v_mm, 1)
            pe.wait_ge(v_done, NT)
            for b, (n, col) in enumerate(qk_blocks):
                project(15 + b, n, col)
                if b >= 1:
                    qk_statistics(b - 1)
            qk_statistics(7)
            for b in range(NB):
                pe.wait_ge(kk_sqr, b + 1)
                nc.tensor.matmul(ps[0:8, 5, :], sel[:, b, 0:8], sq[:, b % 2, :], start=(b == 0), stop=(b == NB - 1)).then_inc(kk_stat, 1)
            pe.wait_ge(proj_v, 23)
            pe.wait_ge(qk_rstd, 1)
            for b in range(8):
                if b >= 4:
                    pe.wait_ge(qk_done, b - 3)
                nc.tensor.matmul(ps[:, b % 4, :], selT[:, b, :], stat[:], start=True, stop=True).then_inc(qk_bc, 1)
            pe.wait_ge(kk_inv, 1)
            for b in range(NB):
                pe.wait_ge(qk_done, b + 5)
                nc.tensor.matmul(ps[:, b, :], selT[0:8, b, :], stat_kk, start=True, stop=True).then_inc(kk_bc, 1)

            def scores(u):
                h, qt = u // NT, u % NT
                if u < 2:
                    pe.wait_ge(kk_done, NB)
                else:
                    pe.wait_ge(s_max, u - 1)
                for cmp in range(2):
                    r = slice(HD * cmp, HD * cmp + HD)
                    last = nc.tensor.matmul(ps[:, 2 * (u % 2) + cmp, :], qkT[r, h, qt * P:(qt + 1) * P], qkT[r, DA + h, :],
                                            start=True, stop=True)
                last.then_inc(s_mm, 1)

            def transpose_mix(u):
                pe.wait_ge(mixed, u + 1)
                if u >= 2:
                    pe.wait_ge(mixT_done, u - 1)
                for kt in range(NT):
                    last = nc.tensor.transpose(ps[:, 4 + u % 2, kt * P:(kt + 1) * P], mix[:, u % 2, kt * P:(kt + 1) * P], ident[:])
                last.then_inc(mixT_mm, 1)

            def values(u):
                h, qt = u // NT, u % NT
                pe.wait_ge(mixT_done, u + 1)
                if h >= 1 and qt == 0:
                    pe.wait_ge(o_copy, h)
                for kt in range(NT):
                    last = nc.tensor.matmul(ps[:, 6, qt * P:(qt + 1) * P], vA[:, kt, h * P:(h + 1) * P],
                                            mixT[:, u % 2, kt * P:(kt + 1) * P], start=(kt == 0), stop=(kt == NT - 1))
                last.then_inc(o_mm, 1)

            def second_modulation(u):
                part_done(pe, u)
                for half in range(2):
                    last = nc.tensor.matmul(ps[:, 7, 2 * u + half:2 * u + half + 1], mod_acc[:, u % 8, half * P:(half + 1) * P],
                                            ones[:, 0:1], start=True, stop=True)
                last.then_inc(mod_sum, 1)

            scores(0)
            scores(1)
            for u in range(UN):
                transpose_mix(u)
                if u + 2 < UN:
                    scores(u + 2)
                if u >= 1:
                    values(u - 1)
                second_modulation(u)
            values(UN - 1)
            pe.wait_ge(o_copy, DA)
            pe.wait_ge(s_max, UN)
            for h in range(DA):
                last = nc.tensor.matmul(ps[0:DA, 0, :], selh[:, h, :], sq_o[:, h, :], start=(h == 0), stop=(h == DA - 1))
            last.then_inc(o_stat, 1)
            pe.wait_ge(o_rstd, 1)
            for h in range(DA):
                nc.tensor.matmul(ps[:, 1 + h, :], selhT[:, h, :], stat_o, start=True, stop=True).then_inc(o_bc, 1)


            def place(major, ch, h):
                half, block = (h, ch) if major == "features" else (ch % 2, NC // 2 * h + ch // 2)
                return slice(HD * half, HD * half + HD), block

            def each(d, name, source, result, *terms):
                b0 = bank_of(d, name)
                pe.nop(nofuse=True)
                apart = [[(0, 0), (0, 1)], [(1, 0), (1, 1)]] if source == result else [[(0, 0), (1, 1)], [(0, 1), (1, 0)]]
                for ch2 in range(0, NC, 2):
                    for two in apart:
                        for n, (lhs, rhs) in enumerate(terms):
                            for h, odd in two:
                                r, block = place(source, ch2 + odd, h)
                                o, o_block = place(result, ch2 + odd, h)
                                right = rhs(r, block)
                                w = right.shape[-1] * (2 if len(right.shape) == 3 else 1)
                                col = o_block * w if result == T else 512 * odd + ch2 // 2 * w
                                into = ps[o, b0 + col // 512, col % 512:col % 512 + w]
                                if len(right.shape) == 3:
                                    into = into.rearrange("p (a n) -> p a n", a=2)
                                last = nc.tensor.matmul(into, lhs(r, block), right,
                                                        start=(n == 0), stop=(n == len(terms) - 1))
                return last

            def turned(bank, rows):
                for ch2 in range(NC // 2):
                    last = nc.tensor.transpose(by_head(ps[:, bank, :], ch2), rows[:, ch2 * P:(ch2 + 1) * P], ident[:])
                return last

            def by_head(bank, ch2):
                return bank.rearrange("p (h c n) -> p h c n", h=2, c=NC // 2)[:, :, ch2, :]

            def at(ap, c0=0, w=CH):
                return lambda r, block: ap[r, block, c0:c0 + w]

            def both(ap):
                return lambda r, block: ap[r, :, block * CH:(block + 1) * CH]

            F, T = "features", "tokens"
            pe.wait_ge(o_done, DA)
            pe.wait_ge(lo_done, 2)
            pe.wait_ge(masks_done, 1)
            with pe.Fori(0, NB) as i:
                pe.wait_ge(pair_w, 2 * i + 2)
                for name, w, slot in (("decay", w2_pair, 0), ("iclr", a2_pair, 1)):
                    for d in range(2):
                        r = slice(HD * d, HD * d + HD)
                        nc.tensor.matmul(ps[:, bank_of(d, name), :], w[r, :], loT[r, slot, :], start=True, stop=True).then_inc(mm[d], 1)
                pe.wait_ge(v_fixed, i + 1)
                turned(7, v_fix).then_inc(vt_mm, 1)
                for d, r in enumerate(dirs):
                    pe.wait_ge(feat_v, 10 * i + 5 * d + 3)
                    pe.wait_ge(by_act[d], upto(ACT_STEPS, "decay", i))
                    turned(bank_of(d, "alpha_t"), r.alpha).then_inc(mm[d], 1)
                for d, r in enumerate(dirs):
                    pe.wait_ge(feat_p, 8 * i + 4 * d + 4)
                    turned(bank_of(d, "beta_t"), r.hat_b).then_inc(mm[d], 1)
                for d, r in enumerate(dirs):
                    pe.wait_ge(feat_v, 10 * i + 5 * d + 5)
                    pe.wait_ge(by_act[d], upto(ACT_STEPS, "alpha_t", i))
                    turned(bank_of(d, "kappa_t"), r.hat_k).then_inc(mm[d], 1)
                pe.wait_ge(vt_done, i + 1)
                for d, r in enumerate(dirs):
                    pe.wait_ge(by_act[d], upto(ACT_STEPS, "beta_t", i))
                    each(d, "gram_b", F, T, (at(by_chunk(r.beta)), both(r.ar))).then_inc(mm[d], 1)
                for d, r in enumerate(dirs):
                    pe.wait_ge(by_act[d], upto(ACT_STEPS, "kappa_t", i))
                    each(d, "gram_k", F, T, (at(by_chunk(r.kappa)), both(r.ar))).then_inc(mm[d], 1)
                for d, r in enumerate(dirs):
                    pe.wait_ge(by_dve[d], upto(DVE_STEPS, "gram_k", i))
                    each(d, "mv", T, T, (at(r.mb), at(v_t))).then_inc(mm[d], 1)
                for k in range(1, LEVELS):
                    for d, r in enumerate(dirs):
                        pe.wait_ge(c_done[d], 7 * i + 1 + k)
                        pe.wait_ge(by_dve[d], upto(DVE_STEPS, f"x{k - 1}", i))
                        pe.wait_ge(by_act[d], upto(ACT_STEPS, f"w{k - 1}" if k > 1 else "mv", i))
                        each(d, f"w{k}", T, T, (at(r.c[k % 2]), at(r.x))).then_inc(mm[d], 1)
                    for d, r in enumerate(dirs):
                        pe.wait_ge(by_dve[d], upto(DVE_STEPS, f"xt{k - 1}", i))
                        pe.wait_ge(by_act[d], upto(ACT_STEPS, f"w{k}", i))
                        if k < LEVELS - 1:
                            each(d, f"x{k}", T, T, (at(r.xt), at(r.w))).then_inc(mm[d], 1)
                        else:
                            each(d, f"xt{k}", T, T, (at(r.w), at(r.xt))).then_inc(mm[d], 1)
                for d, r in enumerate(dirs):
                    pe.wait_ge(by_dve[d], upto(DVE_STEPS, f"xt{LEVELS - 1}", i))
                    each(d, "gh", T, T, (at(r.xt), at(r.rhs, 0, 2 * CH))).then_inc(mm[d], 1)
                for d, r in enumerate(dirs):
                    pe.wait_ge(by_act[d], upto(ACT_STEPS, "gh", i))
                    each(d, "phi", T, F, (at(r.gh), at(r.beta_t))).then_inc(mm[d], 1)
                for d, r in enumerate(dirs):
                    each(d, "psi", T, F, (at(r.kappa_t), at(v_t)), (at(r.beta_t), at(r.gh, CH))).then_inc(mm[d], 1)
                for d, r in enumerate(dirs):
                    pe.wait_ge(by_dve[d], upto(DVE_STEPS, "phi", i))
                    each(d, "rho", T, F, (at(r.gh), at(r.la, CH))).then_inc(mm[d], 1)
                for d, r in enumerate(dirs):
                    pe.wait_ge(by_act[d], upto(ACT_STEPS, "psi", i))
                    each(d, "y", T, F, (at(v_t), at(r.mb, CH)), (at(r.gh, CH), at(r.la, CH))).then_inc(mm[d], 1)
                for d in range(2):
                    pe.wait_ge(by_dve[d], (i + 1) * len(DVE_STEPS))
                    pe.wait_ge(by_act[d], (i + 1) * len(ACT_STEPS))
            for st in range(1, NC - 1):
                pe.wait_ge(state_done, 2 * st)
                for q in range(2 * NB):
                    ch = st if q % 2 == 0 else NC - 1 - st
                    for h in range(2):
                        r = slice(HD * h, HD * h + HD)
                        last = nc.tensor.matmul(ps[r, st % 2, q * CH:(q + 1) * CH], PHI[r, q, ch * CH:(ch + 1) * CH],
                                                states[r, st, q * CH:(q + 1) * CH], start=True, stop=True)
                last.then_inc(state_mm, 1)
            pe.wait_ge(state_done, 2 * (NC - 1))
            for b in range(NB):
                for ch in range(NC):
                    terms = [(q, st) for q, st in ((2 * b, ch), (2 * b + 1, NC - 1 - ch)) if st > 0]
                    for n, (q, st) in enumerate(terms):
                        for h in range(2):
                            r = slice(HD * h, HD * h + HD)
                            last = nc.tensor.matmul(ps[r, 2 + b, ch * CH:(ch + 1) * CH], states[r, st, q * CH:(q + 1) * CH],
                                                    RP[r, q, ch * CH:(ch + 1) * CH], start=(n == 0), stop=(n == len(terms) - 1))
                last.then_inc(yst_mm, 1)
            for b in range(NB):
                pe.wait_ge(y_sum, b + 1)
                nc.tensor.matmul(ps[:, 2 + b, :], half_ones[:], YT[:, b, :], start=True, stop=True).then_inc(mean_mm, 1)
            for b in range(NB):
                pe.wait_ge(y_sqr, b + 1)
                last = nc.tensor.matmul(ps[0:8, 0, :], sel[:, b, 0:8], tmp2[:, b, :], start=(b == 0), stop=(b == NB - 1))
            last.then_inc(y_stat, 1)
            for b in range(NB):
                pe.wait_ge(rk_done, b + 1)
                if b >= 2:
                    pe.wait_ge(bon_done, b - 1)
                nc.tensor.matmul(ps[:, 6 + b % 2, :], half_ones[:], tmp[:, b, :], start=True, stop=True).then_inc(bon_mm, 1)
            pe.wait_ge(centred, NB)
            for b in range(NB):
                if b == 0:
                    pe.wait_ge(y_rstd, 1)
                nc.tensor.matmul(ps[:, 2 + b, :], selT[0:8, b, :], stat_y, start=True, stop=True).then_inc(y_bc, 1)
            for b in range(NB):
                if b < 2:
                    pe.wait_ge(bon_done, NB - 1 + b)
                else:
                    pe.wait_ge(rw_out, b - 1)
                nc.tensor.matmul(ps[:, 6 + b % 2, :], g2_sb[:, b * P:(b + 1) * P], loT[:, 2, :], start=True, stop=True).then_inc(gate_mm, 1)

            for g in range(8):
                pe.wait_ge(spread, g + 1)
                if g >= 2:
                    pe.wait_ge(rows_done, g - 1)
                nc.tensor.matmul(ps[:, g % 2, :], ones[:], col_diag[:, g, :], start=True, stop=True).then_inc(rows_mm, 1)
            pe.wait_ge(rw_out, NB)
            def turn_h2(t):
                pe.wait_ge(h2_done, t + 1)
                for m in (2 * t, 2 * t + 1):
                    if m >= 2:
                        pe.wait_ge(h2T_done, m - 1)
                    for j in range(4):
                        c0 = (4 * (m % 2) + j) * P
                        last = nc.tensor.transpose(ps[:, 6 + m % 2, j * P:(j + 1) * P], h2[:, t, c0:c0 + P], ident[:])
                    last.then_inc(h2T_mm, 1)

            pe.wait_ge(ld_wo, 16)
            for t in range(NT):
                for n in range(2):
                    if 2 * t + n >= 4:
                        pe.wait_ge(wo_gated, 2 * t + n - 3)
                    for k in range(KD):
                        last = nc.tensor.matmul(ps[:, 2 + (2 * t + n) % 4, :], cat(k)[:, t * P:(t + 1) * P], wo[:, k, n * 512:(n + 1) * 512],
                                                start=(k == 0), stop=(k == KD - 1))
                    last.then_inc(wo_mm, 1)
            pe.wait_ge(ld_keys, 16)
            pe.wait_ge(rows_done, 8)
            for g in range(4):
                if g >= 2:
                    pe.wait_ge(keysT_done, g - 1)
                for b in range(4):
                    last = nc.tensor.transpose(ps[:, g % 2, b * P:(b + 1) * P], keys_raw[:, 4 * g + b, :], ident[:])
                last.then_inc(keysT_mm, 1)
            for t in range(NT):
                turn_h2(t)
            pe.wait_ge(keysT_done, 4)
            pe.wait_ge(h2T_done, 2 * NT)

            def query(h, a):
                if a == 0:
                    pe.wait_ge(ld_wq, h * 16 + 16)
                for k in range(KD):
                    last = nc.tensor.matmul(ps[:, 4 + a, :], wq_strip[:, k, a * P:(a + 1) * P], h2T[:, k, :], start=(k == 0), stop=(k == KD - 1))
                last.then_inc(q_mm, 1)

            def key_scores(h, a):
                pe.wait_ge(q_done, h * 2 + (a + 1))
                for t in range(NT):
                    keys = keysT[:, bass.ds(h * 2 + a, 1), :].rearrange("p b n -> p (b n)")
                    last = nc.tensor.matmul(ps[:, 6 + a, t * P:(t + 1) * P], qT[:, a, t * P:(t + 1) * P], keys, start=True, stop=True)
                last.then_inc(sc_mm, 1)

            def expert_turn(h, t, last_head):
                if not last_head:
                    if t == 1:
                        key_scores(h + 1, 0)
                    if t < 2:
                        query(h + 1, t)
                    if t == 2:
                        key_scores(h + 1, 1)
                u = h * NT + t
                if t >= 1:
                    pe.wait_ge(o_gated, u * 2)
                for s in range(TOPK):
                    pe.wait_ge(diags, u * TOPK + (s + 1))
                    pe.wait_ge(ld_v[s % V_SLOTS], u * 32 + 16 * (s // V_SLOTS + 1))
                    for n in range(2):
                        last = nc.tensor.matmul(ps[:, 2 * (t % 2) + n, :], diag[:, s % V_SLOTS, :], v_ring[:, s % V_SLOTS, n * 512:(n + 1) * 512],
                                                start=(s == 0), stop=(s == TOPK - 1))
                    last.then_inc(v_free, 1)
                if t == NT - 1 and not last_head:
                    pe.wait_ge(o_gated, h * (2 * NT) + 2 * NT)

            for n in range(2):
                nc.tensor.matmul(ps[:, 2 + n, :], zero_w[0:1, :], restart[0:1, :], start=True, stop=True)
            for a in range(2):
                query(0, a)
            for a in range(2):
                key_scores(0, a)
            with pe.Fori(0, PH - 1) as h:
                for t in range(NT):
                    expert_turn(h, t, False)
            for t in range(NT):
                expert_turn(PH - 1, t, True)

        @block.vector
        def _(dve):
            step = Tally(dve, dve_s)
            v = nc.vector
            dve.wait_ge(zeroed, 8)
            sel_flat = sel[:].rearrange("p b m -> p (b m)")
            for h in range(2):
                v.memset(sel_flat[HD * h:HD * h + HD, h:h + 127:18], 1.0).then_inc(sel_done, 1)
                v.memset(half_ones[HD * h:HD * h + HD, HD * h:HD * h + HD], 1.0).then_inc(sel_done, 1)
            dve.wait_ge(consts, CONSTS)
            step.link(v.scalar_tensor_tensor(bias_h[:, 0, :], bias_h[:, 0, :], -1.0, bias_h[:, 0, :], ALU.mult, ALU.min))
            for h in (3, 2, 1, 0):
                v.tensor_scalar(bias_h[:, h, :], bias_h[:, 0, :], 2.0 ** (-8.0 * (h + 1) / DA), None, ALU.mult).then_inc(bias_done, 1)
            step.link(v.tensor_scalar(s_idx[:], s_idx[:], CH - 1, None, ALU.bitwise_and))
            step(v.tensor_tensor(xor_idx[:], s_idx[:], t_idx[:], ALU.bitwise_xor))
            step(v.tensor_tensor(tri[:, 0, 0, :], s_idx[:], t_idx[:], ALU.is_lt))
            step(v.tensor_tensor(tri[:, 1, 0, :], s_idx[:], t_idx[:], ALU.is_gt))
            step(v.tensor_tensor(tri[:, 0, 1, :], s_idx[:], t_idx[:], ALU.is_le))
            step(v.tensor_tensor(tri[:, 1, 1, :], s_idx[:], t_idx[:], ALU.is_gt))
            step.link(v.tensor_tensor(eye[:], s_idx[:], t_idx[:], ALU.is_equal))
            for k in range(LEVELS):
                step.link(v.tensor_scalar(level[:, 1, k, :], xor_idx[:], float(2 ** k), None, ALU.is_ge))
                step.link(v.scalar_tensor_tensor(level[:, 1, k, :], xor_idx[:], float(2 ** (k + 1)), level[:, 1, k, :], ALU.is_lt, ALU.mult))
                step(v.tensor_tensor(level[:, 0, k, :], level[:, 1, k, :], tri[:, 0, 0, :], ALU.mult))
                last = v.tensor_tensor(level[:, 1, k, :], level[:, 1, k, :], tri[:, 1, 0, :], ALU.mult)
                if k < LEVELS - 1:
                    step(last)
            last.then_inc(masks_done, 1)
            dve.wait_ge(ss_done, NT)
            step.link(v.tensor_scalar(rstd[:], sumsq[:], 1.0 / D, NORM_EPS, ALU.mult, ALU.add))
            v.reciprocal(rstd[:], rstd[:]).then_inc(rv_done, 1)
            dve.wait_ge(ld_mu, 16 * 6)
            step.link(v.tensor_tensor(mu_self[:], mu[:, 0, :], mu[:, 1, :], ALU.add))
            v.tensor_scalar(mu_self[:], mu_self[:], -1.0, 1.0, ALU.mult, ALU.add).then_inc(mu_done, 1)
            dve.wait_ge(rstd_done, 1)
            for t in range(NT):
                v.tensor_scalar(xs_rows[:, t, :], x_rows[:, t, :], rstd[:, t:t + 1], None, ALU.mult).then_inc(xs_done, 1)
            dve.wait_ge(ld_par, 32)
            dve.wait_ge(w_used, 8)
            step.link(v.tensor_tensor(mod1[:], ps[:, 7, 0:16], ada_bc[:], ALU.add))
            v.scalar_tensor_tensor(mod1[:, 8:16], mod1[:, 8:16], 1.0, n1_col[:], ALU.add, ALU.mult).then_inc(mod1_done, 1)
            dve.wait_ge(ld_lam, 32)
            lam4 = lam[:].rearrange("p (a d) -> p a d", a=4)
            step.link(v.tensor_tensor(lam_p[:].rearrange("p (a d) -> p a d", a=2), lam4[:, 0:4:2, :], lam4[:, 1:4:2, :], ALU.mult))
            v.tensor_reduce(lam_e[:], lam_p[:].rearrange("p (a d) -> p a d", a=2), AX.X, ALU.add).then_inc(lam_sum, 1)
            dve.wait_ge(ld_rw, RW_LOADS)
            step(v.tensor_scalar(ka1_col[:], ka_col[:], -1.0, 1.0, ALU.mult, ALU.add))

            for b in range(15):
                dve.wait_ge(proj_a, b + 1)
                bank, dst = ps[:, b % 4, :], rw_dest(b)
                step.link(v.scalar_tensor_tensor(dst[:, 1:S], bank[:, 0:S - 1], mu[:, 0, b:b + 1], dst[:, 1:S], ALU.mult, ALU.add))
                v.scalar_tensor_tensor(dst[:, 0:S - 1], bank[:, 1:S], mu[:, 1, b:b + 1], dst[:, 0:S - 1], ALU.mult, ALU.add).then_inc(proj_v, 1)
            dve.wait_ge(proj_v, 15)
            for b in range(NB):
                v.tensor_scalar(kkT[:, b, :], kT[:, b, :], kk_col[:, b:b + 1], None, ALU.mult).then_inc(kk_raw, 1)
            def modulation_part(u):
                n = 22 + u
                dve.wait_ge(ld_w[n % 4], 16 * (n // 4 + 1))
                if u >= 8:
                    dve.wait_ge(mod_sum, u - 7)
                w, acc = strip(n), mod_acc[:, u % 8, :]
                step.link(v.tensor_scalar(acc, w[:, 0, :], silu_c[:, 0:1], None, ALU.mult))
                for k in range(1, KD):
                    last = v.scalar_tensor_tensor(acc, w[:, k, :], silu_c[:, k:k + 1], acc, ALU.mult, ALU.add)
                    if k < KD - 1:
                        step.link(last)
                last.then_inc(mod_part[0], 1)

            for b in range(8):
                dve.wait_ge(qk_sqr, b + 1)
                v.tensor_scalar(qkT[:, b, :], ps[:, (15 + b) % 4, :], qk_gain[:, b // 4:b // 4 + 1], None, ALU.mult).then_inc(proj_v, 1)
                if b == 6:
                    modulation_part(0)
            dve.wait_ge(qk_stat, 8)
            step.link(v.tensor_scalar(stat[:], ps[0:16, 4, :], 1.0 / HD, NORM_EPS, ALU.mult, ALU.add))
            v.reciprocal(stat[:], stat[:]).then_inc(qk_var, 1)
            dve.wait_ge(kk_norm, 1)
            step.link(v.tensor_scalar(stat_kk, stat_kk, 1e-12, None, ALU.max))
            v.reciprocal(stat_kk, stat_kk).then_inc(kk_inv, 1)
            for b in range(8):
                dve.wait_ge(qk_bc, b + 1)
                v.tensor_tensor(qkT[:, b, :], ps[:, b % 4, :], qkT[:, b, :], ALU.mult).then_inc(qk_done, 1)
            for b in range(NB):
                dve.wait_ge(kk_bc, b + 1)
                v.tensor_tensor(kkT[:, b, :], ps[:, b, :], kkT[:, b, :], ALU.mult).then_inc(kk_done, 1)
            dve.wait_ge(lam_exp, 1)
            step.link(v.tensor_tensor(neg_lam[:], lam_e[:, 1:2], lam_e[:, 0:1], ALU.subtract))
            step.link(v.tensor_scalar(neg_lam[:], neg_lam[:], -LAMBDA0, None, ALU.add))

            def maxima(u):
                h, qt, e = u // NT, u % NT, u % 2
                dve.wait_ge(s_mm, u + 1)
                first = 384 - qt * P
                for cmp in range(2):
                    step(v.tensor_tensor_reduce(out=probs[:, 2 * e + cmp, :], in0=ps[:, 2 * e + cmp, :],
                                                in1=bias_h[:, h, first:first + S], scale=1.0, scalar=LOWEST,
                                                op0=ALU.add, op1=ALU.max, accum_out=mx[:, e, cmp:cmp + 1]))
                step.eng.wait_ge(step.sem, step.n)
                v.tensor_scalar(nmx[:, e, :], mx[:, e, :], -1.0, None, ALU.mult).then_inc(s_max, 1)

            def mixture(u):
                e = u % 2
                dve.wait_ge(s_exp, 2 * u + 2)
                step.link(v.reciprocal(rden[:, e, :], den[:, e, :]))
                step(v.tensor_scalar(rden[:, e, 1:2], rden[:, e, 1:2], neg_lam[:, 0:1], None, ALU.mult))
                step.link(v.tensor_scalar(probs[:, 2 * e, :], probs[:, 2 * e, :], rden[:, e, 0:1], None, ALU.mult))
                if u >= 2:
                    dve.wait_ge(mixT_mm, u - 1)
                v.scalar_tensor_tensor(mix[:, e, :], probs[:, 2 * e + 1, :], rden[:, e, 1:2], probs[:, 2 * e, :],
                                       ALU.mult, ALU.add).then_inc(mixed, 1)

            dve.wait_ge(bias_done, DA)
            maxima(0)
            maxima(1)
            modulation_part(4)
            for u in range(UN):
                mixture(u)
                if u + 2 < UN:
                    maxima(u + 2)
                if u in (2, 6):
                    modulation_part(u + 6)
            dve.wait_ge(o_stat, 1)
            step.link(v.tensor_scalar(stat_o, ps[0:DA, 0, :], 1.0 / P, NORM_EPS, ALU.mult, ALU.add))
            v.reciprocal(stat_o, stat_o).then_inc(o_var, 1)
            dve.wait_ge(mod_sum, 16)
            step.link(v.tensor_tensor(mod2[:], ps[:, 7, 0:32], ada_bc2[:], ALU.add))
            step.link(v.scalar_tensor_tensor(mod2[:, 16:24], mod2[:, 16:24], 1.0, n2_col[:], ALU.add, ALU.mult))
            for h in range(DA):
                dve.wait_ge(o_bc, h + 1)
                v.tensor_tensor(attT[:, h, :], ps[:, 1 + h, :], attT[:, h, :], ALU.mult).then_inc(o_done, 1)


            with dve.Fori(0, NB) as i:
                for d, r in enumerate(dirs):
                    dve.wait_ge(by_act[d], upto(ACT_STEPS, "decay", i))
                    turn = (lambda ap: ap) if d == 0 else (lambda ap: ap[:, ::-1])
                    v.tensor_tensor_scan(turn(r.cum), restart[:], turn(r.sg), 0.0, ALU.mult, ALU.add).then_inc(cum_done, 1)
                for d, r in enumerate(dirs):
                    end = CH - 1 if d == 0 else 0
                    dve.wait_ge(by_act[d], upto(ACT_STEPS, "iclr", i))
                    v.tensor_scalar(r.kappa, r.a, ka_col[:, bass.ds(i, 1)], ka1_col[:, bass.ds(i, 1)], ALU.mult, ALU.add).then_inc(kap, 1)
                    dve.wait_ge(kap, 4 * i + 2 * d + 1)
                    v.tensor_tensor(r.kappa, r.kappa, pair_of(4, i), ALU.mult).then_inc(kap, 1)
                    dve.wait_ge(exps, 6 * i + 3 * d + 2)
                    v.tensor_copy(ptot[:, d, :].unsqueeze(2), by_chunk(r.pinc)[:, :, end:end + 1]).then_inc(feat_v, 1)
                    dve.wait_ge(kap, 4 * i + 2 * d + 2)
                    v.tensor_tensor(r.kappa, r.kappa, r.pinv, ALU.mult).then_inc(feat_v, 1)
                    dve.wait_ge(exps, 6 * i + 3 * d + 3)
                    v.tensor_tensor(r.alpha, r.pexc, pair_of(12, i), ALU.mult).then_inc(feat_v, 1)
                    v.tensor_tensor(r.rho, r.pinc if d == 0 else r.pexc, pair_of(0, i), ALU.mult).then_inc(feat_v, 1)
                    dve.wait_ge(feat_v, 10 * i + 5 * d + 2)
                    v.tensor_tensor(by_chunk(r.hat_k), by_chunk(r.kappa), ptot[:, d, :].unsqueeze(2).to_broadcast([P, NC, CH]),
                                    ALU.mult).then_inc(feat_v, 1)

                def banks(d, name, width=1):
                    b = bank_of(d, name)
                    return ps[:, b:b + width, :].rearrange("p b n -> p (b n)").rearrange("p (c n) -> p c n", c=NC)

                for name in ("gram_b", "gram_k"):
                    for d, r in enumerate(dirs):
                        dve.wait_ge(mm[d], upto(STEPS, name, i))
                        mask = tri[:, d, :, :].rearrange("p a t -> p (a t)").unsqueeze(1).to_broadcast([P, NC, 2 * CH])
                        v.tensor_tensor(r.la if name == "gram_b" else r.mb, banks(d, name, 2), mask, ALU.mult).then_inc(by_dve[d], 1)
                for d, r in enumerate(dirs):
                    dve.wait_ge(c_done[d], 7 * i + 1)
                    v.tensor_tensor(r.xt, eye[:].unsqueeze(1).to_broadcast([P, NC, CH]), r.c[0], ALU.subtract).then_inc(by_dve[d], 1)
                for d, r in enumerate(dirs):
                    dve.wait_ge(by_dve[d], upto(DVE_STEPS, "xt0", i))
                    v.transpose(flat(r.x), flat(r.xt)).then_inc(by_dve[d], 1)
                for k in range(1, LEVELS - 1):
                    for d, r in enumerate(dirs):
                        dve.wait_ge(mm[d], upto(STEPS, f"x{k}", i))
                        v.tensor_tensor(r.x, r.x, banks(d, f"x{k}"), ALU.subtract).then_inc(by_dve[d], 1)
                    for d, r in enumerate(dirs):
                        dve.wait_ge(by_dve[d], upto(DVE_STEPS, f"x{k}", i))
                        v.transpose(flat(r.xt), flat(r.x)).then_inc(by_dve[d], 1)
                for d, r in enumerate(dirs):
                    dve.wait_ge(mm[d], upto(STEPS, f"xt{LEVELS - 1}", i))
                    v.tensor_tensor(r.xt, r.xt, banks(d, f"xt{LEVELS - 1}"), ALU.subtract).then_inc(by_dve[d], 1)
                for d, r in enumerate(dirs):
                    dve.wait_ge(c_done[d], 7 * i + 7)
                    dve.wait_ge(mm[d], upto(STEPS, "phi", i))
                    v.tensor_tensor(odd_even(pair_of(23 + d, i * 2)), odd_even(flat(r.dg)), feature_banks(bank_of(d, "phi")), ALU.add).then_inc(by_dve[d], 1)
                for d, r in enumerate(dirs):
                    dve.wait_ge(mm[d], upto(STEPS, "rho", i))
                    v.tensor_tensor(odd_even(pair_of(39 + d, i * 2)), odd_even(r.rho),
                                    feature_banks(bank_of(d, "rho")), ALU.add).then_inc(by_dve[d], 1)
                dve.wait_ge(mm[0], upto(STEPS, "y", i))
                v.tensor_copy(odd_even(pair_of(47, i)), feature_banks(bank_of(0, "y"))).then_inc(by_dve[0], 1)
                dve.wait_ge(mm[1], upto(STEPS, "y", i))
                dve.wait_ge(by_dve[0], upto(DVE_STEPS, "y", i))
                v.tensor_tensor(odd_even(pair_of(47, i)), odd_even(pair_of(47, i)), feature_banks(bank_of(1, "y")), ALU.add).then_inc(by_dve[1], 1)
                for d in range(2):
                    dve.wait_ge(mm[d], (i + 1) * len(STEPS))
                    dve.wait_ge(by_act[d], (i + 1) * len(ACT_STEPS))
                    dve.wait_ge(by_dve[d], (i + 1) * len(DVE_STEPS))
                    dve.wait_ge(c_done[d], 7 * i + 7)


            def of_dir(ap, d):
                return ap.rearrange("p (b n) -> p b n", b=NB)[:, :, d * CH:(d + 1) * CH]

            psi = PSI.rearrange("p (b a) n -> p b a n", a=2)
            for st in range(NC - 1):
                for d in range(2):
                    ch = st if d == 0 else NC - 1 - st
                    dst, part = of_dir(states[:, st + 1, :], d), psi[:, :, d, ch * CH:(ch + 1) * CH]
                    if st == 0:
                        v.tensor_copy(dst, part).then_inc(state_done, 1)
                    else:
                        dve.wait_ge(state_mm, st)
                        v.tensor_tensor(dst, of_dir(ps[:, st % 2, :], d), part, ALU.add).then_inc(state_done, 1)
            dve.wait_ge(state_done, 2 * (NC - 1))
            for g in range(8):
                v.tensor_tensor(col_diag[:, g, :].rearrange("p (c n) -> p c n", c=4), ident[:].unsqueeze(1).to_broadcast([P, 4, P]),
                                mod2[:, 4 * g:4 * g + 4].unsqueeze(2).to_broadcast([P, 4, P]), ALU.mult).then_inc(spread, 1)
            for b in range(NB):
                v.scalar_tensor_tensor(tmp[:, b, :], rT[:, b, :], rk_col[:, b:b + 1], kT[:, b, :], ALU.mult, ALU.mult).then_inc(rk_done, 1)
            for b in range(NB):
                dve.wait_ge(yst_mm, b + 1)
                v.tensor_tensor(YT[:, b, :], YT[:, b, :], ps[:, 2 + b, :], ALU.add).then_inc(y_sum, 1)
            for b in range(NB):
                dve.wait_ge(y_sum, b + 1)
                dve.wait_ge(mean_mm, b + 1)
                v.scalar_tensor_tensor(YT[:, b, :], ps[:, 2 + b, :], -1.0 / HD, YT[:, b, :], ALU.mult, ALU.add).then_inc(centred, 1)
            dve.wait_ge(y_stat, 1)
            step.link(v.tensor_scalar(stat_y, ps[0:8, 0, :], 1.0 / HD, GN_EPS, ALU.mult, ALU.add))
            v.reciprocal(stat_y, stat_y).then_inc(y_var, 1)
            for b in range(NB):
                dve.wait_ge(bon_mm, b + 1)
                v.tensor_tensor(tmp[:, b, :], ps[:, 6 + b % 2, :], vT[:, b, :], ALU.mult).then_inc(bon_done, 1)
            dve.wait_ge(y_sqr, NB)
            for b in range(NB):
                dve.wait_ge(y_bc, b + 1)
                step.link(v.tensor_tensor(YT[:, b, :], YT[:, b, :], ps[:, 2 + b, :], ALU.mult))
                step.link(v.tensor_scalar(YT[:, b, :], YT[:, b, :], lg_col[:, b:b + 1], lb_col[:, b:b + 1], ALU.mult, ALU.add))
                dve.wait_ge(bon_done, b + 1)
                step.link(v.tensor_tensor(YT[:, b, :], YT[:, b, :], tmp[:, b, :], ALU.add))
                dve.wait_ge(gate_mm, b + 1)
                v.tensor_tensor(YT[:, b, :], YT[:, b, :], ps[:, 6 + b % 2, :], ALU.mult).then_inc(rw_out, 1)

            dve.wait_ge(rows_done, 2)
            def normalise(t):
                dve.wait_ge(ss2, t + 1)
                step.link(v.tensor_scalar(rstd[:, t:t + 1], sumsq[:, t:t + 1], 1.0 / D, NORM_EPS, ALU.mult, ALU.add))
                v.reciprocal(rstd[:, t:t + 1], rstd[:, t:t + 1]).then_inc(rv2, 1)
                dve.wait_ge(rstd2, t + 1)
                v.scalar_tensor_tensor(h2[:, t, :], x1[:, t, :], rstd[:, t:t + 1], scale2, ALU.mult, ALU.mult).then_inc(h2a, 1)
                dve.wait_ge(h2a, t + 1)
                v.tensor_tensor(h2[:, t, :], h2[:, t, :], shift2, ALU.add).then_inc(h2_done, 1)

            for t in range(NT):
                dve.wait_ge(ld_x[t], 32)
                for n in range(2):
                    g, cols = 2 * t + n, slice(512 * n, 512 * n + 512)
                    dve.wait_ge(wo_mm, g + 1)
                    v.tensor_tensor(h2[:, t, cols], ps[:, 2 + g % 4, :], gate1[:, cols], ALU.mult).then_inc(wo_gated, 1)
                    dve.wait_ge(wo_gated, g + 1)
                    v.tensor_tensor(x1[:, t, cols], x1[:, t, cols], h2[:, t, cols], ALU.add).then_inc(x1_done, 1)
                if t == 0:
                    dve.wait_ge(rows_done, 8)
                normalise(t)

            def choose(h, t):
                u = h * NT + t
                sc = scores[:, t]
                dve.wait_ge(sc_done, h * 2 + 2)

                def best16(srcs, cuts, rows, done):
                    n = len(srcs)

                    def inputs_at(k):
                        dve.wait_ge(best, u * CHOICE_OPS + k)

                    for i in range(n):
                        if done:
                            inputs_at(done)
                        dve.nop(nofuse=True)
                        v.max(top[:, rows + i, 0:8], srcs[i]).then_inc(best, 1)
                    for i in range(n):
                        inputs_at(done + i + 1)
                        dve.nop(nofuse=True)
                        v.max_index(top_i[:, rows + i, 0:8], top[:, rows + i, 0:8], srcs[i]).then_inc(best, 1)
                    for i in range(n):
                        v.match_replace(cuts[i], top[:, rows + i, 0:8], srcs[i], LOWEST).then_inc(best, 1)
                    for i in range(n):
                        inputs_at(done + 2 * n + i + 1)
                        dve.nop(nofuse=True)
                        v.max(top[:, rows + i, 8:16], cuts[i]).then_inc(best, 1)
                    for i in range(n):
                        inputs_at(done + 3 * n + i + 1)
                        dve.nop(nofuse=True)
                        v.max_index(top_i[:, rows + i, 8:16], top[:, rows + i, 8:16], cuts[i]).then_inc(best, 1)

                best16([sc[:, 0, :], sc[:, 1, :]], [sc_cut[:, 0:NKEY], sc_cut[:, NKEY:]], 0, 0)
                dve.wait_ge(best, u * CHOICE_OPS + 10)
                v.tensor_tensor(cand.rearrange("p (a b) -> p a b", a=TOPK), top[:, 0, :].unsqueeze(2).to_broadcast([P, TOPK, TOPK]),
                                top[:, 1, :].unsqueeze(1).to_broadcast([P, TOPK, TOPK]), ALU.add).then_inc(best, 1)
                best16([cand], [cand_cut], 2, 11)
                v.tensor_scalar(neg_top[:], top[:, 2, 0:1], -1.0, None, ALU.mult).then_inc(neg_done, 1)

            def resolve(u):
                base = lambda k: u * 7 + k
                places = top_i[:, 2, :].bitcast(I32)
                dve.wait_ge(best, u * CHOICE_OPS + CHOICE_OPS)
                v.tensor_scalar(ci_hi[:], places, 4, None, ALU.logical_shift_right).then_inc(math_s, 1)
                v.tensor_scalar(ci_lo[:], places, TOPK - 1, None, ALU.bitwise_and).then_inc(math_s, 1)
                for a, ci in enumerate((ci_hi, ci_lo)):
                    dve.wait_ge(math_s, base(a + 1))
                    v.tensor_tensor(pick[:, a], ci[:].unsqueeze(2).to_broadcast([P, TOPK, TOPK]),
                                    iota16i[:].unsqueeze(1).to_broadcast([P, TOPK, TOPK]), ALU.is_equal).then_inc(math_s, 1)
                for a in range(2):
                    dve.wait_ge(math_s, base(a + 3))
                    v.tensor_tensor(pick[:, a], pick[:, a], top_i[:, a, :].bitcast(I32).unsqueeze(1).to_broadcast([P, TOPK, TOPK]),
                                    ALU.mult).then_inc(math_s, 1)
                dve.wait_ge(math_s, base(6))
                v.tensor_reduce(e_half[:], pick, AX.X, ALU.add).then_inc(math_s, 1)
                dve.wait_ge(math_s, base(7))
                v.scalar_tensor_tensor(e_idx[:, bass.ds(u * TOPK, TOPK)], e_half[:, 0, :], float(NKEY), e_half[:, 1, :],
                                       ALU.mult, ALU.add).then_inc(e_done, 1)
                dve.wait_ge(g_exp, u + 1)
                dve.wait_ge(neg_done, u + 1)
                step_r(v.reciprocal(g_den[:], g_den[:]), u + 1)
                v.tensor_scalar(gates[:, bass.ds(u * TOPK, TOPK)], g_exp_t[:], g_den[:, 0:1], None, ALU.mult).then_inc(g_done, 1)

            def step_r(ins, n):
                ins.then_inc(g_rec, 1)
                dve.wait_ge(g_rec, n)

            def add_up(after, t):
                dve.wait_ge(v_free, after * TOPK + V_SLOTS)
                for n in range(2):
                    v.tensor_tensor(gated[:, n, :], ps[:, 2 * (t % 2) + n, :], gate2[:, 512 * n:512 * n + 512], ALU.mult).then_inc(o_gated, 1)
                for n in range(2):
                    cols = slice(512 * n, 512 * n + 512)
                    dve.wait_ge(o_gated, after * 2 + (n + 1))
                    v.tensor_tensor(x1[:, t, cols], x1[:, t, cols], gated[:, n, :], ALU.add).then_inc(o_sum, 1)

            def expert_turn(h, t, last_head):
                u = h * NT + t
                dve.wait_ge(g_done, u + 1)

                def weigh(g):
                    dve.wait_ge(gelu_done, u * 4 + (g + 1))
                    v.tensor_tensor(w16[:, 4 * g:4 * g + 4], gelu16[:, 4 * g:4 * g + 4],
                                    gates[:, bass.ds(u * TOPK + 4 * g, 4)], ALU.mult).then_inc(w_done, 1)

                ahead = (h, t + 2) if t < 2 else (h + 1, t - 2)
                for g in range(4):
                    for b in range(U_SLOTS):
                        s = 4 * g + b
                        dve.wait_ge(ld_u[b], u * 64 + 16 * (g + 1))
                        dve.wait_ge(u_free, u * TOPK + (U_SLOTS + s - 1))
                        v.tensor_tensor_reduce(out=waste[:, s % 2, :], in0=u_ring[:, b, :], in1=h2[:, t, :], scale=1.0, scalar=0.0,
                                               op0=ALU.mult, op1=ALU.add, accum_out=act16[:, s:s + 1]).then_inc(u_free, 1)
                        if b == 0 and g > 0:
                            weigh(g - 1)
                    if g == 0:
                        add_up(u, (t - 1) % NT)
                    if not (last_head and t >= 2):
                        if g == 1:
                            choose(*ahead)
                        if g == 2:
                            resolve(ahead[0] * NT + ahead[1])
                weigh(3)

            for t in range(2):
                choose(0, t)
                resolve(t)
            with dve.Fori(0, PH - 1) as h:
                for t in range(NT):
                    expert_turn(h, t, False)
            v.memset(e_idx[:, UNITS * TOPK:UNITS * TOPK + 1], 0).then_inc(e_done, 1)
            for t in range(NT):
                expert_turn(PH - 1, t, True)
            add_up(UNITS, NT - 1)


_INS = ["x", "c", "ada_w", "ada_b", "norm1_g", "w_in", "da_qnorm_g", "da_knorm_g", "da_lambda", "da_subln_g",
        "rw_shift_mu", "rw_w0", "rw_w2", "rw_a0", "rw_a2", "rw_g2", "rw_k_k", "rw_k_a", "rw_r_k", "rw_ln_g", "rw_ln_b",
        "w_out", "norm2_g", "peer_wq", "peer_keys", "peer_u", "peer_v"]
_FLAT = {"x", "ada_w", "w_in", "w_out", "peer_wq", "peer_u", "peer_v"}


def lay(**inputs):
    import numpy as np
    arrays = {}
    for name in _INS:
        a = np.ascontiguousarray(inputs[name])
        arrays[name] = a.reshape(a.shape[1:]) if name in _FLAT else a
    arrays["peer_keys"] = arrays["peer_keys"].reshape(2 * PH, NKEY, P)
    return arrays


def kernel(**inputs):
    import concourse.bacc as _bacc
    from concourse import mybir as _mybir
    from concourse.bass_utils import run_bass_kernel_spmd as _run

    nc = _bacc.Bacc("TRN2", target_bir_lowering=False, num_devices=1)
    laid = lay(**inputs)
    arrays, args = {}, []
    for name in _INS:
        a = laid[name]
        arrays[f"in_{name}_dram"] = a
        args.append(nc.dram_tensor(f"in_{name}_dram", a.shape, _mybir.dt.from_np(a.dtype), kind="ExternalInput").ap())
    out = nc.dram_tensor("out_0_dram", (S, D), F32, kind="ExternalOutput").ap()
    hymba_kernel(nc, *args, out)
    r = _run(nc, [arrays], core_ids=[0])
    return r.results[0]["out_0_dram"].reshape(1, S, D)
```
